# Optimizing a Trainium2 kernel written in Bass

```python
import math
import jax, jax.numpy as jnp
from jax import lax
import numpy as np

D_MODEL = 1024
BATCH = 1
SEQ = 256
DEPTH = 1

HG_HEADS = 4
HG_DK = 128
HG_DV = 128
HG_KEY_WIDTH = HG_HEADS * HG_DK
HG_WIDTH = HG_HEADS * HG_DV
HG_CHUNK = 64

MB_HEADS = 8
MB_DH = 64
MB_WIDTH = MB_HEADS * MB_DH
MB_BLOCK = 256
MB_TOPK = 3
MB_QCHUNK = 16

REL_BUCKETS = 32
REL_MAX_DIST = 128

N_GROUPS = 4
EXPERTS_PER_GROUP = 8
N_EXPERTS = N_GROUPS * EXPERTS_PER_GROUP
TOP_K = 2
EXPERT_HIDDEN = 512
MOE_BLOCK = 128

DN_ALPHA = (2.0 * DEPTH) ** 0.25
DN_BETA = (8.0 * DEPTH) ** -0.25
NORM_EPS = 1e-5

IN_SIZES = (HG_KEY_WIDTH, HG_KEY_WIDTH, HG_WIDTH, HG_WIDTH, MB_WIDTH, MB_WIDTH, MB_WIDTH, D_MODEL, D_MODEL)
IN_COLS = sum(IN_SIZES)


def layer_norm(x, g, b):
    xf = x.astype(jnp.float32)
    mu = jnp.mean(xf, axis=-1, keepdims=True)
    xc = xf - mu
    var = jnp.mean(xc * xc, axis=-1, keepdims=True)
    return (xc * lax.rsqrt(var + NORM_EPS) * g.astype(jnp.float32) + b.astype(jnp.float32)).astype(x.dtype)

def hgrn2_mixer(q, f_logit, i, g, lb, norm_g):
    B, S, _ = q.shape
    nc = S // HG_CHUNK
    f32 = jnp.float32
    lb = lb.astype(f32)
    z = f_logit.astype(f32)
    log_f = jnp.log(lb + (1.0 - lb) * jax.nn.sigmoid(z))
    k = (1.0 - lb) * jax.nn.sigmoid(-z)
    qf = jax.nn.silu(q.astype(f32))
    vf = i.astype(f32)

    def to_chunks(t, dh):
        return t.reshape(B, nc, HG_CHUNK, HG_HEADS, dh).transpose(1, 0, 3, 2, 4)

    causal = jnp.tril(jnp.ones((HG_CHUNK, HG_CHUNK), dtype=bool))

    def chunk_step(state, inp):
        qc, kc, vc, lfc = inp
        b = jnp.cumsum(lfc, axis=2)
        o_inter = jnp.einsum('bhtk,bhkv->bhtv', qc * jnp.exp(b), state)
        rel = b[:, :, :, None, :] - b[:, :, None, :, :]
        decay = jnp.exp(jnp.where(causal[:, :, None], rel, -jnp.inf))
        scores = jnp.einsum('bhtk,bhtsk,bhsk->bhts', qc, decay, kc)
        o_intra = jnp.einsum('bhts,bhsv->bhtv', scores, vc)
        b_end = b[:, :, -1:, :]
        state = (jnp.exp(b_end[:, :, 0, :])[..., None] * state
                 + jnp.einsum('bhsk,bhsv->bhkv', kc * jnp.exp(b_end - b), vc))
        return state, o_inter + o_intra

    s0 = jnp.zeros((B, HG_HEADS, HG_DK, HG_DV), f32)
    _, o = lax.scan(chunk_step, s0, (to_chunks(qf, HG_DK), to_chunks(k, HG_DK),
                                     to_chunks(vf, HG_DV), to_chunks(log_f, HG_DK)))
    o = o.transpose(1, 0, 3, 2, 4).reshape(B, S, HG_HEADS, HG_DV)
    o = o * lax.rsqrt(jnp.mean(o * o, axis=-1, keepdims=True) + NORM_EPS)
    o = o.reshape(B, S, HG_WIDTH) * norm_g.astype(f32) * jax.nn.silu(g.astype(f32))
    return o.astype(q.dtype)

def t5_bucket(dist):
    max_exact = REL_BUCKETS // 2
    d = jnp.maximum(dist, 1).astype(jnp.float32)
    log_part = max_exact + (jnp.log(d / max_exact) / math.log(REL_MAX_DIST / max_exact)
                            * (REL_BUCKETS - max_exact)).astype(jnp.int32)
    return jnp.where(dist < max_exact, dist, jnp.minimum(log_part, REL_BUCKETS - 1))

def moba_mixer(q, k, v, rel_bias):
    B, S, _ = q.shape
    f32 = jnp.float32
    nb = -(-S // MB_BLOCK)
    s_pad = nb * MB_BLOCK
    k_sel = min(MB_TOPK, nb)
    scale = MB_DH ** -0.5

    def to_heads(t):
        t = jnp.pad(t, ((0, 0), (0, s_pad - S), (0, 0)))
        return t.reshape(B, s_pad, MB_HEADS, MB_DH).transpose(0, 2, 1, 3)

    qh, kh, vh = to_heads(q), to_heads(k), to_heads(v)
    kb = kh.reshape(B, MB_HEADS, nb, MB_BLOCK, MB_DH)
    vb = vh.reshape(B, MB_HEADS, nb, MB_BLOCK, MB_DH)
    k_mean = jnp.mean(kb, axis=3)
    gate = jnp.einsum('bhsd,bhnd->bhsn', qh, k_mean).astype(f32)
    pos = jnp.arange(s_pad)
    fully_past = jnp.arange(nb)[None, :] < (pos // MB_BLOCK)[:, None]
    gate = jnp.where(fully_past, gate, -jnp.inf)
    top_val, top_idx = lax.top_k(gate, k_sel)
    top_ok = jnp.isfinite(top_val)

    rb = rel_bias.astype(f32).T
    b_ix = jnp.arange(B)[:, None, None, None]
    h_ix = jnp.arange(MB_HEADS)[None, :, None, None]

    def attend(c):
        t0 = c * MB_QCHUNK
        tq = t0 + jnp.arange(MB_QCHUNK)
        qc = lax.dynamic_slice_in_dim(qh, t0, MB_QCHUNK, axis=2)
        idx = lax.dynamic_slice_in_dim(top_idx, t0, MB_QCHUNK, axis=2)
        ok = lax.dynamic_slice_in_dim(top_ok, t0, MB_QCHUNK, axis=2)
        kg = kb[b_ix, h_ix, idx]
        vg = vb[b_ix, h_ix, idx]
        kpos = idx[..., None] * MB_BLOCK + jnp.arange(MB_BLOCK)
        bucket = t5_bucket(tq[None, None, :, None, None] - kpos)
        s_past = (jnp.einsum('bhqd,bhqjkd->bhqjk', qc, kg).astype(f32) * scale
                  + rb[h_ix[..., None], bucket])
        s_past = jnp.where(ok[..., None], s_past, -jnp.inf).reshape(B, MB_HEADS, MB_QCHUNK, k_sel * MB_BLOCK)
        j0 = (t0 // MB_BLOCK) * MB_BLOCK
        k_own = lax.dynamic_slice_in_dim(kh, j0, MB_BLOCK, axis=2)
        v_own = lax.dynamic_slice_in_dim(vh, j0, MB_BLOCK, axis=2)
        dist_own = tq[:, None] - (j0 + jnp.arange(MB_BLOCK))[None, :]
        s_own = (jnp.einsum('bhqd,bhkd->bhqk', qc, k_own).astype(f32) * scale
                 + rb[:, t5_bucket(jnp.maximum(dist_own, 0))])
        s_own = jnp.where(dist_own >= 0, s_own, -jnp.inf)
        p = jax.nn.softmax(jnp.concatenate([s_past, s_own], axis=-1), axis=-1)
        p_past = p[..., :k_sel * MB_BLOCK].reshape(B, MB_HEADS, MB_QCHUNK, k_sel, MB_BLOCK).astype(vg.dtype)
        p_own = p[..., k_sel * MB_BLOCK:].astype(v_own.dtype)
        return (jnp.einsum('bhqjk,bhqjkd->bhqd', p_past, vg)
                + jnp.einsum('bhqk,bhkd->bhqd', p_own, v_own))

    o = lax.map(attend, jnp.arange(s_pad // MB_QCHUNK))
    o = o.transpose(1, 0, 3, 2, 4).reshape(B, s_pad, MB_WIDTH)[:, :S]
    return o

def hier_moe(x, w_group, b_group, w_expert, b_expert, w_gate_up, w_down):
    B, S, D = x.shape
    n_tok = B * S
    n_asg = n_tok * TOP_K
    f32 = jnp.float32
    xt = x.reshape(n_tok, D)
    g_logits = (xt @ w_group + b_group).astype(f32)
    grp = jnp.argmax(g_logits, axis=-1)
    p_grp = jnp.take_along_axis(jax.nn.softmax(g_logits, axis=-1), grp[:, None], axis=1)
    e_logits = (xt @ w_expert + b_expert).astype(f32).reshape(n_tok, N_GROUPS, EXPERTS_PER_GROUP)
    e_in_grp = jnp.take_along_axis(e_logits, grp[:, None, None], axis=1)[:, 0]
    top_v, top_i = lax.top_k(e_in_grp, TOP_K)
    weights = (jax.nn.softmax(top_v, axis=-1) * p_grp).reshape(n_asg)
    expert = (grp[:, None] * EXPERTS_PER_GROUP + top_i).reshape(n_asg)
    token = jnp.repeat(jnp.arange(n_tok), TOP_K)
    order = jnp.argsort(expert)
    e_s, tok_s, w_s = expert[order], token[order], weights[order]
    counts = jax.ops.segment_sum(jnp.ones((n_asg,), jnp.int32), expert, num_segments=N_EXPERTS)
    starts = jnp.cumsum(counts) - counts
    padded = (counts + MOE_BLOCK - 1) // MOE_BLOCK * MOE_BLOCK
    pad_end = jnp.cumsum(padded)
    pad_start = pad_end - padded
    dest = pad_start[e_s] + jnp.arange(n_asg) - starts[e_s]
    n_blk = -(-n_asg // MOE_BLOCK) + N_EXPERTS
    n_rows = n_blk * MOE_BLOCK
    x_buf = jnp.zeros((n_rows, D), x.dtype).at[dest].set(xt[tok_s])
    blk_expert = jnp.minimum(jnp.searchsorted(pad_end, jnp.arange(n_blk) * MOE_BLOCK, side='right'),
                             N_EXPERTS - 1)

    def expert_block(args):
        xb, e = args
        gate, up = jnp.split(xb @ w_gate_up[e], 2, axis=-1)
        return (jax.nn.silu(gate) * up) @ w_down[e]

    y_buf = lax.map(expert_block, (x_buf.reshape(n_blk, MOE_BLOCK, D), blk_expert)).reshape(n_rows, D)
    y = jnp.zeros((n_tok, D), x.dtype).at[tok_s].add(y_buf[dest] * w_s[:, None].astype(x.dtype))
    return y.reshape(B, S, D)

def first_inputs(seed: int = 0) -> dict:
    key = jax.random.key(seed)
    ks = jax.random.split(key, 20)
    f32 = jnp.float32
    L = DEPTH

    def normal(k, shape, std):
        return jax.random.normal(k, shape, f32) * std

    col_scale = jnp.concatenate([jnp.full((n,), s, f32) for n, s in
                                 zip(IN_SIZES, (1.0, 1.0, DN_BETA, 1.0, 1.0, 1.0, DN_BETA, 1.0, 1.0))])
    return {
        'x': normal(ks[0], (BATCH, SEQ, D_MODEL), 1.0),
        'w_in': normal(ks[1], (L, D_MODEL, IN_COLS), D_MODEL ** -0.5) * col_scale,
        'b_in': normal(ks[2], (L, IN_COLS), 0.02),
        'lb_logits': normal(ks[3], (L + 1, HG_KEY_WIDTH), 0.5),
        'hg_norm_g': 1.0 + normal(ks[4], (L, HG_WIDTH), 0.1),
        'rel_bias': normal(ks[5], (REL_BUCKETS, MB_HEADS), 0.5),
        'w_proj_a': normal(ks[6], (L, HG_WIDTH, D_MODEL), DN_BETA * HG_WIDTH ** -0.5),
        'w_proj_b': normal(ks[7], (L, MB_WIDTH, D_MODEL), DN_BETA * MB_WIDTH ** -0.5),
        'w_out': normal(ks[8], (L, D_MODEL, D_MODEL), DN_BETA * D_MODEL ** -0.5),
        'ln1_g': 1.0 + normal(ks[9], (L, D_MODEL), 0.1),
        'ln1_b': normal(ks[10], (L, D_MODEL), 0.02),
        'w_group': normal(ks[11], (L, D_MODEL, N_GROUPS), D_MODEL ** -0.5),
        'b_group': normal(ks[12], (L, N_GROUPS), 0.01),
        'w_expert': normal(ks[13], (L, D_MODEL, N_EXPERTS), D_MODEL ** -0.5),
        'b_expert': normal(ks[14], (L, N_EXPERTS), 0.01),
        'w_gate_up': normal(ks[15], (L, N_EXPERTS, D_MODEL, 2 * EXPERT_HIDDEN), D_MODEL ** -0.5),
        'w_down': normal(ks[16], (L, N_EXPERTS, EXPERT_HIDDEN, D_MODEL), DN_BETA * EXPERT_HIDDEN ** -0.5),
        'ln2_g': 1.0 + normal(ks[17], (L, D_MODEL), 0.1),
        'ln2_b': normal(ks[18], (L, D_MODEL), 0.02),
    }

def first_block(x, w_in, b_in, lb_logits, hg_norm_g, rel_bias, w_proj_a, w_proj_b, w_out, ln1_g, ln1_b,
              w_group, b_group, w_expert, b_expert, w_gate_up, w_down, ln2_g, ln2_b):
    split_at = [int(s) for s in np.cumsum(IN_SIZES)[:-1]]
    lower_bounds = jnp.cumsum(jax.nn.softmax(lb_logits.astype(jnp.float32), axis=0), axis=0)
    for l in range(DEPTH):
        h = x
        proj = h @ w_in[l] + b_in[l]
        hg_q, hg_f, hg_i, hg_g, mb_q, mb_k, mb_v, gate_a, gate_b = jnp.split(proj, split_at, axis=-1)
        y_a = hgrn2_mixer(hg_q, hg_f, hg_i, hg_g, lower_bounds[l], hg_norm_g[l]) @ w_proj_a[l]
        y_b = moba_mixer(mb_q, mb_k, mb_v, rel_bias) @ w_proj_b[l]
        mixed = (jax.nn.sigmoid(gate_a) * y_a + jax.nn.sigmoid(gate_b) * y_b) @ w_out[l]
        x = layer_norm(DN_ALPHA * h + mixed, ln1_g[l], ln1_b[l])
        ffn = hier_moe(x, w_group[l], b_group[l], w_expert[l], b_expert[l], w_gate_up[l], w_down[l])
        x = layer_norm(DN_ALPHA * x + ffn, ln2_g[l], ln2_b[l])
    return x


DEPTH_2 = 2

N_MIXERS = 4
N_META = 16
Q_BLOCK = 128
EPS = 1e-6
POOL_WINDOWS = (2, 4, 8, 16)
N_POOL_GROUPS = len(POOL_WINDOWS)
POOL_GROUP = D_MODEL // N_POOL_GROUPS
N_HEADS = 16
HEAD_DIM = D_MODEL // N_HEADS
MLA_HEADS = 16
MLA_Q_RANK = 384
MLA_KV_RANK = 256
MLA_NOPE = 64
MLA_ROPE = 32
MLA_V = 64
ROPE_THETA = 10000.0
D_FF = ((-(-8 * D_MODEL // 3) + 255) // 256) * 256


def _n_layers_of(m):
    return len(range(m, DEPTH_2, N_MIXERS))

def rmsnorm(x, g):
    xf = x.astype(jnp.float32)
    y = xf * lax.rsqrt(jnp.mean(xf * xf, axis=-1, keepdims=True) + EPS)
    return (y * g.astype(jnp.float32)).astype(x.dtype)

def swiglu(h, w_gate, w_up, w_down):
    return (jax.nn.silu(h @ w_gate) * (h @ w_up)) @ w_down

def sweep_queries(attend, q_parts, kv_parts):
    L = q_parts[0].shape[1]
    pos = jnp.arange(L)
    meta_out = attend(tuple(a[:, :N_META] for a in q_parts), pos[:N_META],
                      tuple(a[:, :N_META] for a in kv_parts), pos[:N_META])
    n_blk = (L - N_META) // Q_BLOCK

    def body(i):
        start = N_META + i * Q_BLOCK
        qs = tuple(lax.dynamic_slice_in_dim(a, start, Q_BLOCK, axis=1) for a in q_parts)
        return attend(qs, start + jnp.arange(Q_BLOCK), kv_parts, pos)

    out = lax.map(body, jnp.arange(n_blk))
    B = out.shape[1]
    out = jnp.moveaxis(out, 0, 1).reshape((B, n_blk * Q_BLOCK) + out.shape[3:])
    return jnp.concatenate([meta_out, out], axis=1)

def softmax_block(q, k, v, qpos, kpos, scale, q_decay=None, k_decay=None):
    s = jnp.einsum('bqhd,bkhd->bhqk', q, k).astype(jnp.float32) * scale
    if q_decay is not None:
        s = s + (jnp.transpose(q_decay, (0, 2, 1))[:, :, :, None]
                 - jnp.transpose(k_decay, (0, 2, 1))[:, :, None, :]).astype(jnp.float32)
    mask = kpos[None, :] <= qpos[:, None]
    s = jnp.where(mask, s, jnp.finfo(jnp.float32).min)
    p = jax.nn.softmax(s, axis=-1)
    return jnp.einsum('bhqk,bkhd->bqhd', p.astype(v.dtype), v)

def pool_mixer(h, w, scale):
    B, L, _ = h.shape
    hf = h.astype(jnp.float32)
    pos = jnp.arange(L)
    outs = []
    for g, win in enumerate(POOL_WINDOWS):
        xg = hf[..., g * POOL_GROUP:(g + 1) * POOL_GROUP]
        cs = jnp.cumsum(xg, axis=1)
        lag = jnp.pad(cs[:, :-win], ((0, 0), (win, 0), (0, 0)))
        cnt = jnp.minimum(pos + 1, win).astype(jnp.float32)[None, :, None]
        outs.append((cs - lag) / cnt - xg)
    pooled = jnp.stack(outs, axis=2).astype(h.dtype)
    mixed = jnp.einsum('blgc,gcd->blgd', pooled, w).reshape(B, L, D_MODEL)
    return mixed * scale

def _sb_attend(qs, qpos, kvs, kpos):
    (q,) = qs
    k, v = kvs
    z = jnp.einsum('bqhd,bkhd->bhqk', q, k).astype(jnp.float32) * (HEAD_DIM ** -0.5)
    mask = kpos[None, :] < qpos[:, None]
    log_keep = jnp.where(mask, jax.nn.log_sigmoid(-z), 0.0)
    later = lax.cumsum(log_keep, axis=3, reverse=True) - log_keep
    a = jnp.where(mask, jnp.exp(jax.nn.log_sigmoid(z) + later), 0.0)
    return jnp.einsum('bhqk,bkhd->bqhd', a.astype(v.dtype), v)

def sb_mixer(h, w_qkv, w_o):
    B, L, _ = h.shape
    qkv = (h @ w_qkv).reshape(B, L, 3, N_HEADS, HEAD_DIM)
    q, k, v = qkv[:, :, 0], qkv[:, :, 1], qkv[:, :, 2]
    o = sweep_queries(_sb_attend, (q,), (k, v))
    return o.reshape(B, L, N_HEADS * HEAD_DIM) @ w_o

def _rope(x, cos, sin):
    xf = x.astype(jnp.float32)
    half = xf.shape[-1] // 2
    x1, x2 = xf[..., :half], xf[..., half:]
    return jnp.concatenate([x1 * cos - x2 * sin, x2 * cos + x1 * sin], axis=-1).astype(x.dtype)

def _mla_attend(qs, qpos, kvs, kpos):
    (q,) = qs
    k, v = kvs
    return softmax_block(q, k, v, qpos, kpos, (MLA_NOPE + MLA_ROPE) ** -0.5)

def mla_mixer(h, w_down, q_norm, kv_norm, w_uq, w_ukv, w_o):
    B, L, _ = h.shape
    down = h @ w_down
    c_q = rmsnorm(down[..., :MLA_Q_RANK], q_norm)
    c_kv = rmsnorm(down[..., MLA_Q_RANK:MLA_Q_RANK + MLA_KV_RANK], kv_norm)
    k_rope = down[..., MLA_Q_RANK + MLA_KV_RANK:]
    q = (c_q @ w_uq).reshape(B, L, MLA_HEADS, MLA_NOPE + MLA_ROPE)
    kv = (c_kv @ w_ukv).reshape(B, L, MLA_HEADS, MLA_NOPE + MLA_V)
    q_nope, q_rope = q[..., :MLA_NOPE], q[..., MLA_NOPE:]
    k_nope, v = kv[..., :MLA_NOPE], kv[..., MLA_NOPE:]
    inv = ROPE_THETA ** (-jnp.arange(0, MLA_ROPE, 2, dtype=jnp.float32) / MLA_ROPE)
    ang = jnp.arange(L, dtype=jnp.float32)[:, None] * inv[None, :]
    cos, sin = jnp.cos(ang), jnp.sin(ang)
    q_rope = _rope(q_rope, cos[:, None, :], sin[:, None, :])
    k_rope = _rope(k_rope, cos, sin)
    q = jnp.concatenate([q_nope, q_rope], axis=-1)
    k = jnp.concatenate([k_nope, jnp.broadcast_to(k_rope[:, :, None, :], (B, L, MLA_HEADS, MLA_ROPE))], axis=-1)
    o = sweep_queries(_mla_attend, (q,), (k, v))
    return o.reshape(B, L, MLA_HEADS * MLA_V) @ w_o

def _fox_attend(qs, qpos, kvs, kpos):
    q, fq = qs
    k, v, fk = kvs
    return softmax_block(q, k, v, qpos, kpos, HEAD_DIM ** -0.5, fq, fk)

def fox_mixer(h, w_qkvf, b_f, w_o):
    B, L, _ = h.shape
    proj = h @ w_qkvf
    qkv = proj[..., :3 * N_HEADS * HEAD_DIM].reshape(B, L, 3, N_HEADS, HEAD_DIM)
    q, k, v = qkv[:, :, 0], qkv[:, :, 1], qkv[:, :, 2]
    f_logit = proj[..., 3 * N_HEADS * HEAD_DIM:].astype(jnp.float32) + b_f.astype(jnp.float32)
    F = jnp.cumsum(jax.nn.log_sigmoid(f_logit), axis=1)
    o = sweep_queries(_fox_attend, (q, F), (k, v, F))
    return o.reshape(B, L, N_HEADS * HEAD_DIM) @ w_o

def second_inputs(seed: int = 0) -> dict:
    key = jax.random.key(seed)
    ks = jax.random.split(key, 24)
    f32 = jnp.float32

    def w(k, shape, fan_in):
        return jax.random.normal(k, shape, f32) * (fan_in ** -0.5)

    def gain(k, shape):
        return 1.0 + 0.02 * jax.random.normal(k, shape, f32)

    nA, nB, nC, nD = (_n_layers_of(m) for m in range(N_MIXERS))
    D = D_MODEL
    return {
        "x": jax.random.normal(ks[0], (BATCH, SEQ, D), f32),
        "meta": jax.random.normal(ks[1], (N_META, D), f32),
        "norm_mix": gain(ks[2], (DEPTH_2, D)),
        "norm_ffn": gain(ks[3], (DEPTH_2, D)),
        "pool_w": w(ks[4], (nA, N_POOL_GROUPS, POOL_GROUP, POOL_GROUP), POOL_GROUP),
        "pool_scale": gain(ks[5], (nA, D)),
        "sb_w_qkv": w(ks[6], (nB, D, 3 * N_HEADS * HEAD_DIM), D),
        "sb_w_o": w(ks[7], (nB, N_HEADS * HEAD_DIM, D), N_HEADS * HEAD_DIM),
        "mla_w_down": w(ks[8], (nC, D, MLA_Q_RANK + MLA_KV_RANK + MLA_ROPE), D),
        "mla_q_norm": gain(ks[9], (nC, MLA_Q_RANK)),
        "mla_kv_norm": gain(ks[10], (nC, MLA_KV_RANK)),
        "mla_w_uq": w(ks[11], (nC, MLA_Q_RANK, MLA_HEADS * (MLA_NOPE + MLA_ROPE)), MLA_Q_RANK),
        "mla_w_ukv": w(ks[12], (nC, MLA_KV_RANK, MLA_HEADS * (MLA_NOPE + MLA_V)), MLA_KV_RANK),
        "mla_w_o": w(ks[13], (nC, MLA_HEADS * MLA_V, D), MLA_HEADS * MLA_V),
        "fox_w_qkvf": w(ks[14], (nD, D, 3 * N_HEADS * HEAD_DIM + N_HEADS), D),
        "fox_b_f": 2.0 + 0.5 * jax.random.normal(ks[15], (nD, N_HEADS), f32),
        "fox_w_o": w(ks[16], (nD, N_HEADS * HEAD_DIM, D), N_HEADS * HEAD_DIM),
        "ffn_w_gate": w(ks[17], (DEPTH_2, D, D_FF), D),
        "ffn_w_up": w(ks[18], (DEPTH_2, D, D_FF), D),
        "ffn_w_down": w(ks[19], (DEPTH_2, D_FF, D), D_FF),
        "final_norm": gain(ks[20], (D,)),
    }

def second_block(x, meta, norm_mix, norm_ffn, pool_w, pool_scale, sb_w_qkv, sb_w_o,
              mla_w_down, mla_q_norm, mla_kv_norm, mla_w_uq, mla_w_ukv, mla_w_o,
              fox_w_qkvf, fox_b_f, fox_w_o, ffn_w_gate, ffn_w_up, ffn_w_down, final_norm):
    B = x.shape[0]
    meta_b = jnp.broadcast_to(meta[None].astype(x.dtype), (B, N_META, D_MODEL))
    h = jnp.concatenate([meta_b, x], axis=1)
    for i in range(DEPTH_2):
        m, j = i % N_MIXERS, i // N_MIXERS
        a = rmsnorm(h, norm_mix[i])
        if m == 0:
            mix = pool_mixer(a, pool_w[j], pool_scale[j])
        elif m == 1:
            mix = sb_mixer(a, sb_w_qkv[j], sb_w_o[j])
        elif m == 2:
            mix = mla_mixer(a, mla_w_down[j], mla_q_norm[j], mla_kv_norm[j],
                            mla_w_uq[j], mla_w_ukv[j], mla_w_o[j])
        else:
            mix = fox_mixer(a, fox_w_qkvf[j], fox_b_f[j], fox_w_o[j])
        h = h + mix
        h = h + swiglu(rmsnorm(h, norm_ffn[i]), ffn_w_gate[i], ffn_w_up[i], ffn_w_down[i])
    h = rmsnorm(h, final_norm)
    return h[:, N_META:]


def setup_inputs(seed=0):
    out = dict(first_inputs(seed))
    for name, value in second_inputs(seed + 1).items():
        if name != "x":
            out[name + "_2"] = value
    return out


def reference(
    x, w_in, b_in, lb_logits, hg_norm_g, rel_bias, w_proj_a, w_proj_b, w_out, ln1_g, ln1_b,
    w_group, b_group, w_expert, b_expert, w_gate_up, w_down, ln2_g, ln2_b, meta_2, norm_mix_2,
    norm_ffn_2, pool_w_2, pool_scale_2, sb_w_qkv_2, sb_w_o_2, mla_w_down_2, mla_q_norm_2,
    mla_kv_norm_2, mla_w_uq_2, mla_w_ukv_2, mla_w_o_2, fox_w_qkvf_2, fox_b_f_2, fox_w_o_2,
    ffn_w_gate_2, ffn_w_up_2, ffn_w_down_2, final_norm_2,
):
    x = first_block(
        x, w_in, b_in, lb_logits, hg_norm_g, rel_bias, w_proj_a, w_proj_b, w_out, ln1_g, ln1_b,
        w_group, b_group, w_expert, b_expert, w_gate_up, w_down, ln2_g, ln2_b,
    )
    return second_block(
        x, meta_2, norm_mix_2, norm_ffn_2, pool_w_2, pool_scale_2, sb_w_qkv_2, sb_w_o_2,
        mla_w_down_2, mla_q_norm_2, mla_kv_norm_2, mla_w_uq_2, mla_w_ukv_2, mla_w_o_2,
        fox_w_qkvf_2, fox_b_f_2, fox_w_o_2, ffn_w_gate_2, ffn_w_up_2, ffn_w_down_2,
        final_norm_2,
    )


_drawn_inputs = setup_inputs


def setup_inputs(seed=0):
    import zlib

    import numpy as np

    out = dict(_drawn_inputs(seed))
    spreads = {}
    factors = {'b_in': 3.787,
     'lb_logits': 5.752,
     'hg_norm_g': 3.24,
     'rel_bias': 3.893,
     'b_group': 4.096,
     'b_expert': 7.213,
     'ln2_b': 13.742,
     'norm_mix_2': 3.107,
     'norm_ffn_2': 3.443,
     'pool_scale_2': 3.699,
     'final_norm_2': 8.03}
    for name, (base, spread) in spreads.items():
        noise = np.random.default_rng([zlib.crc32(name.encode()), seed]).standard_normal(out[name].shape)
        drawn = base * np.exp(spread * noise) if base else spread * noise
        out[name] = __import__('jax').numpy.asarray(drawn.astype(out[name].dtype))
    for name, factor in factors.items():
        out[name] = (out[name] * factor).astype(out[name].dtype)
    return out
```

```python
import math

import numpy as np
import concourse.bass as bass
from concourse import mybir

F32 = mybir.dt.float32
F32R = mybir.dt.float32r
U32 = mybir.dt.uint32
I32 = mybir.dt.int32
ALU = mybir.AluOpType
ACT = mybir.ActivationFunctionType
AX = mybir.AxisListType.X

D = 1024
S = 256
NMETA = 16
L = S + NMETA
DFF = 2816
ALPHA = 2.0 ** 0.25
CAP = 64
KEEP = CAP
NE = 32
OVR = S - CAP
FAR = 1.0e6

CM = {}
_at = 0
for _n, _w in (("ident", 128), ("trineg", 128), ("negones", 128), ("ones", 128), ("ustrict", 128),
               ("masks", 8 * 128), ("iota", 256), ("inv", 16), ("iota4", 4), ("iota32", 32)):
    CM[_n] = (_at, _w)
    _at += _w
CMW = _at
PC = {}
_at = 0
for _n, _w in (("b_in", 44), ("lb", 8), ("hgn", 4), ("nm", 16), ("nf", 16), ("ps", 8), ("fn", 8)):
    PC[_n] = (_at, _w)
    _at += _w
PCW = _at


def shape_constants():
    p = np.arange(128)
    cm = np.zeros((128, CMW), np.float32)

    def put(name, a):
        o, w = CM[name]
        cm[:, o:o + w] = a

    put("ident", np.eye(128))
    put("trineg", -(p[:, None] >= p[None, :]).astype(np.float32))
    put("negones", -1.0)
    put("ones", 1.0)
    put("ustrict", (p[:, None] < p[None, :]).astype(np.float32))
    masks = []
    for m in (64, 32, 16, 8, 4, 2, 1):
        same = (p[:, None] // (2 * m)) == (p[None, :] // (2 * m))
        masks.append(same & (p[:, None] % (2 * m) < m) & (p[None, :] % (2 * m) >= m))
    masks.append(np.eye(128, dtype=bool))
    put("masks", np.concatenate(masks, 1).astype(np.float32))
    put("iota", np.arange(256)[None, :])
    put("inv", 1.0 / (np.arange(16) + 1.0)[None, :])
    put("iota4", np.arange(4)[None, :])
    put("iota32", np.arange(32)[None, :])
    d = np.arange(256)
    f = np.log(np.maximum(d, 1).astype(np.float32) / np.float32(16)) / np.float32(math.log(8.0)) * np.float32(16)
    bucket = np.where(d < 16, d, np.minimum(16 + f.astype(np.int32), 31))
    hot = np.zeros((33, 384), np.float32)
    hot[bucket, 127 + d] = 1.0
    hot[32, :127] = -1.0e30
    scan = np.ones((128, 1024), np.float32)
    scan[:, ::64] = 0.0
    return cm, hot, scan


class Queue:

    def __init__(self, eng, sem):
        self.eng, self.sem, self.n, self.seen = eng, sem, 0, {}

    def wait(self, *tokens):
        for t in tokens:
            if t is not None and self.seen.get(t[0].name, 0) < t[1]:
                self.seen[t[0].name] = t[1]
                self.eng.wait_ge(t[0], t[1])

    def go(self, f):
        self.n += 1
        f(self.eng).then_inc(self.sem, 1)
        return self.sem, self.n

    def quiet(self, f):
        f(self.eng)


def build(nc, t, out):
    sems = []

    def sem(name):
        s = nc.alloc_semaphore(name)
        sems.append(s)
        return s

    pe, act, dve, pool, sp = (Queue(q, sem(n)) for q, n in (
        (nc.tensor, "s_pe"), (nc.scalar, "s_act"), (nc.vector, "s_dve"), (nc.gpsimd, "s_pool"), (nc.sync, "s_sp")))
    dma_count = {}

    def dma(q, dst, src, s, **kw):
        dma_count[s.name] = dma_count.get(s.name, 0) + 16
        q.quiet(lambda e: e.dma_start(dst, src, **kw).then_inc(s, 16))
        return s, dma_count[s.name]

    base = (nc.sbuf_base + 63) // 64 * 64
    KB = 1024

    def sb(name, cols, at, dt=F32, rows=128):
        return nc.alloc_sbuf_tensor_at(name, [rows, cols], dt, offset=base + at)

    def view(x, off, dims, p0=0, rows=128):
        a = x[:, :]
        w = a.ap[0][0]
        return bass.AP(tensor=a.tensor, offset=p0 * w + off, ap=[[w, rows]] + [list(v) for v in dims])

    PS = nc.alloc_psum_tensor("PS", [128, 4096], F32)

    def bank(b, off, *dims, p0=0, rows=128):
        return view(PS, 512 * b + off, dims, p0, rows)

    free = [None] * 8

    def mm(o, a, b, start, stop, last=False, **kw):
        f = lambda e: e.matmul(o, a, b, start=start, stop=stop, **kw)
        return pe.go(f) if last else pe.quiet(f)

    RN, HN = 6, 3
    raw = [sb(f"raw{i}", 2048, 8 * KB * i) for i in range(RN)]
    hi = [sb(f"hi{i}", 2048, 48 * KB + 8 * KB * i, F32R) for i in range(HN)]
    lo = [sb(f"lo{i}", 2048, 72 * KB + 8 * KB * i, F32R) for i in range(HN)]
    cm = sb("cm", CMW, 96 * KB)
    pc = sb("pc", PCW, 96 * KB + 7936)
    small = sb("small", 128, 96 * KB + 7936 + 512)
    flag = sb("flag", 8, 96 * KB + 7936 + 1024, U32)
    A0 = 105 * KB

    def con(name, off=0, w=None, p0=0, rows=128):
        o, cw = CM[name]
        return view(cm, o + off, [[1, w or cw]], p0, rows)

    def par(name, i=0, w=1):
        return view(pc, PC[name][0] + i, [[1, w]])

    units = []

    def tcols(w, rows, c0, n):
        return w[rows[0]:rows[1], c0:c0 + n].rearrange("(c p) n -> p c n", p=128)

    win = t["w_in"]
    for nm in ("f", "q", "i", "mq", "mk", "mv", "g"):
        c0 = {"q": 0, "f": 512, "i": 1024, "g": 1536, "mq": 2048, "mk": 2560, "mv": 3072}[nm]
        for j in range(2):
            units.append((nm, j, tcols(win, (0, D), c0 + 256 * j, 256), 256, 8))
    for nm, c0 in (("ga", 3584), ("gb", 4608)):
        for j in range(4):
            units.append((nm, j, tcols(win, (0, D), c0 + 256 * j, 256), 256, 8))
    for nm in ("w_proj_a", "w_proj_b"):
        for j in range(2):
            units.append((nm, j, tcols(t[nm], (0, 512), 512 * j, 512), 512, 4))
    for j in range(4):
        units.append(("w_out", j, tcols(t["w_out"], (0, D), 256 * j, 256), 256, 8))

    def gu(e):
        for j in range(4):
            units.append(("gu", (e, j), tcols(t["w_gate_up"][e], (256 * j, 256 * j + 256), 0, 1024), 1024, 2))

    def dn(e):
        for j in range(2):
            units.append(("dn", (e, j), tcols(t["w_down"][e], (256 * j, 256 * j + 256), 0, 1024), 1024, 2))

    for e in range(NE):
        gu(e)
        if e:
            dn(e - 1)
    dn(NE - 1)

    def ffn_units(i):
        for f in range(11):
            units.append(("fg", (i, f), tcols(t["ffn_w_gate"][i], (0, D), 256 * f, 256), 256, 8))
            units.append(("fu", (i, f), tcols(t["ffn_w_up"][i], (0, D), 256 * f, 256), 256, 8))
        for c in range(4):
            for k in range(3):
                n = 8 if k < 2 else 6
                units.append(("fd", (i, c, k), tcols(t["ffn_w_down"][i], (1024 * k, 1024 * k + 128 * n), 256 * c, 256), 256, n))

    for g in range(4):
        units.append(("pw", g, tcols(t["pool_w"][g], (0, 256), 0, 256), 256, 2))
    ffn_units(0)
    for j in range(12):
        units.append(("qkv", j, tcols(t["sb_w_qkv"], (0, D), 256 * j, 256), 256, 8))
    for j in range(4):
        units.append(("wo", j, tcols(t["sb_w_o"], (0, D), 256 * j, 256), 256, 8))
    ffn_units(1)
    NU = len(units)

    s_raw = [sem(f"s_raw{i}") for i in range(RN)]
    loaded, hi_tok, lo_tok, used = {}, {}, {}, {}

    def load(i):
        if i >= NU:
            return
        _, _, src, n, c = units[i]
        if i >= RN:
            sp.wait(hi_tok[i - RN], lo_tok[i - RN])
        loaded[i] = dma(sp, view(raw[i % RN], 0, [[n, c], [1, n]]), src, s_raw[i % RN])

    state = {"prepped": 0, "next": 0}

    def prep():
        i = state["prepped"]
        if i >= NU:
            return
        state["prepped"] += 1
        kind, _, _, n, c = units[i]
        r, h, l = (view(x, 0, [[1, n * c]]) for x in (raw[i % RN], hi[i % HN], lo[i % HN]))
        hf = view(hi[i % HN], 0, [[1, n * c]]).bitcast(F32)
        act.wait(loaded[i], used.get(i - HN))
        hi_tok[i] = act.go(lambda e: e.copy(h, r))
        q = pool if kind == "dn" and units[i][1][1] == 0 else dve
        q.wait(loaded[i], hi_tok[i], used.get(i - HN))
        lo_tok[i] = q.go(lambda e: e.tensor_tensor(l, r, hf, ALU.subtract))
        load(i + RN)

    class Unit:
        pass

    def take(kind, tag):
        i = state["next"]
        state["next"] += 1
        assert units[i][0] == kind and units[i][1] == tag, (units[i][:2], kind, tag)
        while state["prepped"] <= min(i + 2, NU - 1):
            prep()
        pe.wait(hi_tok[i], lo_tok[i])
        u = Unit()
        n = units[i][3]
        u.i = i
        u.h = lambda k, c0, w: view(hi[i % HN], n * k + c0, [[1, w]])
        u.l = lambda k, c0, w: view(lo[i % HN], n * k + c0, [[1, w]])
        return u

    def release(u, tok):
        used[u.i] = tok

    def stationary_w(u, o, m, ks, xh, xl, start=True, stop=True):
        for n, k in enumerate(ks):
            a, b = start and n == 0, stop and n == len(ks) - 1
            mm(o, u.h(n, 128 * m, 128), xh(k), a, False)
            mm(o, u.h(n, 128 * m, 128), xl(k), False, False)
            tok = mm(o, u.l(n, 128 * m, 128), xh(k), False, b, last=(n == len(ks) - 1))
        return tok

    def moving_w(u, o, c0, w, ks, xh, xl, start=True, stop=True):
        for n, k in enumerate(ks):
            a, b = start and n == 0, stop and n == len(ks) - 1
            mm(o, xh(k), u.h(n, c0, w), a, False)
            mm(o, xl(k), u.h(n, c0, w), False, False)
            tok = mm(o, xh(k), u.l(n, c0, w), False, b, last=(n == len(ks) - 1))
        return tok

    at = A0
    def area(name, cols, dt=F32, rows=128):
        nonlocal at
        x = sb(name, cols, at, dt, rows)
        at += 4 * cols
        return x

    XH, XL = area("XH", 2048, F32R), area("XL", 2048, F32R)
    QT, BT, KT, VA, GT = (area(n, 1024) for n in ("QT", "BT", "KT", "VA", "GT"))
    MQ, MK, MV = (area(n, 1024) for n in ("MQ", "MK", "MV"))
    SGA, SGB = area("SGA", 2048), area("SGB", 2048)
    D0, D1 = area("D0", 1024), area("D1", 1024)
    at -= 4096
    SL = area("SL", 1024)
    QE, KE = area("QE", 1024), area("KE", 1024)
    AA0, AA1 = area("AA0", 1024), area("AA1", 512)
    TT = [area(f"TT{i}", 512) for i in range(2)]
    PT = area("PT", 768)
    rowp = area("rowp", 1060 , rows=1)
    assert at <= 207 * KB, at
    SCN = sb("SCN", 1024, A0 + 4 * (2048 * 2 + 1024 * 8 + 4096 + 1024))
    xraw = sb("xraw", 2048, A0 + 4 * (2048 * 2 + 1024 * 8))
    hot = sb("hot", 384, A0 + 4 * (2048 * 3 + 1024 * 8), rows=33)
    rbs = sb("rbs", 8, A0 + 4 * (2048 * 3 + 1024 * 8) + 1536, rows=33)
    wtab = sb("wtab", 384, A0 + 4 * (2048 * 3 + 1024 * 8) + 1600, rows=8)

    d_tab = nc.dram_tensor("d_tab", (8, 384), F32).ap()
    d_o = nc.dram_tensor("d_o", (NE * OVR, D), F32).ap()
    d_y = nc.dram_tensor("d_y", (NE * CAP, D), F32).ap()

    s_x, s_c, s_p, s_r, s_scn, s_hot, s_xt = (sem(n) for n in ("s_x", "s_c", "s_p", "s_r", "s_scn", "s_hot", "s_xt"))
    tx = dma(sp, xraw[:, :], t["xT"], s_x)
    load(0)
    tp = dma(act, pc[:, :], t["pc"], s_p)
    tr = dma(act, rowp[:, :], t["rows"], s_r)
    tcm = dma(act, cm[:, :], t["cm"], s_c)
    load(1)
    dma(act, rbs[:, :], t["rb"], s_hot)
    thot = dma(act, hot[:, :], t["hot"], s_hot)
    tscn = dma(act, SCN[:, :], t["scan"], s_scn)
    load(2)
    load(3)
    load(4)
    load(5)

    act.wait(tx)
    txh = act.go(lambda e: e.copy(XH[:, :], xraw[:, :]))
    dve.wait(tx, txh)
    txl = dve.go(lambda e: e.tensor_tensor(XL[:, :], xraw[:, :], XH[:, :].bitcast(F32), ALU.subtract))
    xh = lambda k: view(XH, 256 * k, [[1, 256]])
    xl = lambda k: view(XL, 256 * k, [[1, 256]])
    xht = lambda i: (lambda k: view(XH, 256 * k + 128 * i, [[1, 128]]))
    xlt = lambda i: (lambda k: view(XL, 256 * k + 128 * i, [[1, 128]]))

    sm = lambda o, w=1: view(small, o, [[1, w]])
    dve.wait(tp)
    a0 = dve.go(lambda e: e.tensor_tensor(sm(0, 4), par("lb", 0, 4), par("lb", 4, 4), ALU.max))
    dve.wait(a0)
    dve.go(lambda e: e.tensor_tensor(sm(4, 4), par("lb", 0, 4), sm(0, 4), ALU.subtract))
    a0 = dve.go(lambda e: e.tensor_tensor(sm(8, 4), par("lb", 4, 4), sm(0, 4), ALU.subtract))
    nb = dve.go(lambda e: e.tensor_scalar(sm(32, 4), par("b_in", 4, 4), -1.0, None, ALU.mult))
    act.wait(a0)
    a0 = act.go(lambda e: e.activation(sm(12, 8), sm(4, 8), ACT.Exp))
    dve.wait(a0)
    a0 = dve.go(lambda e: e.tensor_tensor(sm(20, 4), sm(12, 4), sm(16, 4), ALU.add))
    dve.wait(a0)
    a0 = dve.go(lambda e: e.reciprocal(sm(20, 4), sm(20, 4)))
    dve.wait(a0)
    dve.go(lambda e: e.tensor_tensor(sm(24, 4), sm(12, 4), sm(20, 4), ALU.mult))
    tlb = dve.go(lambda e: e.tensor_tensor(sm(28, 4), sm(16, 4), sm(20, 4), ALU.mult))
    LB, OLB = 24, 28
    dve.go(lambda e: e.memset(QE[:, :], 0.0))
    tz = dve.go(lambda e: e.memset(KE[:, :], 0.0))

    s_tab = sem("s_tab")
    s_tt = [sem("s_tt0"), sem("s_tt1")]
    pe.wait(thot)
    tk = mm(bank(7, 0, [1, 384], rows=8), rbs[:, :], hot[:, :], True, True, last=True)
    dve.wait(tk)
    tk = dve.go(lambda e: e.tensor_copy(wtab[:, :], bank(7, 0, [1, 384], rows=8)))
    free[7] = tk
    act.wait(tk)
    ttab = dma(act, d_tab, wtab[:, :], s_tab)
    pool.wait(ttab)

    def toeplitz(pair, q):
        return dma(q, view(TT[pair % 2], 0, [[256, 2], [1, 256]]),
                   bass.AP(tensor=d_tab.tensor, offset=768 * pair, ap=[[1, 128], [384, 2], [1, 256]]), s_tt[pair % 2])

    tt_tok = {0: toeplitz(0, pool), 1: toeplitz(1, pool)}

    nproj = [0]

    def project_t(nm, j, evac):
        b = nproj[0] % 3
        nproj[0] += 1
        u = take(nm, j)
        pe.wait(free[b], txh, txl)
        for m in range(2):
            tok = stationary_w(u, bank(b, 256 * m, [1, 256]), m, range(8), xh, xl)
        release(u, tok)
        free[b] = evac(b, tok)

    def project_n(nm, j, row, evac):
        b = nproj[0] % 3
        nproj[0] += 1
        u = take(nm, j)
        pe.wait(free[b], txh, txl, tr, tcm)
        for i in range(2):
            o = bank(b, 256 * i, [1, 256])
            mm(o, con("ones", p0=0, rows=1), view(rowp, row + 256 * j, [[1, 256]], rows=1), True, False)
            tok = moving_w(u, o, 0, 256, range(8), xht(i), xlt(i), start=False)
        release(u, tok)
        free[b] = evac(b, tok)

    fk = {}

    def evac_f(j):
        def f(b, tok):
            act.wait(tok, tp, nb)
            for m in range(2):
                h = 2 * j + m
                act.go(lambda e: e.activation(view(BT, 256 * h, [[1, 256]]), bank(b, 256 * m, [1, 256]), ACT.Sigmoid, bias=par("b_in", 4 + h)))
                r = act.go(lambda e: e.activation(view(KT, 256 * h, [[1, 256]]), bank(b, 256 * m, [1, 256]), ACT.Sigmoid, bias=sm(32 + h), scale=-1.0))
                dve.wait(r, tlb)
                fk["k", h] = dve.go(lambda e: e.tensor_scalar(view(KT, 256 * h, [[1, 256]]), view(KT, 256 * h, [[1, 256]]), sm(OLB + h), None, ALU.mult))
                fk["f", h] = dve.go(lambda e: e.tensor_scalar(view(BT, 256 * h, [[1, 256]]), view(BT, 256 * h, [[1, 256]]), sm(OLB + h), sm(LB + h), ALU.mult, ALU.add))
            return r
        return f

    def evac_act(dst, bcol, func, key):
        def f(b, tok):
            act.wait(tok, tp)
            for m in range(2):
                r = act.go(lambda e, m=m: e.activation(dst(m), bank(b, 256 * m, [1, 256]), func, bias=par("b_in", bcol + m)))
            fk[key] = r
            return r
        return f

    def evac_tok(dst, key):
        def f(b, tok):
            dve.wait(tok)
            r = dve.go(lambda e: e.tensor_copy(dst, bank(b, 0, [256, 2], [1, 256])))
            fk[key] = r
            return r
        return f

    project_t("f", 0, evac_f(0))
    project_t("f", 1, evac_f(1))
    act.wait(fk["f", 3])
    tk = act.go(lambda e: e.activation(BT[:, :], BT[:, :], ACT.Ln))
    dve.wait(tk, tscn)
    tb = dve.go(lambda e: e.tensor_tensor_scan(BT[:, :], SCN[:, :], BT[:, :], 0.0, ALU.mult, ALU.add))
    for j in range(2):
        project_t("q", j, evac_act(lambda m, j=j: view(QT, 256 * (2 * j + m), [[1, 256]]), 2 * j, ACT.Silu, ("q", j)))

    DE = [D0, D1]
    LV = [128, 64, 32, 16, 8, 4, 2, 1, 0]
    lev = {"free": {0: None, 1: tb}}

    def level_d(n):
        m, d = LV[n], DE[n % 2]
        if m == 0:
            return
        pool.wait(tb, lev["free"][n % 2])
        if m == 128:
            blk = lambda x, c, k: view(x, 64 * c, [[256, 4], [64, k], [1, 64]])
            end = lambda c, k: view(BT, 64 * c + 63, [[256, 4], [64, k], [0, 64]])
            r = pool.go(lambda e: e.tensor_tensor(blk(d, 0, 2), end(0, 2), blk(BT, 0, 2), ALU.subtract))
            pool.wait(r)
            pool.go(lambda e: e.tensor_tensor(blk(d, 0, 1), blk(d, 0, 1), end(1, 1), ALU.add))
            r = pool.go(lambda e: e.tensor_tensor(blk(d, 3, 1), blk(BT, 3, 1), end(2, 1), ALU.add))
            act.wait(r)
            act.go(lambda e: e.activation(view(d, 128, [[256, 4], [1, 64]]), view(BT, 128, [[256, 4], [1, 64]]), ACT.Exp))
            act.go(lambda e: e.activation(view(d, 192, [[256, 4], [1, 64]]), view(d, 192, [[256, 4], [1, 64]]), ACT.Exp))
            r = act.go(lambda e: e.activation(view(d, 0, [[256, 4], [1, 128]]), view(d, 0, [[256, 4], [1, 128]]), ACT.Exp))
        else:
            nbk = 512 // m
            half = lambda x, o: view(x, o, [[2 * m, nbk], [1, m]])
            mid = view(BT, m - 1, [[2 * m, nbk], [0, m]])
            r = pool.go(lambda e: e.tensor_tensor(half(d, 0), mid, half(BT, 0), ALU.subtract))
            if m < 64:
                r = pool.go(lambda e: e.tensor_tensor(half(d, m), half(BT, m), mid, ALU.subtract))
                act.wait(r)
                r = act.go(lambda e: e.activation(d[:, :], d[:, :], ACT.Exp))
            else:
                act.wait(r)
                act.go(lambda e: e.activation(half(d, 0), half(d, 0), ACT.Exp))
                r = act.go(lambda e: e.activation(half(d, m), half(BT, m), ACT.Exp))
        lev["e", n] = r

    def level_s(n):
        m, d = LV[n], DE[n % 2]
        dve.wait(lev.get(("e", n)), fk["q", 1], fk["k", 3], fk["k", 1], lev.get("pe"), tz)
        if m == 128:
            lh = lambda x, o: view(x, o, [[256, 4], [1, 128]])
            dve.go(lambda e: e.tensor_tensor(lh(KE, 0), lh(KT, 0), lh(d, 0), ALU.mult))
            r = dve.go(lambda e: e.tensor_tensor(lh(QE, 128), lh(QT, 128), lh(d, 128), ALU.mult))
        elif m:
            half = lambda x, o: view(x, o, [[2 * m, 512 // m], [1, m]])
            dve.go(lambda e: e.tensor_tensor(half(KE, 0), half(KT, 0), half(d, 0), ALU.mult))
            r = dve.go(lambda e: e.tensor_tensor(half(QE, m), half(QT, m), half(d, m), ALU.mult))
        else:
            r = None
        if m:
            lev["free"][n % 2] = r
        kx, qx = (KE, QE) if m else (KT, QT)
        pe.wait(r, fk["q", 1], fk["k", 3], free[3], free[4])
        if m == 128:
            for h in range(4):
                r = mm(bank(3, 128 * h, [1, 128]), view(kx, 256 * h, [[1, 128]]), view(qx, 256 * h + 128, [[1, 128]]), True, True, last=(h == 3))
            dve.wait(r)
            free[3] = dve.go(lambda e: e.tensor_copy(view(AA0, 128, [[256, 4], [1, 128]]), bank(3, 0, [128, 4], [1, 128])))
        else:
            for i in range(2):
                for h in range(4):
                    r = mm(bank(3 + i, 128 * h, [1, 128]), view(kx, 256 * h + 128 * i, [[1, 128]]),
                           view(qx, 256 * h + 128 * i, [[1, 128]]), True, True, last=(h == 3))
                mask = view(cm, CM["masks"][0] + 128 * (n - 1), [[0, 4], [1, 128]]).bitcast(U32)
                o = view(AA0, 0, [[256, 4], [1, 128]]) if i == 0 else view(AA1, 0, [[128, 4], [1, 128]])
                dve.wait(r, tcm, lev["a"])
                free[3 + i] = dve.go(lambda e, i=i, o=o, mask=mask: e.copy_predicated(o, mask, bank(3 + i, 0, [128, 4], [1, 128])))
                lev["acc"] = free[3 + i]
        lev["pe"] = r

    dve.go(lambda e: e.memset(AA0[:, :], 0.0))
    lev["a"] = dve.go(lambda e: e.memset(AA1[:, :], 0.0))
    dve.wait(lev["a"])
    level_d(0)
    level_d(1)
    n = 0
    for j in range(2):
        project_n("i", j, 0, evac_tok(view(VA, 256 * j, [[512, 2], [1, 256]]), ("v", j)))
        level_s(n)
        level_d(n + 2)
        n += 1
    for nm, c0, dst in (("mq", 16, MQ), ("mk", 20, MK)):
        for j in range(2):
            project_t(nm, j, evac_act(lambda m, j=j, dst=dst: view(dst, 256 * (2 * j + m), [[1, 256]]), c0 + 2 * j, ACT.Identity, (nm, j)))
            level_s(n)
            if n + 2 < 9:
                level_d(n + 2)
            n += 1
    for j in range(2):
        project_n("mv", j, 512, evac_tok(view(MV, 256 * j, [[512, 2], [1, 256]]), ("mv", j)))
        level_s(n)
        if n + 2 < 9:
            level_d(n + 2)
        n += 1
    for j in range(2):
        project_t("g", j, evac_act(lambda m, j=j: view(GT, 256 * (2 * j + m), [[1, 256]]), 12 + 2 * j, ACT.Silu, ("g", j)))
        if n < 9:
            level_s(n)
            n += 1
    for h in range(4):
        dve.wait(fk["g", h // 2])
        fk["gn"] = dve.go(lambda e, h=h: e.tensor_scalar(view(GT, 256 * h, [[1, 256]]), view(GT, 256 * h, [[1, 256]]), par("hgn", h), None, ALU.mult))

    def gate(nm, j, c0, dst):
        project_t(nm, j, evac_act(lambda m: view(dst, 256 * (2 * j + m), [[1, 256]]), c0 + 2 * j, ACT.Sigmoid, (nm, j)))

    OT = sb("OT", 1024, A0 + 4 * (2048 * 2 + 1024 * 8 + 4096))
    SQ = QE
    OAH = sb("OAH", 1024, A0 + 4 * (2048 * 2), F32R)
    OAL = sb("OAL", 1024, A0 + 4 * (2048 * 2 + 1024), F32R)
    OBH = sb("OBH", 1024, A0 + 4 * (2048 * 2 + 2048), F32R)
    OBL = sb("OBL", 1024, A0 + 4 * (2048 * 2 + 3072), F32R)
    gate("ga", 0, 28, SGA)
    pe.wait(lev["acc"], free[3], fk["v", 0], fk["v", 1], free[5], free[6])
    for h in range(4):
        o = lambda c, w: bank(5 + h // 2, 256 * (h % 2) + c, [1, w])
        mm(o(0, 256), view(VA, 128 * h, [[1, 128]]), view(AA0, 256 * h, [[1, 256]]), True, False)
        r = mm(o(128, 128), view(VA, 512 + 128 * h, [[1, 128]]), view(AA1, 128 * h, [[1, 128]]), False, True, last=(h % 2 == 1))
    dve.wait(r)
    to = dve.go(lambda e: e.tensor_copy(OT[:, :], bank(5, 0, [1, 1024])))
    act.wait(r, lev["pe"], to)
    tq = act.go(lambda e: e.activation(SQ[:, :], OT[:, :], ACT.Square))
    gate("ga", 1, 28, SGA)
    pe.wait(tq, to, tcm)
    for i in range(2):
        r = mm(bank(5 + i, 0, [1, 512]), con("ones"), view(SQ, 512 * i, [[1, 512]]), True, True, last=True)
    dve.wait(r, tq)
    r = dve.go(lambda e: e.tensor_scalar(KE[:, :], bank(5, 0, [1, 1024]), 1.0 / 128, 1e-5, ALU.mult, ALU.add))
    free[5] = free[6] = r
    dve.wait(r)
    r = dve.go(lambda e: e.reciprocal(KE[:, :], KE[:, :]))
    act.wait(r)
    r = act.go(lambda e: e.activation(KE[:, :], KE[:, :], ACT.Sqrt))
    dve.wait(r, to)
    r = dve.go(lambda e: e.tensor_tensor(OT[:, :], OT[:, :], KE[:, :], ALU.mult))
    dve.wait(r, fk["gn"])
    r = dve.go(lambda e: e.tensor_tensor(OT[:, :], OT[:, :], GT[:, :], ALU.mult))
    act.wait(r, lev["pe"])
    toh = act.go(lambda e: e.copy(OAH[:, :], OT[:, :]))
    dve.wait(toh)
    tol = dve.go(lambda e: e.tensor_tensor(OAL[:, :], OT[:, :], OAH[:, :].bitcast(F32), ALU.subtract))
    xtok = sb("xtok", 2048, A0 + 4 * (2048 * 3 + 1024 * 8 + 2048 + 2048))
    pool.wait(toh, tol)
    txt = dma(pool, view(xtok, 0, [[1024, 2], [1, 1024]]), t["x"][0].rearrange("(i p) n -> p i n", p=128), s_xt)
    gate("ga", 2, 28, SGA)
    gate("ga", 3, 28, SGA)

    moba = {"pt": [None, None], "sl": tol}

    def moba_scores(g):
        pe.wait(fk["mq", 0], fk["mq", 1], fk["mk", 0], fk["mk", 1], free[3], free[4])
        for a in range(2):
            p0 = 64 * a
            mq = lambda i: view(MQ, 256 * g + 128 * i, [[1, 128]], p0, 64)
            mm(bank(3 + a, 0, [1, 128]), mq(0), view(MK, 256 * g, [[1, 128]], p0, 64), True, True)
            r = mm(bank(3 + a, 128, [1, 256]), mq(1), view(MK, 256 * g, [[1, 256]], p0, 64), True, True, last=(a == 1))
        x = TT[g % 2]
        dve.wait(r, tt_tok[g], moba["sl"], moba["pt"][0], moba["pt"][1])
        r0 = dve.go(lambda e: e.scalar_tensor_tensor(view(SL, 0, [[384, 2], [1, 128]]), bank(3, 0, [512, 2], [1, 128]), 0.125,
                                                     view(x, 127, [[256, 2], [-1, 128]]), ALU.mult, ALU.add))
        r1 = dve.go(lambda e: e.scalar_tensor_tensor(view(SL, 128, [[384, 2], [1, 256]]), bank(3, 128, [512, 2], [1, 256]), 0.125,
                                                     view(x, 255, [[256, 2], [-1, 256]]), ALU.mult, ALU.add))
        free[3] = free[4] = r1
        if g + 2 < 4:
            pool.wait(r1)
            tt_tok[g + 2] = toeplitz(g + 2, pool)
        dve.wait(r1)
        dve.go(lambda e: e.tensor_reduce(sm(64, 2), view(SL, 0, [[384, 2], [1, 128]]), AX, ALU.max))
        r = dve.go(lambda e: e.tensor_reduce(sm(66, 2), view(SL, 128, [[384, 2], [1, 256]]), AX, ALU.max))
        dve.wait(r)
        r = dve.go(lambda e: e.tensor_scalar(sm(68, 4), sm(64, 4), -1.0, None, ALU.mult))
        act.wait(r)
        for a in range(2):
            for i in range(2):
                s = view(SL, 384 * a + 128 * i, [[1, 128 + 128 * i]])
                r = act.go(lambda e, s=s, c=68 + 2 * i + a, z=72 + 2 * i + a: e.activation(s, s, ACT.Exp, bias=sm(c), accum_out=sm(z)))
        dve.wait(r)
        r = dve.go(lambda e: e.reciprocal(sm(76, 4), sm(72, 4)))
        dve.wait(r)
        for a in range(2):
            for i in range(2):
                s = view(SL, 384 * a + 128 * i, [[1, 128 + 128 * i]])
                r = dve.go(lambda e, s=s, c=76 + 2 * i + a: e.tensor_scalar(s, s, sm(c), None, ALU.mult))
        moba["p"] = r

    def moba_out(g):
        pe.wait(moba["p"], tcm, free[5], free[6], free[7])
        tr_ = []
        for a in range(2):
            for c, s in ((0, 0), (128, 128), (256, 256)):
                r = pe.go(lambda e, c=c, s=s, a=a: e.transpose(bank(5 + a, c, [1, 128]), view(SL, 384 * a + s, [[1, 128]]), con("ident")))
            q = act if a else dve
            q.wait(r, moba.get("pv"))
            f = (lambda e, a=a: e.copy(view(PT, 384 * a, [[1, 384]]), bank(5 + a, 0, [1, 384]))) if a else \
                (lambda e, a=a: e.tensor_copy(view(PT, 384 * a, [[1, 384]]), bank(5 + a, 0, [1, 384])))
            free[5 + a] = q.go(f)
            tr_.append(free[5 + a])
            moba["pt"][a] = r
        pe.wait(*tr_)
        pe.wait(fk["mv", 0], fk["mv", 1])
        for a in range(2):
            h = 2 * g + a
            mm(bank(7, 0, [1, 256], p0=64 * a, rows=64), view(MV, 64 * h, [[1, 64]]), view(PT, 384 * a, [[1, 256]]), True, False)
            r = mm(bank(7, 128, [1, 128], p0=64 * a, rows=64), view(MV, 512 + 64 * h, [[1, 64]]), view(PT, 384 * a + 256, [[1, 128]]), False, True, last=(a == 1))
        moba["pv"] = r
        act.wait(r, tol)
        rh = act.go(lambda e: e.copy(view(OBH, 256 * g, [[1, 256]]), bank(7, 0, [1, 256])))
        dve.wait(rh)
        free[7] = dve.go(lambda e: e.tensor_tensor(view(OBL, 256 * g, [[1, 256]]), bank(7, 0, [1, 256]),
                                                   view(OBH, 256 * g, [[1, 256]]).bitcast(F32), ALU.subtract))
        moba["hl"] = (rh, free[7])

    moba_scores(0)
    for g in range(4):
        gate("gb", g, 36, SGB)
        moba_out(g)
        if g < 3:
            moba_scores(g + 1)

    MXH = sb("MXH", 2048, A0, F32R)
    MXL = sb("MXL", 2048, A0 + 8192, F32R)
    xdone = used[state["next"] - 1]
    mix = {}
    for w, src, sg, need in (("w_proj_a", (OAH, OAL), SGA, (toh, tol)), ("w_proj_b", (OBH, OBL), SGB, moba["hl"])):
        for j in range(2):
            b = 0 if j == 0 else 2
            u = take(w, j)
            pe.wait(*need)
            pe.wait(free[b], free[b + 1])
            for m in range(4):
                tok = stationary_w(u, bank(b + m // 2, 256 * (m % 2), [1, 256]), m, range(4),
                                   lambda k: view(src[0], 256 * k, [[1, 256]]), lambda k: view(src[1], 256 * k, [[1, 256]]))
            release(u, tok)
            dve.wait(tok, fk["ga", 3], fk["gb", 3])
            s = view(sg, 1024 * j, [[1, 1024]])
            r = dve.go(lambda e, s=s, b=b: e.tensor_tensor(s, bank(b, 0, [1, 1024]), s, ALU.mult))
            free[b] = free[b + 1] = r
            if w == "w_proj_b":
                dve.wait(r, mix["a", j])
                o, x = view(SGA, 1024 * j, [[1, 1024]]), view(SGB, 1024 * j, [[1, 1024]])
                r = dve.go(lambda e, o=o, x=x: e.tensor_tensor(o, o, x, ALU.add))
                act.wait(r, xdone)
                h, l = view(MXH, 1024 * j, [[1, 1024]]), view(MXL, 1024 * j, [[1, 1024]])
                rh = act.go(lambda e, o=o, h=h: e.copy(h, o))
                dve.wait(rh, xdone)
                mix["b", j] = (rh, dve.go(lambda e, o=o, h=h, l=l: e.tensor_tensor(l, o, h.bitcast(F32), ALU.subtract)))
            else:
                mix["a", j] = r
    LG = sb("LG", 1024, A0 + 56 * KB)
    LBT = sb("LBT", 1024, A0 + 60 * KB)
    s_ln, s_ln2 = sem("s_ln"), sem("s_ln2")

    def bcast_row(q, dst, src, s_ln):
        return dma(q, dst[:, :], bass.AP(tensor=src.tensor, offset=src.offset, ap=[[0, 128], [1, 1024]]), s_ln)

    act_last_sg = mix["b", 1]
    act.wait(*act_last_sg)
    bcast_row(act, LG, t["ln1_g"], s_ln)
    tln = bcast_row(act, LBT, t["ln1_b"], s_ln)
    for j in range(4):
        u = take("w_out", j)
        pe.wait(*mix["b", 0])
        pe.wait(*mix["b", 1])
        for i in range(2):
            b = 4 + 2 * i + j // 2
            pe.wait(free[b])
            tok = moving_w(u, bank(b, 256 * (j % 2), [1, 256]), 0, 256, range(8),
                           lambda k: view(MXH, 256 * k + 128 * i, [[1, 128]]), lambda k: view(MXL, 256 * k + 128 * i, [[1, 128]]))
            mix["o", i] = tok
        release(u, tok)

    X1 = sb("X1", 2048, A0 + 16 * KB)
    X1H = sb("X1H", 2048, A0, F32R)
    X1L = sb("X1L", 2048, A0 + 8 * KB, F32R)
    RTR = sb("RTR", 1024, A0 + 24 * KB)
    ST = sb("ST", 64, A0 + 28 * KB)

    def layer_norm(i, xin, g, b, tok, tl, reads=None):
        o = view(xin, 1024 * i, [[1, 1024]])
        st = lambda c, w: view(ST, 32 * i + c, [[1, w]])
        dve.wait(tok)
        dve.go(lambda e: e.bn_stats(st(0, 6), view(xin, 1024 * i, [[1, 512]])))
        r = dve.go(lambda e: e.bn_stats(st(6, 6), view(xin, 1024 * i + 512, [[1, 512]])))
        dve.wait(r)
        r = dve.go(lambda e: e.bn_aggr(st(12, 2), st(0, 12)))
        dve.wait(r)
        r = dve.go(lambda e: e.tensor_scalar(st(14, 1), st(13, 1), 1e-5, None, ALU.add))
        dve.wait(r)
        r = dve.go(lambda e: e.reciprocal(st(14, 1), st(14, 1)))
        act.wait(r)
        r = act.go(lambda e: e.activation(st(14, 1), st(14, 1), ACT.Sqrt))
        dve.wait(r)
        r = dve.go(lambda e: e.tensor_scalar(o, o, st(12, 1), st(14, 1), ALU.subtract, ALU.mult))
        dve.wait(r, tl)
        r = dve.go(lambda e: e.tensor_tensor(o, o, g[:, :], ALU.mult))
        dve.wait(r)
        return dve.go(lambda e: e.tensor_tensor(o, o, b[:, :], ALU.add))

    x1_tok = []
    for i in range(2):
        dve.wait(mix["o", i], txt)
        r = dve.go(lambda e, i=i: e.scalar_tensor_tensor(view(X1, 1024 * i, [[1, 1024]]), view(xtok, 1024 * i, [[1, 1024]]), ALPHA,
                                                         bank(4 + 2 * i, 0, [1, 1024]), ALU.mult, ALU.add))
        free[4 + 2 * i] = free[5 + 2 * i] = r
        x1_tok.append(layer_norm(i, X1, LG, LBT, r, tln))
    wout_done = used[state["next"] - 1]

    X1T = sb("X1T", 2048, A0 + 32 * KB)
    WR = sb("WR", 288, A0 + 40 * KB)
    s_wr = sem("s_wr")
    act.wait(*x1_tok)
    twr = dma(act, WR[:, :], t["wr"], s_wr)
    for i in range(2):
        pe.wait(x1_tok[i])
        pe.wait(free[2 * i], free[2 * i + 1])
        for k in range(8):
            r = pe.go(lambda e, i=i, k=k: e.transpose(bank(2 * i, 128 * k, [1, 128]), view(X1, 1024 * i + 128 * k, [[1, 128]]), con("ident"))) \
                if k == 7 else pe.quiet(lambda e, i=i, k=k: e.transpose(bank(2 * i, 128 * k, [1, 128]), view(X1, 1024 * i + 128 * k, [[1, 128]]), con("ident")))
        act.wait(r)
        free[2 * i] = free[2 * i + 1] = act.go(lambda e, i=i: e.copy(view(X1T, 128 * i, [[256, 8], [1, 128]]), bank(2 * i, 0, [128, 8], [1, 128])))
    pe.wait(twr, free[0], free[2], free[4], tr)
    for i in range(2):
        o = bank(4, 64 * i, [1, 36])
        mm(o, con("ones", rows=1), view(rowp, 1024, [[1, 36]], rows=1), True, False)
        for k in range(8):
            r = mm(o, view(X1T, 256 * k + 128 * i, [[1, 128]]), view(WR, 36 * k, [[1, 36]]), False, k == 7, last=(k == 7))
    act.wait(wout_done, *x1_tok)
    tx1h = act.go(lambda e: e.copy(X1H[:, :], X1[:, :]))
    rt = lambda o, *d: view(RTR, o, list(d))
    LGT, GP, GM, GI, EXP, OH, EM, ES, V8, I8, EF, O0, O1, OS, RK, RKM, CNT, RA, DST, ROW, TMP = \
        0, 72, 88, 104, 120, 128, 136, 200, 216, 232, 250, 256, 320, 384, 448, 512, 576, 640, 648, 656, 664
    UI = sb("UI", 64, A0 + 28 * KB + 256, U32)
    OV, OD, OVM, MAXC = 680, 684, 688, 692
    dve.wait(r)
    r0 = dve.go(lambda e: e.tensor_copy(rt(LGT, [36, 2], [1, 36]), bank(4, 0, [64, 2], [1, 36])))
    free[4] = r0
    r = dve.go(lambda e: e.memset(rt(GP, [1, 16]), -3.0e38))
    dve.wait(r, r0)
    r = dve.go(lambda e: e.tensor_copy(rt(GP, [8, 2], [1, 4]), rt(LGT, [36, 2], [1, 4])))
    dve.wait(r)
    for i in range(2):
        r = dve.go(lambda e, i=i: e.max(rt(GM + 8 * i, [1, 8]), rt(GP + 8 * i, [1, 8])))
    dve.wait(r)
    for i in range(2):
        r = dve.go(lambda e, i=i: e.max_index(view(UI, 8 * i, [[1, 8]]), rt(GM + 8 * i, [1, 8]), rt(GP + 8 * i, [1, 8])))
    r2 = dve.go(lambda e: e.tensor_tensor(rt(TMP, [4, 2], [1, 4]), rt(GP, [8, 2], [1, 4]), rt(GM, [8, 2], [0, 4]), ALU.subtract))
    act.wait(r2)
    re = act.go(lambda e: e.activation(rt(TMP, [1, 8]), rt(TMP, [1, 8]), ACT.Exp))
    dve.wait(r)
    r = dve.go(lambda e: e.tensor_copy(rt(GI, [1, 2]), view(UI, 0, [[8, 2]])))
    dve.wait(r)
    r = dve.go(lambda e: e.tensor_tensor(rt(OH, [4, 2], [1, 4]), view(cm, CM["iota4"][0], [[0, 2], [1, 4]]), rt(GI, [1, 2], [0, 4]), ALU.is_equal))
    dve.wait(r)
    r = dve.go(lambda e: e.tensor_tensor(rt(EM, [32, 2], [8, 4], [1, 8]), rt(LGT + 4, [36, 2], [8, 4], [1, 8]), rt(OH, [4, 2], [1, 4], [0, 8]), ALU.mult))
    dve.wait(r)
    r = dve.go(lambda e: e.tensor_reduce(rt(ES, [8, 2], [1, 8]), rt(EM, [32, 2], [1, 8], [8, 4]), AX, ALU.add))
    dve.wait(r)
    for i in range(2):
        r = dve.go(lambda e, i=i: e.max(rt(V8 + 8 * i, [1, 8]), rt(ES + 8 * i, [1, 8])))
    dve.wait(r)
    for i in range(2):
        r = dve.go(lambda e, i=i: e.max_index(view(UI, 16 + 8 * i, [[1, 8]]), rt(V8 + 8 * i, [1, 8]), rt(ES + 8 * i, [1, 8])))
    dve.wait(r)
    r = dve.go(lambda e: e.tensor_copy(rt(EF, [2, 2], [1, 2]), view(UI, 16, [[8, 2], [1, 2]])))
    dve.wait(r)
    r = dve.go(lambda e: e.scalar_tensor_tensor(rt(EF, [2, 2], [1, 2]), rt(GI, [1, 2], [0, 2]), 8.0, rt(EF, [2, 2], [1, 2]), ALU.mult, ALU.add))
    dve.wait(r)
    for a, o in ((0, O0), (1, O1)):
        r = dve.go(lambda e, a=a, o=o: e.tensor_tensor(rt(o, [32, 2], [1, 32]), view(cm, CM["iota32"][0], [[0, 2], [1, 32]]), rt(EF + a, [2, 2], [0, 32]), ALU.is_equal))
    dve.wait(r)
    ros = dve.go(lambda e: e.tensor_tensor(rt(OS, [1, 64]), rt(O0, [1, 64]), rt(O1, [1, 64]), ALU.add))
    pe.wait(ros, free[5])
    mm(bank(5, 0, [1, 32]), con("ustrict"), rt(OS, [1, 32]), True, True)
    mm(bank(5, 32, [1, 32]), con("ones"), rt(OS, [1, 32]), True, False)
    mm(bank(5, 32, [1, 32]), con("ustrict"), rt(OS + 32, [1, 32]), False, True)
    mm(bank(5, 64, [1, 32]), con("ones"), rt(OS, [1, 32]), True, False)
    r = mm(bank(5, 64, [1, 32]), con("ones"), rt(OS + 32, [1, 32]), False, True, last=True)
    GW = 700
    dve.wait(re)
    dve.go(lambda e: e.tensor_reduce(rt(GW, [1, 2]), rt(TMP, [4, 2], [1, 4]), AX, ALU.add))
    rd = dve.go(lambda e: e.tensor_tensor(rt(GW + 2, [1, 2]), rt(V8 + 1, [8, 2]), rt(V8, [8, 2]), ALU.subtract))
    act.wait(rd)
    rd = act.go(lambda e: e.activation(rt(GW + 2, [1, 2]), rt(GW + 2, [1, 2]), ACT.Exp))
    dve.wait(rd)
    rd = dve.go(lambda e: e.tensor_scalar(rt(GW + 4, [1, 2]), rt(GW + 2, [1, 2]), 1.0, None, ALU.add))
    dve.wait(rd)
    rd = dve.go(lambda e: e.tensor_tensor(rt(GW + 4, [1, 2]), rt(GW + 4, [1, 2]), rt(GW, [1, 2]), ALU.mult))
    dve.wait(rd)
    rd = dve.go(lambda e: e.reciprocal(rt(GW + 6, [1, 2]), rt(GW + 4, [1, 2])))
    dve.wait(rd)
    tw = dve.go(lambda e: e.tensor_tensor(rt(GW + 8, [1, 2]), rt(GW + 6, [1, 2]), rt(GW + 2, [1, 2]), ALU.mult))
    W0, W1 = GW + 6, GW + 8
    dve.wait(r)
    rr = dve.go(lambda e: e.tensor_copy(rt(RK, [1, 64]), bank(5, 0, [1, 64])))
    rc = dve.go(lambda e: e.tensor_copy(rt(CNT, [1, 32]), bank(5, 64, [1, 32])))
    free[5] = rc
    dve.wait(rr)
    for a, o in ((0, O0), (1, O1)):
        r = dve.go(lambda e, o=o: e.tensor_tensor(rt(RKM, [1, 64]), rt(RK, [1, 64]), rt(o, [1, 64]), ALU.mult))
        dve.wait(r)
        r = dve.go(lambda e, a=a: e.tensor_reduce(rt(RA + a, [2, 2]), rt(RKM, [32, 2], [1, 32]), AX, ALU.add))
        dve.wait(r)
    r = dve.go(lambda e: e.tensor_scalar(rt(OV, [1, 4]), rt(RA, [1, 4]), float(KEEP), None, ALU.is_ge))
    dve.go(lambda e: e.tensor_scalar(rt(OVM, [1, 4]), rt(RA, [1, 4]), float(KEEP), None, ALU.is_lt))
    dve.go(lambda e: e.scalar_tensor_tensor(rt(DST, [1, 4]), rt(EF, [1, 4]), float(CAP), rt(RA, [1, 4]), ALU.mult, ALU.add))
    r = dve.go(lambda e: e.scalar_tensor_tensor(rt(OD, [1, 4]), rt(EF, [1, 4]), float(OVR), rt(RA, [1, 4]), ALU.mult, ALU.add))
    dve.wait(r)
    dve.go(lambda e: e.tensor_tensor(rt(ROW, [1, 4]), rt(DST, [1, 4]), rt(OVM, [1, 4]), ALU.mult))
    r = dve.go(lambda e: e.scalar_tensor_tensor(rt(OD, [1, 4]), rt(OD, [1, 4]), float(-KEEP), rt(OV, [1, 4]), ALU.add, ALU.mult))
    dve.wait(r)
    dve.go(lambda e: e.tensor_copy(view(UI, 32, [[1, 4]]), rt(ROW, [1, 4])))
    r = dve.go(lambda e: e.tensor_copy(view(UI, 36, [[1, 4]]), rt(OD, [1, 4])))
    dve.wait(r)
    dve.go(lambda e: e.scalar_tensor_tensor(rt(OD, [1, 4]), rt(OVM, [1, 4]), -FAR, rt(OD, [1, 4]), ALU.mult, ALU.add))
    r = dve.go(lambda e: e.tensor_reduce(rt(MAXC, [1, 1]), rt(CNT, [1, 32]), AX, ALU.max))
    dve.wait(r)
    r = dve.go(lambda e: e.tensor_scalar(rt(MAXC, [1, 1]), rt(MAXC, [1, 1]), float(KEEP), None, ALU.is_gt))
    dve.wait(r)
    trow = dve.go(lambda e: e.tensor_copy(view(flag, 0, [[1, 1]]), rt(MAXC, [1, 1])))
    tdst = dve.go(lambda e: e.scalar_tensor_tensor(rt(DST, [1, 4]), rt(OV, [1, 4]), FAR, rt(DST, [1, 4]), ALU.mult, ALU.add))
    dve.wait(tdst)

    dve.wait(tx1h)
    tx1l = dve.go(lambda e: e.tensor_tensor(X1L[:, :], X1[:, :], X1H[:, :].bitcast(F32), ALU.subtract))

    XS = [sb(f"XS{i}", 4096, A0 + 41 * KB + 16 * KB * i, F32R) for i in range(2)]
    SS = [sb(f"SS{i}", 512, A0 + 73 * KB + 2 * KB * i, F32R) for i in range(2)]
    SF = sb("SF", 512, A0 + 29 * KB)
    DG = sb("DG", 8, A0 + 31 * KB)
    T1 = sb("T1", 1024, A0 + 77 * KB, rows=64)
    G1 = sb("G1", 1024, A0 + 81 * KB, rows=64)
    HM = sb("HM", 512, A0 + 85 * KB, rows=64)
    T2 = sb("T2", 1024, A0 + 87 * KB, rows=64)
    YY = [sb(f"YY{i}", 1024, A0 + 91 * KB + 4 * KB * i, rows=64) for i in range(2)]
    HT = [sb(f"HT{i}", 512, A0 + 32 * KB + 2 * KB * i, F32R) for i in range(2)]
    GB, DB, TB, SB_ = 0, 2, 4, (5, 6)
    xs_tok, xs_free, ss_free = {}, [None, None], [None, None]
    ex = {}

    def select(g):
        x = SS[g % 2]
        pool.wait(tdst, tcm, ss_free[g % 2], ex.get("dg"))
        r = pool.go(lambda e: e.tensor_scalar(view(DG, 0, [[1, 4]]), rt(DST, [1, 4]), float(-256 * g), None, ALU.add))
        pool.wait(r, ex.get("sf"))
        for i in range(2):
            rs = pool.go(lambda e, i=i: e.tensor_scalar(view(SF, 256 * i, [[1, 256]]), con("iota"), view(DG, 2 * i, [[1, 1]]), None, ALU.is_equal))
            r2 = pool.go(lambda e, i=i: e.tensor_scalar(view(x, 256 * i, [[1, 256]]), con("iota"), view(DG, 2 * i + 1, [[1, 1]]), None, ALU.is_equal))
        pool.wait(r2)
        ex["dg"] = r2
        r = pool.go(lambda e: e.tensor_tensor(x[:, :], x[:, :].bitcast(F32), SF[:, :], ALU.add))
        ex["sf"] = r
        ex["sel", g] = r

    def gather(g, ks):
        for k in ks:
            b = SB_[k % 2]
            pe.wait(ex["sel", g], tx1h, tx1l, free[b])
            for half, x in ((0, X1H), (1, X1L)):
                for i in range(2):
                    r = mm(bank(b, 256 * half, [1, 256]), view(x, 1024 * i + 128 * k, [[1, 128]]), view(SS[g % 2], 256 * i, [[1, 256]]),
                           i == 0, i == 1, last=(half == 1 and i == 1))
            act.wait(r, xs_free[g % 2])
            free[b] = act.go(lambda e, b=b, k=k: e.copy(view(XS[g % 2], 512 * k, [[64, 2], [128, 4], [1, 64]]), bank(b, 0, [256, 2], [64, 4], [1, 64])))
            xs_tok[g, k] = free[b]
            if k == 7:
                ss_free[g % 2] = r
                ex["last_gather"] = r

    def up(e):
        g = e // 4
        for j in range(4):
            u = take("gu", (e, j))
            if j == 0:
                pe.wait(free[GB], free[GB + 1])
            for kk in range(2):
                k = 2 * j + kk
                pe.wait(xs_tok[g, k])
                x = view(XS[g % 2], 512 * k + 128 * (e % 4), [[1, 128]])
                for c in range(2):
                    o = bank(GB + c, 0, [1, 512])
                    mm(o, x, u.h(kk, 512 * c, 512), k == 0, False)
                    tok = mm(o, x, u.l(kk, 512 * c, 512), False, k == 7, last=(kk == 1 and c == 1))
            release(u, tok)
        if e % 4 == 3:
            xs_free[g % 2] = tok
        act.wait(tok, ex.get("g1"))
        ra = act.go(lambda q: q.copy(T1[:, :], bank(GB, 0, [1, 1024], p0=64, rows=64)))
        dve.wait(ra, ex.get("hm"))
        r = dve.go(lambda q: q.tensor_tensor(G1[:, :], bank(GB, 0, [1, 1024], rows=64), T1[:, :], ALU.add))
        free[GB] = free[GB + 1] = ex["g1"] = r
        act.wait(r)
        r = act.go(lambda q: q.activation(view(T1, 0, [[1, 512]], rows=64), view(G1, 0, [[1, 512]], rows=64), ACT.Silu))
        dve.wait(r, ex.get("tr"))
        ex["hm"] = ex["g1"] = dve.go(lambda q: q.tensor_tensor(HM[:, :], view(T1, 0, [[1, 512]], rows=64), view(G1, 512, [[1, 512]], rows=64), ALU.mult))

    def turn(e):
        pe.wait(ex["hm"], free[TB])
        for k in range(4):
            f = lambda q, k=k: q.transpose(bank(TB, 64 * k, [1, 64]), view(HM, 128 * k, [[1, 128]], rows=64), con("ident", w=64, rows=64))
            r = pe.go(f) if k == 3 else pe.quiet(f)
        ex["tr"] = r
        x = HT[e % 2]
        act.wait(r, ex.get(("down", e - 2)))
        ra = act.go(lambda q: q.copy(view(x, 0, [[128, 4], [1, 64]]), bank(TB, 0, [64, 4], [1, 64])))
        dve.wait(ra, ex.get(("down", e - 2)))
        rb = dve.go(lambda q: q.tensor_tensor(view(x, 64, [[128, 4], [1, 64]]), bank(TB, 0, [64, 4], [1, 64]), view(x, 0, [[128, 4], [1, 64]]).bitcast(F32), ALU.subtract))
        free[TB] = rb
        ex["ht", e] = (ra, rb)

    s_y = [sem("s_y0"), sem("s_y1")]
    y_tok = {}

    def down(e):
        x = HT[e % 2]
        for j in range(2):
            u = take("dn", (e, j))
            if j == 0:
                pe.wait(free[DB], free[DB + 1], *ex["ht", e])
            for kk in range(2):
                k = 2 * j + kk
                for c in range(2):
                    o = bank(DB + c, 0, [1, 512])
                    s = view(x, 128 * k, [[1, 128]])
                    mm(o, s, u.h(kk, 512 * c, 512), k == 0, False)
                    tok = mm(o, s, u.l(kk, 512 * c, 512), False, k == 3, last=(kk == 1 and c == 1))
            release(u, tok)
        ex["down", e] = tok
        act.wait(tok, ex.get("t2"))
        ra = act.go(lambda q: q.copy(T2[:, :], bank(DB, 0, [1, 1024], p0=64, rows=64)))
        dve.wait(ra, y_tok.get(e - 2))
        y = YY[e % 2]
        r = dve.go(lambda q: q.tensor_tensor(y[:, :], bank(DB, 0, [1, 1024], rows=64), T2[:, :], ALU.add))
        free[DB] = free[DB + 1] = ex["t2"] = r
        pool.wait(r)
        y_tok[e] = dma(pool, d_y[CAP * e:CAP * (e + 1), :], y[:, :], s_y[e % 2])

    act.wait(*[free[4], rd])
    select(0)
    gather(0, range(8))
    for e in range(NE):
        g = e // 4
        if e % 4 == 0 and g + 1 < 8:
            select(g + 1)
        up(e)
        if e:
            down(e - 1)
        if g + 1 < 8:
            gather(g + 1, (2 * (e % 4), 2 * (e % 4) + 1))
        turn(e)
    down(NE - 1)

    RR = [sb(f"RR{i}", 1024, A0 + 4 * KB * i) for i in range(4)]
    LG2 = sb("LG2", 1024, A0 + 77 * KB)
    LB2 = sb("LB2", 1024, A0 + 81 * KB)
    s_g = [sem(f"s_g{i}") for i in range(4)]
    pool.wait(trow, y_tok[NE - 2], y_tok[NE - 1], ex["last_gather"], ex["t2"])
    rr_tok = []
    for n in range(4):
        pool.quiet(lambda e: e.indirect_dma_start(RR[n][:, :], None, d_y, bass.IndirectOffsetOnAxis(ap=view(UI, 32 + n, [[1, 1]]), axis=0)).then_inc(s_g[n], 16))
        rr_tok.append((s_g[n], 16))
    bcast_row(pool, LG2, t["ln2_g"], s_ln2)
    tln2 = bcast_row(pool, LB2, t["ln2_b"], s_ln2)

    s_ov = [sem(f"s_ov_{n}") for n in ("pe", "act", "dve", "pool", "sp")]
    s_ow, s_oy, s_og = sem("s_ow"), sem("s_oy"), [sem(f"s_og{i}") for i in range(4)]
    before = [(q.sem, q.n) for q in (pe, act, dve, pool)] + rr_tok + [tln2]
    engines = (nc.tensor, nc.scalar, nc.vector, nc.gpsimd, nc.sync)
    for q in (pe, act, dve, pool, sp):
        q.wait(trow)
    over = nc.values_load(view(flag, 0, [[1, 1]], rows=1).bitcast(I32), min_val=0, max_val=1)
    with nc.If(over > 0):
        ope, oact, odve, opool, osp = (Queue(q, x) for q, x in zip(engines, s_ov))
        for q in (ope, oact, odve, opool, osp):
            q.wait(*before)
        GUW = sb("GUW", 8192, A0 + 41 * KB)
        DNW = sb("DNW", 4096, A0 + 85 * KB)
        XG = sb("XG", 1536, A0 + 32 * KB)
        OS_ = sb("OS_", 384, A0 + 73 * KB)
        OT_ = sb("OT_", 512, A0 + 75 * KB)
        OG = sb("OG", 512, A0 + 38 * KB)
        OY = sb("OY", 512, A0 + 29 * KB)
        OX = sb("OX", 192, A0 + 31 * KB)
        nc.all_engine_barrier()
        with nc.Fori(0, NE) as ei:
            ope, oact, odve, opool, osp = (Queue(q, x) for q, x in zip(engines, s_ov))
            nd = [0]

            def odma(q, dst, src, s_, n):
                q.eng.dma_start(dst, src).then_inc(s_, 16)
                return s_, n

            odma(osp, view(GUW, 0, [[1024, 8], [1, 1024]]), t["w_gate_up"][bass.ds(ei, 1)].rearrange("o (c p) n -> p (o c) n", p=128), s_ow, 16)
            w_tok = odma(osp, view(DNW, 0, [[1024, 4], [1, 1024]]), t["w_down"][bass.ds(ei, 1)].rearrange("o (c p) n -> p (o c) n", p=128), s_ow, 32)
            for i in range(2):
                sl = view(OS_, OVR * i, [[1, OVR]])
                r = odve.go(lambda e: e.tensor_scalar(sl, con("iota", w=OVR), rt(OD + 2 * i, [1, 1]), None, ALU.is_equal))
                r = odve.go(lambda e: e.tensor_scalar(view(OX, 0, [[1, OVR]]), con("iota", w=OVR), rt(OD + 2 * i + 1, [1, 1]), None, ALU.is_equal))
                odve.wait(r)
                ts = odve.go(lambda e: e.tensor_tensor(sl, sl, view(OX, 0, [[1, OVR]]), ALU.add))
                odve.wait(ts)
            odve.go(lambda e: e.tensor_scalar(rt(OD, [1, 4]), rt(OD, [1, 4]), float(-OVR), None, ALU.add))

            def omm(o, a, b, start, stop):
                return ope.go(lambda e: e.matmul(o, a, b, start=start, stop=stop))

            ope.wait(ts)
            rg = None
            for k in range(8):
                ope.wait(rg)
                for i in range(2):
                    r = omm(bank(0, 0, [1, OVR]), view(X1, 1024 * i + 128 * k, [[1, 128]]), view(OS_, OVR * i, [[1, OVR]]), i == 0, i == 1)
                oact.wait(r)
                rg = oact.go(lambda e: e.copy(view(XG, OVR * k, [[1, OVR]]), bank(0, 0, [1, OVR])))
            ope.wait(rg, w_tok)
            ry = None
            for s0, w in ((0, 128), (128, 64)):
                for c in range(2):
                    for k in range(8):
                        r = omm(bank(1 + c, 0, [1, 512], rows=w), view(XG, OVR * k + s0, [[1, w]]), view(GUW, 1024 * k + 512 * c, [[1, 512]]), k == 0, k == 7)
                oact.wait(r)
                r = oact.go(lambda e: e.activation(view(OG, 0, [[1, 512]], rows=w), bank(1, 0, [1, 512], rows=w), ACT.Silu))
                odve.wait(r)
                r = odve.go(lambda e: e.tensor_tensor(view(OG, 0, [[1, 512]], rows=w), view(OG, 0, [[1, 512]], rows=w), bank(2, 0, [1, 512], rows=w), ALU.mult))
                ope.wait(r)
                for k in range(4):
                    r = ope.go(lambda e: e.transpose(bank(3, w * k, [1, w]), view(OG, 128 * k, [[1, 128]], rows=w), con("ident", w=w, rows=w)))
                odve.wait(r)
                r = odve.go(lambda e: e.tensor_copy(view(OT_, 0, [[1, 4 * w]]), bank(3, 0, [1, 4 * w])))
                ope.wait(r)
                for c in range(2):
                    for k in range(4):
                        r = omm(bank(4, 0, [1, 512], rows=w), view(OT_, w * k, [[1, w]]), view(DNW, 1024 * k + 512 * c, [[1, 512]]), k == 0, k == 3)
                    odve.wait(r, ry)
                    r = odve.go(lambda e: e.tensor_copy(view(OY, 0, [[1, 512]], rows=w), bank(4, 0, [1, 512], rows=w)))
                    ope.wait(r)
                    osp.wait(r)
                    nd[0] += 16
                    ry = odma(osp, d_o[bass.ds(ei * OVR + s0, w), 512 * c:512 * c + 512], view(OY, 0, [[1, 512]], rows=w), s_oy, nd[0])
            osp.wait(ry)
            nc.all_engine_barrier(sems_to_clear=range(s_ov[0].num, s_ov[4].num + 1))
            for q, x in ((osp, s_ow), (osp, s_oy)):
                q.eng.sem_clear(x)
            nc.all_engine_barrier()
        odve = Queue(nc.vector, s_ov[2])
        for n in range(4):
            ro = sb(f"RO{n}", 1024, A0 + 41 * KB + 4 * KB * n)
            nc.gpsimd.indirect_dma_start(ro[:, :], None, d_o, bass.IndirectOffsetOnAxis(ap=view(UI, 36 + n, [[1, 1]]), axis=0)).then_inc(s_og[n], 16)
            nc.vector.wait_ge(s_og[n], 16)
            r = odve.go(lambda e: e.copy_predicated(RR[n][:, :], rt(OV + n, [0, 1024]).bitcast(U32), ro[:, :]))
        odve.wait(r)
        nc.all_engine_barrier()
    x2_tok = []
    for i in range(2):
        o = view(X1, 1024 * i, [[1, 1024]])
        dve.wait(rr_tok[2 * i], tw)
        r = dve.go(lambda e, i=i: e.tensor_scalar(RR[2 * i][:, :], RR[2 * i][:, :], rt(W0 + i, [1, 1]), None, ALU.mult))
        dve.wait(r, rr_tok[2 * i + 1])
        r = dve.go(lambda e, i=i: e.scalar_tensor_tensor(RR[2 * i][:, :], RR[2 * i + 1][:, :], rt(W1 + i, [1, 1]), RR[2 * i][:, :], ALU.mult, ALU.add))
        dve.wait(r)
        r = dve.go(lambda e, i=i, o=o: e.scalar_tensor_tensor(o, o, ALPHA, RR[2 * i][:, :], ALU.mult, ALU.add))
        x2_tok.append(layer_norm(i, X1, LG2, LB2, r, tln2))

    HH = sb("HH", 8 * L, A0 + 34 * KB + 2048)
    HW = 8 * L * 4
    assert HW == 8704
    AH = sb("AH", 8 * L + 128, A0, F32R)
    AL = sb("AL", 8 * L + 128, A0 + HW + 512, F32R)
    o2 = A0 + 2 * (HW + 512)
    HH = sb("HH2", 8 * L, o2 + 6 * KB)
    assert o2 + 6 * KB >= A0 + 24 * KB
    o2 += 6 * KB + HW
    RS = sb("RS", L, o2)
    o2 += 4 * L
    AF = sb("AF", 8 * L, o2)
    o2 += HW
    FH = sb("FH", 22 * L, o2, F32R)
    FL = sb("FL", 22 * L, o2 + 88 * L, F32R)
    F2 = [sb(f"F2{i}", 2 * L, o2 + 2 * 88 * L + 8 * L * i) for i in range(2)]
    assert o2 + 2 * 88 * L + 16 * L <= 207 * KB, (o2 + 2 * 88 * L + 16 * L) / KB

    s_m = sem("s_m")
    pool.wait(*x2_tok)
    tmeta = dma(pool, view(HH, 0, [[L, 8], [1, NMETA]]), t["metaT"].rearrange("p (c n) -> p c n", c=8), s_m)
    hh_tok = [tmeta]
    for i in range(2):
        pe.wait(x2_tok[i])
        pe.wait(free[2 * i], free[2 * i + 1])
        for k in range(8):
            f = lambda e, i=i, k=k: e.transpose(bank(2 * i, 128 * k, [1, 128]), view(X1, 1024 * i + 128 * k, [[1, 128]]), con("ident"))
            r = pe.go(f) if k == 7 else pe.quiet(f)
        act.wait(r, x2_tok[1])
        free[2 * i] = free[2 * i + 1] = act.go(lambda e, i=i: e.copy(view(HH, NMETA + 128 * i, [[L, 8], [1, 128]]), bank(2 * i, 0, [128, 8], [1, 128])))
        hh_tok.append(free[2 * i])

    dve.wait(r)
    dve.go(lambda e: e.memset(view(AH, 8 * L, [[1, 128]]).bitcast(F32), 0.0))
    ttail = dve.go(lambda e: e.memset(view(AL, 8 * L, [[1, 128]]).bitcast(F32), 0.0))
    hc = lambda x, k, n=1: view(x, L * k, [[1, n * L]])
    nrm = {}

    def rms(gname, gi, ready, afree):
        act.wait(*ready)
        act.wait(*afree)
        for half in range(2):
            r = act.go(lambda e, half=half: e.activation(hc(AF, 4 * half, 4), hc(HH, 4 * half, 4), ACT.Square))
            pe.wait(r, free[7])
            for k in range(4 * half, 4 * half + 4):
                tk = mm(bank(7, 0, [1, L]), con("ones"), hc(AF, k), k == 0, k == 7, last=(k == 7))
        dve.wait(tk)
        r = dve.go(lambda e: e.tensor_scalar(RS[:, :], bank(7, 0, [1, L]), 1.0 / D, 1e-6, ALU.mult, ALU.add))
        free[7] = r
        dve.wait(r)
        r = dve.go(lambda e: e.reciprocal(RS[:, :], RS[:, :]))
        act.wait(r)
        r = act.go(lambda e: e.activation(RS[:, :], RS[:, :], ACT.Sqrt))
        dve.wait(r)
        toks = []
        for k in range(8):
            toks.append(dve.go(lambda e, k=k: e.scalar_tensor_tensor(hc(AF, k), hc(HH, k), par(gname, gi + k), RS[:, :], ALU.mult, ALU.mult)))
        return toks

    def halves(toks, wfree):
        out = []
        act.wait(*wfree)
        dve.wait(*wfree)
        for c in range(0, 8, 4):
            act.wait(toks[c + 3])
            rh = act.go(lambda e, c=c: e.copy(hc(AH, c, 4), hc(AF, c, 4)))
            dve.wait(rh)
            rl = dve.go(lambda e, c=c: e.tensor_tensor(hc(AL, c, 4), hc(AF, c, 4), hc(AH, c, 4).bitcast(F32), ALU.subtract))
            out += [(rh, rl)] * 4
        return out

    A1T = rms("nm", 0, hh_tok, ())
    PW = sb("PW", 8 * L, A0 + 2 * (HW + 512) + 6 * KB + 2 * HW + 4 * L)
    PB = sb("PB", 8 * L, A0 + 2 * (HW + 512) + 6 * KB + 3 * HW + 4 * L)
    h_tok = list(A1T)
    pooled = {}
    for g in range(4):
        win = 2 << g
        c = lambda x, o, w: view(x, 2 * L * g + o, [[L, 2], [1, w]])
        src, dst = AF, PW
        r = A1T[2 * g + 1]
        s = 1
        while s < win:
            dve.wait(r)
            dve.go(lambda e, a=c(dst, 0, s), b=c(src, 0, s): e.tensor_copy(a, b))
            r = dve.go(lambda e, a=c(dst, s, L - s), b=c(src, s, L - s), d=c(src, 0, L - s): e.tensor_tensor(a, b, d, ALU.add))
            src, dst = dst, (PB if dst is PW else PW)
            s *= 2
        dve.wait(r)
        r = dve.go(lambda e, s_=src, c=c, win=win: e.tensor_tensor(c(s_, 0, win), c(s_, 0, win), view(cm, CM["inv"][0], [[0, 2], [1, win]]), ALU.mult))
        r = dve.go(lambda e, s_=src, c=c, win=win: e.tensor_scalar(c(s_, win, L - win), c(s_, win, L - win), 1.0 / win, None, ALU.mult))
        dve.wait(r)
        r = dve.go(lambda e, s_=src, c=c: e.tensor_tensor(c(s_, 0, L), c(s_, 0, L), c(AF, 0, L), ALU.subtract))
        act.wait(r)
        rh = act.go(lambda e, s_=src, c=c: e.copy(c(AH, 0, L), c(s_, 0, L)))
        dve.wait(rh)
        rl = dve.go(lambda e, s_=src, c=c: e.tensor_tensor(c(AL, 0, L), c(s_, 0, L), c(AH, 0, L).bitcast(F32), ALU.subtract))
        pooled[g] = (rh, rl)
    hn = []
    ah, al = (lambda k: hc(AH, k)), (lambda k: hc(AL, k))
    for g in range(4):
        u = take("pw", g)
        pe.wait(*pooled[g])
        for m in range(2):
            b = (2 * g + m) % 4
            pe.wait(free[b])
            tok = stationary_w(u, bank(b, 0, [1, L]), m, range(2), lambda k: hc(AH, 2 * g + k), lambda k: hc(AL, 2 * g + k))
            k = 2 * g + m
            dve.wait(tok)
            r = dve.go(lambda e, k=k, b=b: e.scalar_tensor_tensor(hc(HH, k), bank(b, 0, [1, L]), par("ps", k), hc(HH, k), ALU.mult, ALU.add))
            free[b] = r
        release(u, tok)
        hn.append(r)

    def ffn(i, ready, wfree):
        toks = rms("nf", 8 * i, ready, wfree)
        hl = halves(toks, wfree)
        fh = {}
        for f in range(11):
            bb = 4 * (f % 2)
            for which, nm in enumerate(("fg", "fu")):
                u = take(nm, (i, f))
                for m in range(2):
                    b = (bb + 2 * which + m) % 8
                    pe.wait(free[b])
                    if f == 0:
                        for p in hl:
                            pe.wait(*p)
                    tok = stationary_w(u, bank(b, 0, [1, L]), m, range(8), ah, al)
                release(u, tok)
                if which == 0:
                    gtok = tok
            x = F2[f % 2]
            pair = lambda b: bank(b, 0, [512, 2], [1, L])
            act.wait(gtok, fh.get(f - 2))
            r = act.go(lambda e, x=x, bb=bb: e.activation(view(x, 0, [[L, 2], [1, L]]), pair(bb), ACT.Silu))
            free[bb] = free[bb + 1] = r
            dve.wait(r, tok)
            r = dve.go(lambda e, x=x, bb=bb: e.tensor_tensor(view(x, 0, [[L, 2], [1, L]]), view(x, 0, [[L, 2], [1, L]]), pair(bb + 2), ALU.mult))
            free[bb + 2] = free[bb + 3] = r
            act.wait(r)
            rh = act.go(lambda e, x=x, f=f: e.copy(hc(FH, 2 * f, 2), x[:, :]))
            dve.wait(rh)
            rl = dve.go(lambda e, x=x, f=f: e.tensor_tensor(hc(FL, 2 * f, 2), x[:, :], hc(FH, 2 * f, 2).bitcast(F32), ALU.subtract))
            fh[f] = rl
        done = []
        for c in range(4):
            b0 = 2 * (c % 2)
            for k3 in range(3):
                u = take("fd", (i, c, k3))
                n = 8 if k3 < 2 else 6
                pe.wait(rl)
                for m in range(2):
                    if k3 == 0:
                        pe.wait(free[b0 + m])
                    tok = stationary_w(u, bank(b0 + m, 0, [1, L]), m, range(8 * k3, 8 * k3 + n), lambda k: hc(FH, k), lambda k: hc(FL, k),
                                       start=(k3 == 0), stop=(k3 == 2))
                    if k3 == 2:
                        k = 2 * c + m
                        dve.wait(tok)
                        r = dve.go(lambda e, k=k, b=b0 + m: e.tensor_tensor(hc(HH, k), bank(b, 0, [1, L]), hc(HH, k), ALU.add))
                        free[b0 + m] = r
                release(u, tok)
            done.append(r)
        return done, tok

    h1, pe_f = ffn(0, hn, (hn[3],))

    toks = rms("nm", 8, h1, (pe_f,))
    hl = halves(toks, (pe_f,))
    o3 = A0 + 2 * (HW + 512) + 6 * KB + 2 * HW + 4 * L
    Q2 = sb("Q2", 8 * L, o3)
    K2 = sb("K2", 8 * L, o3 + HW)
    V2 = sb("V2", 3072, o3 + 2 * HW)
    o3 += 2 * HW + 12 * KB
    WA = 432
    BA, BE, BS = ([sb(f"{n}{i}", WA, o3 + 4 * WA * (3 * i + j)) for i in range(2)] for j, n in enumerate(("BA", "BE", "BS")))
    o3 += 24 * WA
    assert o3 <= 207 * KB, o3 / KB
    OH2, OL2 = AH, AL
    qk = {}
    for j in range(12):
        u = take("qkv", j)
        for p in hl:
            pe.wait(*p)
        if j < 8:
            x, jj = (Q2, j) if j < 4 else (K2, j - 4)
            b0 = 2 * (j % 2)
            for m in range(2):
                pe.wait(free[b0 + m])
                tok = stationary_w(u, bank(b0 + m, 0, [1, L]), m, range(8), ah, al)
            act.wait(tok, pe_f)
            r = act.go(lambda e, x=x, jj=jj, b0=b0, j=j: e.activation(view(x, 2 * L * jj, [[L, 2], [1, L]]), bank(b0, 0, [512, 2], [1, L]), ACT.Copy,
                                                                      scale=0.125 if j < 4 else 1.0))
            free[b0] = free[b0 + 1] = r
            qk[j] = r
        else:
            jj = j - 8
            for i in range(3):
                b = 4 + (3 * jj + i) % 3
                pe.wait(free[b], ttail)
                tok = moving_w(u, bank(b, 0, [1, 256]), 0, 256, range(8), lambda k: view(AH, L * k + 128 * i, [[1, 128]]),
                               lambda k: view(AL, L * k + 128 * i, [[1, 128]]))
                dve.wait(tok, pe_f)
                n = 128 if i < 2 else 16
                r = dve.go(lambda e, i=i, jj=jj, b=b, n=n: e.tensor_copy(view(V2, 1024 * i + 256 * jj, [[1, 256]], rows=n), bank(b, 0, [1, 256], rows=n)))
                free[b] = r
            qk[j] = r
        release(u, tok)
    qkv_done = tok
    TL = ((128, 0, 272, 0), (128, 128, 144, 272), (16, 256, 16, 416))
    att = {}
    o_tok = {}

    def att_scores(h):
        c, p0 = h // 2, 64 * (h % 2)
        b = 2 * (h % 2)
        w = h % 2
        pe.wait(qk[c // 2], qk[4 + c // 2], free[b], free[b + 1])
        for i, (n, q0, wd, _) in enumerate(TL):
            bb, col = (b, 0) if i == 0 else (b + 1, 0 if i == 1 else 256)
            r = mm(bank(bb, col, [1, wd], rows=n), view(K2, L * c + 128 * i, [[1, n]], p0, 64), view(Q2, L * c + q0, [[1, wd]], p0, 64),
                   i < 2, True, last=(i == 2), skip_group_check=True)
        A, E, P = BA[w], BE[w], BS[w]
        act.wait(r, att.get(("pv", h - 2)), att.get(("r", h - 2)))
        z = [(bank(b if i == 0 else b + 1, 256 if i == 2 else 0, [1, wd], rows=n), col, wd, n) for i, (n, q0, wd, col) in enumerate(TL)]
        for zz, col, wd, n in z:
            r = act.go(lambda e, zz=zz, col=col, wd=wd, n=n: e.activation(view(A, col, [[1, wd]], rows=n), zz, ACT.Abs))
        act.wait(r)
        for zz, col, wd, n in (z[0], z[2]):
            wd = WA - 16 if col == 0 else 16
            r = act.go(lambda e, col=col, wd=wd, n=n: e.activation(view(E, col, [[1, wd]], rows=n), view(A, col, [[1, wd]], rows=n), ACT.Exp, scale=-1.0))
        act.wait(r)
        for zz, col, wd, n in (z[0], z[2]):
            wd = WA - 16 if col == 0 else 16
            r = act.go(lambda e, col=col, wd=wd, n=n: e.activation(view(E, col, [[1, wd]], rows=n), view(E, col, [[1, wd]], rows=n), ACT.Ln, bias=1.0))
        dve.wait(r, att.get(("r", h - 2)))
        for zz, col, wd, n in z:
            r = dve.go(lambda e, zz=zz, col=col, wd=wd, n=n: e.scalar_tensor_tensor(view(P, col, [[1, wd]], rows=n), zz, 0.0,
                                                                                   view(E, col, [[1, wd]], rows=n), ALU.max, ALU.add))
        att["sp", h] = mask(P, r)

    def mask(x, tok):
        pool.wait(tok)
        for n, _, _, col in TL:
            a = view(x, col, [[1, n]], rows=n)
            r = pool.go(lambda e, a=a, n=n: e.affine_select(out=a, in_=a, compare_op=ALU.is_gt, fill=0.0, base=0, pattern=[[1, n]], channel_multiplier=-1))
        return r

    def att_decay(h):
        b, w = 2 * (h % 2), h % 2
        P = BS[w]
        pe.wait(att["sp", h])
        kw = dict(skip_group_check=True)
        x = lambda i, off, wd: view(P, TL[i][3] + off, [[1, wd]], rows=TL[i][0])
        mm(bank(b, 0, [1, 272]), con("trineg"), x(0, 0, 272), False, True, **kw)
        mm(bank(b, 128, [1, 144]), con("negones"), x(1, 0, 144), False, True, **kw)
        mm(bank(b, 256, [1, 16]), con("negones", rows=16), x(2, 0, 16), False, True, **kw)
        mm(bank(b + 1, 0, [1, 144]), con("trineg"), x(1, 0, 144), False, True, **kw)
        mm(bank(b + 1, 128, [1, 16]), con("negones", rows=16), x(2, 0, 16), False, True, **kw)
        r = mm(bank(b + 1, 256, [1, 16], rows=16), con("trineg", w=16, rows=16), x(2, 0, 16), False, True, last=True, **kw)
        att["r", h] = r
        A = BA[w]
        act.wait(r)
        for i, (n, q0, wd, col) in enumerate(TL):
            zz = bank(b if i == 0 else b + 1, 256 if i == 2 else 0, [1, wd], rows=n)
            r = act.go(lambda e, zz=zz, col=col, wd=wd, n=n: e.activation(view(A, col, [[1, wd]], rows=n), zz, ACT.Exp))
        free[b] = free[b + 1] = r
        att["a", h] = mask(A, r)

    def att_out(h):
        w, c = h % 2, h // 2
        bo = 4 + c % 2
        A = BA[w]
        pe.wait(att["a", h], qk[8 + h // 4])
        if w == 0:
            pe.wait(free[bo])
        for i, (n, q0, wd, col) in enumerate(TL):
            r = mm(bank(bo, q0, [1, wd], p0=64 * w, rows=64), view(V2, 1024 * i + 64 * h, [[1, 64]], rows=n), view(A, col, [[1, wd]], rows=n),
                   i == 0, i == 2, last=(i == 2))
        att["pv", h] = r
        if w == 1:
            act.wait(r, qkv_done)
            rh = act.go(lambda e: e.copy(hc(OH2, c), bank(bo, 0, [1, L])))
            dve.wait(rh, qkv_done)
            free[bo] = dve.go(lambda e: e.tensor_tensor(hc(OL2, c), bank(bo, 0, [1, L]), hc(OH2, c).bitcast(F32), ALU.subtract))
            o_tok[c] = (rh, free[bo])

    for h in range(17):
        if h >= 2:
            att_out(h - 2)
        if h < 16:
            att_scores(h)
        if h >= 1:
            att_decay(h - 1)
    att_out(15)
    hn = []
    for j in range(4):
        u = take("wo", j)
        for m in range(2):
            b = 2 * (j % 2) + m
            pe.wait(free[b], *[x for c in range(8) for x in o_tok[c]])
            tok = stationary_w(u, bank(b, 0, [1, L]), m, range(8), lambda k: hc(OH2, k), lambda k: hc(OL2, k))
            k = 2 * j + m
            dve.wait(tok)
            r = dve.go(lambda e, k=k, b=b: e.tensor_tensor(hc(HH, k), bank(b, 0, [1, L]), hc(HH, k), ALU.add))
            free[b] = r
        release(u, tok)
        hn.append(r)
    wo_done = tok
    h2, pe_f = ffn(1, hn, (wo_done,))

    toks = rms("fn", 0, h2, (pe_f,))
    OUTB = sb("OUTB", 2048, A0)
    s_o = [sem("s_o0"), sem("s_o1")]
    fin = []
    for i in range(2):
        b = 2 * i
        pe.wait(free[b], free[b + 1], *toks)
        for k in range(8):
            f = lambda e, k=k, i=i, b=b: e.transpose(bank(b, 128 * k, [1, 128]), view(AF, L * k + NMETA + 128 * i, [[1, 128]]), con("ident"))
            r = pe.go(f) if k == 7 else pe.quiet(f)
        q, f = (act, lambda e, b=b, i=i: e.copy(view(OUTB, 1024 * i, [[1, 1024]]), bank(b, 0, [1, 1024]))) if i else \
               (dve, lambda e, b=b, i=i: e.tensor_copy(view(OUTB, 1024 * i, [[1, 1024]]), bank(b, 0, [1, 1024])))
        q.wait(r, pe_f)
        r = q.go(f)
        sp.wait(r)
        fin.append(dma(sp, out[0, 128 * i:128 * (i + 1), :], view(OUTB, 1024 * i, [[1, 1024]]), s_o[i]))
    sp.wait(*fin)
    sp.wait(ttab, y_tok[NE - 1], y_tok[NE - 2])
    assert state["next"] == NU


def layout(inputs):
    g = {k: np.ascontiguousarray(np.asarray(v)) for k, v in inputs.items()}
    cmat, hot, scan = shape_constants()
    col = lambda v: np.asarray(v).reshape(-1, 128).T
    x = g["x"]
    a = {
        "x": x,
        "xT": x[0].T.reshape(8, 128, S).transpose(1, 0, 2).reshape(128, 2048),
        "cm": cmat, "hot": hot, "scan": scan,
        "pc": np.concatenate([col(g["b_in"][0]), col(g["lb_logits"]), col(g["hg_norm_g"][0]), col(g["norm_mix_2"]),
                              col(g["norm_ffn_2"]), col(g["pool_scale_2"][0]), col(g["final_norm_2"])], 1),
        "rows": np.concatenate([g["b_in"][0, 1024:1536], g["b_in"][0, 3072:3584], g["b_group"][0], g["b_expert"][0]])[None, :],
        "rb": np.concatenate([g["rel_bias"], np.ones((1, 8), np.float32)], 0),
        "wr": np.concatenate([g["w_group"][0], g["w_expert"][0]], 1).reshape(8, 128, 36).transpose(1, 0, 2).reshape(128, 288),
        "metaT": g["meta_2"].T.reshape(8, 128, NMETA).transpose(1, 0, 2).reshape(128, 8 * NMETA),
        "w_in": g["w_in"][0], "w_proj_a": g["w_proj_a"][0], "w_proj_b": g["w_proj_b"][0], "w_out": g["w_out"][0],
        "ln1_g": g["ln1_g"][0], "ln1_b": g["ln1_b"][0], "ln2_g": g["ln2_g"][0], "ln2_b": g["ln2_b"][0],
        "w_gate_up": g["w_gate_up"][0], "w_down": g["w_down"][0],
        "pool_w": g["pool_w_2"][0], "sb_w_qkv": g["sb_w_qkv_2"][0], "sb_w_o": g["sb_w_o_2"][0],
        "ffn_w_gate": g["ffn_w_gate_2"], "ffn_w_up": g["ffn_w_up_2"], "ffn_w_down": g["ffn_w_down_2"],
    }
    return {k: np.ascontiguousarray(v) for k, v in a.items()}


def kernel(**inputs):
    import concourse.bacc as _bacc
    from concourse.bass_utils import run_bass_kernel_spmd as _run

    nc = _bacc.Bacc("TRN2", target_bir_lowering=False, num_devices=1)
    arrays, args = {}, {}
    for name, a in layout(inputs).items():
        arrays[f"in_{name}_dram"] = a
        args[name] = nc.dram_tensor(f"in_{name}_dram", a.shape, mybir.dt.from_np(a.dtype), kind="ExternalInput").ap()
    out = nc.dram_tensor("out_0_dram", (1, S, D), F32, kind="ExternalOutput").ap()
    build(nc, args, out)
    r = _run(nc, [arrays], core_ids=[0])
    return r.results[0]["out_0_dram"]
```

```python
import math

import numpy as np
import concourse.bass as bass
from concourse import mybir

F32 = mybir.dt.float32
F32R = mybir.dt.float32r
U32 = mybir.dt.uint32
I32 = mybir.dt.int32
ALU = mybir.AluOpType
ACT = mybir.ActivationFunctionType
AX = mybir.AxisListType.X

D = 1024
S = 256
NMETA = 16
L = S + NMETA
DFF = 2816
ALPHA = 2.0 ** 0.25
CAP = 64
KEEP = CAP
NE = 32
OVR = S - CAP
FAR = 1.0e6
BANDW = 416
POOLW = 4 * BANDW + 8 * L
HIDE = -(2.0 ** 99)
ATILES = ((0, 0, 256, 0), (128, 112, 144, 256), (256, 240, 16, 400))
AW = 416

CM = {}
_at = 0
for _n, _w in (("ident", 128), ("trineg", 128), ("negones", 128), ("ones", 128), ("ustrict", 128),
               ("masks", 8 * 128), ("iota", 256), ("inv", 16), ("iota4", 4), ("iota32", 32)):
    CM[_n] = (_at, _w)
    _at += _w
CMW = _at
PC = {}
_at = 0
for _n, _w in (("b_in", 44), ("lb", 8), ("hgn", 4), ("nm", 16), ("nf", 16), ("ps", 8), ("fn", 8)):
    PC[_n] = (_at, _w)
    _at += _w
PCW = _at


def shape_constants():
    p = np.arange(128)
    cm = np.zeros((128, CMW), np.float32)

    def put(name, a):
        o, w = CM[name]
        cm[:, o:o + w] = a

    put("ident", np.eye(128))
    put("trineg", -(p[:, None] >= p[None, :]).astype(np.float32))
    put("negones", -1.0)
    put("ones", 1.0)
    put("ustrict", (p[:, None] < p[None, :]).astype(np.float32))
    masks = []
    for m in (64, 32, 16, 8, 4, 2, 1):
        same = (p[:, None] // (2 * m)) == (p[None, :] // (2 * m))
        masks.append(same & (p[:, None] % (2 * m) < m) & (p[None, :] % (2 * m) >= m))
    masks.append(np.eye(128, dtype=bool))
    put("masks", np.concatenate(masks, 1).astype(np.float32))
    put("iota", np.arange(256)[None, :])
    put("inv", 1.0 / (np.arange(16) + 1.0)[None, :])
    put("iota4", np.arange(4)[None, :])
    put("iota32", np.arange(32)[None, :])
    d = np.arange(256)
    f = np.log(np.maximum(d, 1).astype(np.float32) / np.float32(16)) / np.float32(math.log(8.0)) * np.float32(16)
    bucket = np.where(d < 16, d, np.minimum(16 + f.astype(np.int32), 31))
    hot = np.zeros((33, 384), np.float32)
    hot[bucket, 127 + d] = 1.0
    hot[32, :127] = -1.0e30
    scan = np.ones((128, 1024), np.float32)
    scan[:, ::64] = 0.0
    pool = np.zeros((128, POOLW), np.float32)
    pos = np.arange(L)
    for g in range(4):
        win = 2 << g
        x = np.arange(BANDW)[None, :] - 144 - p[:, None]
        pool[:, BANDW * g:BANDW * (g + 1)] = ((x >= 0) & (x < win)) - float(win) * (x == 0)
        o = 4 * BANDW + L * g
        x = pos[None, :] - np.arange(NMETA)[:, None]
        cnt = np.minimum(pos + 1, win)
        pool[:NMETA, o:o + L] = ((x >= 0) & (x < win)) - (x == 0) * cnt[None, :]
        o = 4 * BANDW + 4 * L + L * g
        pool[:, o:o + L] = 1.0 / cnt[None, :]
    am = np.zeros((128, 128 + AW), np.float32)
    am[:, :128] = np.eye(128)
    for k0, q0, w, c in ATILES:
        am[:, 128 + c:128 + c + w] = np.where(k0 + p[:, None] < NMETA + q0 + np.arange(w)[None, :], 0.0, HIDE)
    return cm, hot, scan, pool, am


class Queue:

    def __init__(self, eng, sem):
        self.eng, self.sem, self.n, self.seen = eng, sem, 0, {}

    def wait(self, *tokens):
        for t in tokens:
            if t is not None and self.seen.get(t[0].name, 0) < t[1]:
                self.seen[t[0].name] = t[1]
                self.eng.wait_ge(t[0], t[1])

    def go(self, f):
        self.n += 1
        f(self.eng).then_inc(self.sem, 1)
        return self.sem, self.n

    def quiet(self, f):
        f(self.eng)


def build(nc, t, out):
    sems = []

    def sem(name):
        s = nc.alloc_semaphore(name)
        sems.append(s)
        return s

    pe, act, dve, pool, sp = (Queue(q, sem(n)) for q, n in (
        (nc.tensor, "s_pe"), (nc.scalar, "s_act"), (nc.vector, "s_dve"), (nc.gpsimd, "s_pool"), (nc.sync, "s_sp")))
    dma_count = {}

    def dma(q, dst, src, s, **kw):
        dma_count[s.name] = dma_count.get(s.name, 0) + 16
        q.quiet(lambda e: e.dma_start(dst, src, **kw).then_inc(s, 16))
        return s, dma_count[s.name]

    base = (nc.sbuf_base + 63) // 64 * 64
    KB = 1024

    def sb(name, cols, at, dt=F32, rows=128):
        return nc.alloc_sbuf_tensor_at(name, [rows, cols], dt, offset=base + at)

    def view(x, off, dims, p0=0, rows=128):
        a = x[:, :]
        w = a.ap[0][0]
        return bass.AP(tensor=a.tensor, offset=p0 * w + off, ap=[[w, rows]] + [list(v) for v in dims])

    PS = nc.alloc_psum_tensor("PS", [128, 4096], F32)

    def bank(b, off, *dims, p0=0, rows=128):
        return view(PS, 512 * b + off, dims, p0, rows)

    free = [None] * 8

    def mm(o, a, b, start, stop, last=False, **kw):
        f = lambda e: e.matmul(o, a, b, start=start, stop=stop, **kw)
        return pe.go(f) if last else pe.quiet(f)

    RN, HN = 6, 3
    raw = [sb(f"raw{i}", 2048, 8 * KB * i) for i in range(RN)]
    hi = [sb(f"hi{i}", 2048, 48 * KB + 8 * KB * i, F32R) for i in range(HN)]
    lo = [sb(f"lo{i}", 2048, 72 * KB + 8 * KB * i, F32R) for i in range(HN)]
    cm = sb("cm", CMW, 96 * KB)
    pc = sb("pc", PCW, 96 * KB + 7936)
    small = sb("small", 128, 96 * KB + 7936 + 512)
    flag = sb("flag", 8, 96 * KB + 7936 + 1024, U32)
    A0 = 105 * KB

    def con(name, off=0, w=None, p0=0, rows=128):
        o, cw = CM[name]
        return view(cm, o + off, [[1, w or cw]], p0, rows)

    def par(name, i=0, w=1):
        return view(pc, PC[name][0] + i, [[1, w]])

    units = []

    def tcols(w, rows, c0, n):
        return w[rows[0]:rows[1], c0:c0 + n].rearrange("(c p) n -> p c n", p=128)

    win = t["w_in"]
    for nm in ("f", "q", "i", "mq", "mk", "mv", "g"):
        c0 = {"q": 0, "f": 512, "i": 1024, "g": 1536, "mq": 2048, "mk": 2560, "mv": 3072}[nm]
        for j in range(2):
            units.append((nm, j, tcols(win, (0, D), c0 + 256 * j, 256), 256, 8))
    for nm, c0 in (("ga", 3584), ("gb", 4608)):
        for j in range(4):
            units.append((nm, j, tcols(win, (0, D), c0 + 256 * j, 256), 256, 8))
    for nm in ("w_proj_a", "w_proj_b"):
        for j in range(2):
            units.append((nm, j, tcols(t[nm], (0, 512), 512 * j, 512), 512, 4))
    for j in range(4):
        units.append(("w_out", j, tcols(t["w_out"], (0, D), 256 * j, 256), 256, 8))

    def gu(e):
        for j in range(4):
            units.append(("gu", (e, j), tcols(t["w_gate_up"][e], (256 * j, 256 * j + 256), 0, 1024), 1024, 2))

    def dn(e):
        for j in range(2):
            units.append(("dn", (e, j), tcols(t["w_down"][e], (256 * j, 256 * j + 256), 0, 1024), 1024, 2))

    for e in range(NE):
        gu(e)
        if e:
            dn(e - 1)
    dn(NE - 1)

    def ffn_units(i):
        for f in range(11):
            units.append(("fg", (i, f), tcols(t["ffn_w_gate"][i], (0, D), 256 * f, 256), 256, 8))
            units.append(("fu", (i, f), tcols(t["ffn_w_up"][i], (0, D), 256 * f, 256), 256, 8))
        for c in range(4):
            for k in range(3):
                n = 8 if k < 2 else 6
                units.append(("fd", (i, c, k), tcols(t["ffn_w_down"][i], (1024 * k, 1024 * k + 128 * n), 256 * c, 256), 256, n))

    for g in range(4):
        units.append(("pw", g, tcols(t["pool_w"][g], (0, 256), 0, 256), 256, 2))
    ffn_units(0)
    for j in range(4):
        for i in range(3):
            units.append(("qkv", (i, j), tcols(t["sb_w_qkv"], (0, D), 1024 * i + 256 * j, 256), 256, 8))
    for j in range(4):
        units.append(("wo", j, tcols(t["sb_w_o"], (0, 768), 256 * j, 256), 256, 6))
    units.append(("wo", 4, tcols(t["sb_w_o"], (768, 1024), 0, 1024), 1024, 2))
    ffn_units(1)
    NU = len(units)

    s_raw = [sem(f"s_raw{i}") for i in range(RN)]
    loaded, hi_tok, lo_tok, used = {}, {}, {}, {}

    E0 = next(i for i, u in enumerate(units) if u[0] == "gu")
    EN = 5
    rbuf = lambda i: extra[i - E0] if E0 <= i < E0 + EN else raw[(i if i < E0 else i - EN) % RN]
    s_ex = [sem(f"s_ex{i}") for i in range(EN)]
    extra = {}

    def load(i):
        if i >= NU:
            return
        _, _, src, n, c = units[i]
        prev = i - RN - EN if E0 + EN <= i < E0 + EN + RN else i - RN
        if prev >= 0:
            sp.wait(hi_tok[prev], lo_tok[prev])
        loaded[i] = dma(sp, view(rbuf(i), 0, [[n, c], [1, n]]), src, s_raw[(i if i < E0 else i - EN) % RN])

    state = {"prepped": 0, "next": 0}

    def prep():
        i = state["prepped"]
        if i >= NU:
            return
        state["prepped"] += 1
        kind, _, _, n, c = units[i]
        r, h, l = (view(x, 0, [[1, n * c]]) for x in (rbuf(i), hi[i % HN], lo[i % HN]))
        hf = view(hi[i % HN], 0, [[1, n * c]]).bitcast(F32)
        act.wait(loaded[i], used.get(i - HN))
        hi_tok[i] = act.go(lambda e: e.copy(h, r))
        q = pool if kind == "dn" and units[i][1][1] == 0 or i in (E0 + 1, E0 + 2) else dve
        q.wait(loaded[i], hi_tok[i], used.get(i - HN))
        lo_tok[i] = q.go(lambda e: e.tensor_tensor(l, r, hf, ALU.subtract))
        if i < E0:
            load(i + RN if i + RN < E0 else i + RN + EN)
        elif i >= E0 + EN:
            load(i + RN)

    class Unit:
        pass

    def take(kind, tag, ahead=2):
        i = state["next"]
        state["next"] += 1
        assert units[i][0] == kind and units[i][1] == tag, (units[i][:2], kind, tag)
        while state["prepped"] <= min(i + ahead, NU - 1):
            prep()
        pe.wait(hi_tok[i], lo_tok[i])
        u = Unit()
        n = units[i][3]
        u.i = i
        u.h = lambda k, c0, w: view(hi[i % HN], n * k + c0, [[1, w]])
        u.l = lambda k, c0, w: view(lo[i % HN], n * k + c0, [[1, w]])
        return u

    def release(u, tok):
        used[u.i] = tok

    def stationary_w(u, o, m, ks, xh, xl, start=True, stop=True, need=None):
        for n, k in enumerate(ks):
            if need is not None:
                pe.wait(*need[k])
            a, b = start and n == 0, stop and n == len(ks) - 1
            mm(o, u.h(n, 128 * m, 128), xh(k), a, False)
            mm(o, u.h(n, 128 * m, 128), xl(k), False, False)
            tok = mm(o, u.l(n, 128 * m, 128), xh(k), False, b, last=(n == len(ks) - 1))
        return tok

    def moving_w(u, o, c0, w, ks, xh, xl, start=True, stop=True):
        for n, k in enumerate(ks):
            a, b = start and n == 0, stop and n == len(ks) - 1
            mm(o, xh(k), u.h(n, c0, w), a, False)
            mm(o, xl(k), u.h(n, c0, w), False, False)
            tok = mm(o, xh(k), u.l(n, c0, w), False, b, last=(n == len(ks) - 1))
        return tok

    at = A0
    def area(name, cols, dt=F32, rows=128):
        nonlocal at
        x = sb(name, cols, at, dt, rows)
        at += 4 * cols
        return x

    XH, XL = area("XH", 2048, F32R), area("XL", 2048, F32R)
    QT, BT, KT, VA, GT = (area(n, 1024) for n in ("QT", "BT", "KT", "VA", "GT"))
    MQ, MK, MV = (area(n, 1024) for n in ("MQ", "MK", "MV"))
    SGA, SGB = area("SGA", 2048), area("SGB", 2048)
    D0, D1 = area("D0", 1024), area("D1", 1024)
    at -= 4096
    SL = area("SL", 1024)
    QE, KE = area("QE", 1024), area("KE", 1024)
    AA0, AA1 = area("AA0", 1024), area("AA1", 512)
    TT = [area(f"TT{i}", 512) for i in range(2)]
    PT = area("PT", 768)
    at = A0 + 99 * KB - 1280
    rowp = area("rowp", 1060, rows=1)
    assert at <= 207 * KB, at
    SCN = sb("SCN", 1024, A0 + 4 * (2048 * 2 + 1024 * 8 + 4096 + 1024))
    xraw = sb("xraw", 2048, A0 + 4 * (2048 * 2 + 1024 * 8))
    hot = sb("hot", 384, A0 + 4 * (2048 * 3 + 1024 * 8), rows=33)
    rbs = sb("rbs", 8, A0 + 4 * (2048 * 3 + 1024 * 8) + 1536, rows=33)
    wtab = sb("wtab", 384, A0 + 4 * (2048 * 3 + 1024 * 8) + 1600, rows=8)

    d_tab = nc.dram_tensor("d_tab", (8, 384), F32).ap()
    d_o = nc.dram_tensor("d_o", (NE * OVR, D), F32).ap()
    d_y = nc.dram_tensor("d_y", (NE * CAP, D), F32).ap()

    s_x, s_c, s_p, s_r, s_scn, s_hot, s_xt = (sem(n) for n in ("s_x", "s_c", "s_p", "s_r", "s_scn", "s_hot", "s_xt"))
    s_x1 = sem("s_x1")
    tx = []
    for n in range(2):
        half = lambda x: view(x, 1024 * n, [[1, 1024]])
        tx.append(dma(act if n else sp, half(xraw), t["xT"][:, 1024 * n:1024 * n + 1024], (s_x, s_x1)[n]))
    load(0)
    load(1)
    tp = dma(act, pc[:, :], t["pc"], s_p)
    load(2)
    tscn = dma(act, SCN[:, :], t["scan"], s_scn)
    tr = dma(act, rowp[:, :], t["rows"], s_r)
    dma(act, rbs[:, :], t["rb"], s_hot)
    thot = dma(act, hot[:, :], t["hot"], s_hot)
    load(3)
    tcm = dma(act, cm[:, :], t["cm"], s_c)
    load(4)
    load(5)

    xs_ready = {}
    for n in range(2):
        h, l, r = (view(x, 1024 * n, [[1, 1024]]) for x in (XH, XL, xraw))
        act.wait(tx[n])
        txh = act.go(lambda e: e.copy(h, r))
        dve.wait(tx[n], txh)
        txl = dve.go(lambda e: e.tensor_tensor(l, r, h.bitcast(F32), ALU.subtract))
        for k in range(4 * n, 4 * n + 4):
            xs_ready[k] = (txh, txl)
    prep()
    xh = lambda k: view(XH, 256 * k, [[1, 256]])
    xl = lambda k: view(XL, 256 * k, [[1, 256]])
    xht = lambda i: (lambda k: view(XH, 256 * k + 128 * i, [[1, 128]]))
    xlt = lambda i: (lambda k: view(XL, 256 * k + 128 * i, [[1, 128]]))

    sm = lambda o, w=1: view(small, o, [[1, w]])
    dve.wait(tp)
    a0 = dve.go(lambda e: e.tensor_tensor(sm(0, 4), par("lb", 0, 4), par("lb", 4, 4), ALU.max))
    dve.wait(a0)
    dve.go(lambda e: e.tensor_tensor(sm(4, 4), par("lb", 0, 4), sm(0, 4), ALU.subtract))
    a0 = dve.go(lambda e: e.tensor_tensor(sm(8, 4), par("lb", 4, 4), sm(0, 4), ALU.subtract))
    nb = dve.go(lambda e: e.tensor_scalar(sm(32, 4), par("b_in", 4, 4), -1.0, None, ALU.mult))
    act.wait(a0)
    a0 = act.go(lambda e: e.activation(sm(12, 8), sm(4, 8), ACT.Exp))
    dve.wait(a0)
    a0 = dve.go(lambda e: e.tensor_tensor(sm(20, 4), sm(12, 4), sm(16, 4), ALU.add))
    dve.wait(a0)
    a0 = dve.go(lambda e: e.reciprocal(sm(20, 4), sm(20, 4)))
    dve.wait(a0)
    dve.go(lambda e: e.tensor_tensor(sm(24, 4), sm(12, 4), sm(20, 4), ALU.mult))
    tlb = dve.go(lambda e: e.tensor_tensor(sm(28, 4), sm(16, 4), sm(20, 4), ALU.mult))
    LB, OLB = 24, 28
    pool.go(lambda e: e.memset(QE[:, :], 0.0))
    tz = pool.go(lambda e: e.memset(KE[:, :], 0.0))

    nproj = [0]

    def project_t(nm, j, evac):
        b = nproj[0] % 3
        nproj[0] += 1
        u = take(nm, j)
        pe.wait(free[b])
        for m in range(2):
            tok = stationary_w(u, bank(b, 256 * m, [1, 256]), m, range(8), xh, xl, need=xs_ready)
        release(u, tok)
        free[b] = evac(b, tok)

    def project_n(nm, j, row, evac):
        b = nproj[0] % 3
        nproj[0] += 1
        u = take(nm, j)
        pe.wait(free[b], txh, txl, tr, tcm)
        for i in range(2):
            o = bank(b, 256 * i, [1, 256])
            mm(o, con("ones", p0=0, rows=1), view(rowp, row + 256 * j, [[1, 256]], rows=1), True, False)
            tok = moving_w(u, o, 0, 256, range(8), xht(i), xlt(i), start=False)
        release(u, tok)
        free[b] = evac(b, tok)

    fk = {}

    def evac_f(j):
        def f(b, tok):
            act.wait(tok, tp, nb)
            for m in range(2):
                h = 2 * j + m
                act.go(lambda e: e.activation(view(BT, 256 * h, [[1, 256]]), bank(b, 256 * m, [1, 256]), ACT.Sigmoid, bias=par("b_in", 4 + h)))
                r = act.go(lambda e: e.activation(view(KT, 256 * h, [[1, 256]]), bank(b, 256 * m, [1, 256]), ACT.Sigmoid, bias=sm(32 + h), scale=-1.0))
                dve.wait(r, tlb)
                fk["k", h] = dve.go(lambda e: e.tensor_scalar(view(KT, 256 * h, [[1, 256]]), view(KT, 256 * h, [[1, 256]]), sm(OLB + h), None, ALU.mult))
                fk["f", h] = dve.go(lambda e: e.tensor_scalar(view(BT, 256 * h, [[1, 256]]), view(BT, 256 * h, [[1, 256]]), sm(OLB + h), sm(LB + h), ALU.mult, ALU.add))
            return r
        return f

    def evac_act(dst, bcol, func, key):
        def f(b, tok):
            act.wait(tok, tp)
            for m in range(2):
                r = act.go(lambda e, m=m: e.activation(dst(m), bank(b, 256 * m, [1, 256]), func, bias=par("b_in", bcol + m)))
            fk[key] = r
            return r
        return f

    def evac_tok(dst, key):
        def f(b, tok):
            dve.wait(tok)
            r = dve.go(lambda e: e.tensor_copy(dst, bank(b, 0, [256, 2], [1, 256])))
            fk[key] = r
            return r
        return f

    project_t("f", 0, evac_f(0))
    project_t("f", 1, evac_f(1))

    s_tab = sem("s_tab")
    s_tt = [sem("s_tt0"), sem("s_tt1")]
    pe.wait(thot)
    tk = mm(bank(7, 0, [1, 384], rows=8), rbs[:, :], hot[:, :], True, True, last=True)
    dve.wait(tk)
    tk = dve.go(lambda e: e.tensor_copy(wtab[:, :], bank(7, 0, [1, 384], rows=8)))
    free[7] = tk
    act.wait(tk)
    ttab = dma(act, d_tab, wtab[:, :], s_tab)
    def toeplitz(pair, q):
        return dma(q, view(TT[pair % 2], 0, [[256, 2], [1, 256]]),
                   bass.AP(tensor=d_tab.tensor, offset=768 * pair, ap=[[1, 128], [384, 2], [1, 256]]), s_tt[pair % 2])

    act.wait(fk["f", 3])
    tk = act.go(lambda e: e.activation(BT[:, :], BT[:, :], ACT.Ln))
    dve.wait(tk, tscn)
    tb = dve.go(lambda e: e.tensor_tensor_scan(BT[:, :], SCN[:, :], BT[:, :], 0.0, ALU.mult, ALU.add))
    DE = [D0, D1]
    LV = [128, 64, 32, 16, 8, 4, 2, 1, 0]
    lev = {"free": {0: None, 1: tb}}

    def level_d(n):
        m, d = LV[n], DE[n % 2]
        if m == 0:
            return
        pool.wait(tb, lev["free"][n % 2])
        if m == 128:
            blk = lambda x, c, k: view(x, 64 * c, [[256, 4], [64, k], [1, 64]])
            end = lambda c, k: view(BT, 64 * c + 63, [[256, 4], [64, k], [0, 64]])
            r = pool.go(lambda e: e.tensor_tensor(blk(d, 0, 2), end(0, 2), blk(BT, 0, 2), ALU.subtract))
            pool.wait(r)
            pool.go(lambda e: e.tensor_tensor(blk(d, 0, 1), blk(d, 0, 1), end(1, 1), ALU.add))
            r = pool.go(lambda e: e.tensor_tensor(blk(d, 3, 1), blk(BT, 3, 1), end(2, 1), ALU.add))
            act.wait(r)
            act.go(lambda e: e.activation(view(d, 128, [[256, 4], [1, 64]]), view(BT, 128, [[256, 4], [1, 64]]), ACT.Exp))
            act.go(lambda e: e.activation(view(d, 192, [[256, 4], [1, 64]]), view(d, 192, [[256, 4], [1, 64]]), ACT.Exp))
            r = act.go(lambda e: e.activation(view(d, 0, [[256, 4], [1, 128]]), view(d, 0, [[256, 4], [1, 128]]), ACT.Exp))
        else:
            nbk = 512 // m
            half = lambda x, o: view(x, o, [[2 * m, nbk], [1, m]])
            mid = view(BT, m - 1, [[2 * m, nbk], [0, m]])
            r = pool.go(lambda e: e.tensor_tensor(half(d, 0), mid, half(BT, 0), ALU.subtract))
            if m < 64:
                r = pool.go(lambda e: e.tensor_tensor(half(d, m), half(BT, m), mid, ALU.subtract))
                act.wait(r)
                r = act.go(lambda e: e.activation(d[:, :], d[:, :], ACT.Exp))
            else:
                act.wait(r)
                act.go(lambda e: e.activation(half(d, 0), half(d, 0), ACT.Exp))
                r = act.go(lambda e: e.activation(half(d, m), half(BT, m), ACT.Exp))
        lev["e", n] = r

    def level_m(n):
        m, d = LV[n], DE[n % 2]
        dve.wait(lev.get(("e", n)), fk["q", 1], fk["k", 3], fk["k", 1], lev.get("pe"), tz)
        if m == 128:
            lh = lambda x, o: view(x, o, [[256, 4], [1, 128]])
            dve.go(lambda e: e.tensor_tensor(lh(KE, 0), lh(KT, 0), lh(d, 0), ALU.mult))
            r = dve.go(lambda e: e.tensor_tensor(lh(QE, 128), lh(QT, 128), lh(d, 128), ALU.mult))
        elif m:
            half = lambda x, o: view(x, o, [[2 * m, 512 // m], [1, m]])
            dve.go(lambda e: e.tensor_tensor(half(KE, 0), half(KT, 0), half(d, 0), ALU.mult))
            r = dve.go(lambda e: e.tensor_tensor(half(QE, m), half(QT, m), half(d, m), ALU.mult))
        else:
            r = None
        if m:
            lev["free"][n % 2] = r
        lev["m"] = r

    def level_s(n):
        m, r = LV[n], lev["m"]
        kx, qx = (KE, QE) if m else (KT, QT)
        pe.wait(r, fk["q", 1], fk["k", 3], free[3], free[4])
        if m == 128:
            for h in range(4):
                r = mm(bank(3, 128 * h, [1, 128]), view(kx, 256 * h, [[1, 128]]), view(qx, 256 * h + 128, [[1, 128]]), True, True, last=(h == 3))
            dve.wait(r, lev["a"])
            free[3] = dve.go(lambda e: e.tensor_copy(view(AA0, 128, [[256, 4], [1, 128]]), bank(3, 0, [128, 4], [1, 128])))
        else:
            for i in range(2):
                for h in range(4):
                    r = mm(bank(3 + i, 128 * h, [1, 128]), view(kx, 256 * h + 128 * i, [[1, 128]]),
                           view(qx, 256 * h + 128 * i, [[1, 128]]), True, True, last=(h == 3))
                mask = view(cm, CM["masks"][0] + 128 * (n - 1), [[0, 4], [1, 128]]).bitcast(U32)
                o = view(AA0, 0, [[256, 4], [1, 128]]) if i == 0 else view(AA1, 0, [[128, 4], [1, 128]])
                dve.wait(r, tcm, lev["a"])
                free[3 + i] = dve.go(lambda e, i=i, o=o, mask=mask: e.copy_predicated(o, mask, bank(3 + i, 0, [128, 4], [1, 128])))
                lev["acc"] = free[3 + i]
        lev["pe"] = r

    dve.go(lambda e: e.memset(AA0[:, :], 0.0))
    lev["a"] = dve.go(lambda e: e.memset(AA1[:, :], 0.0))
    for j in range(2):
        project_t("q", j, evac_act(lambda m, j=j: view(QT, 256 * (2 * j + m), [[1, 256]]), 2 * j, ACT.Silu, ("q", j)))
    level_d(0)
    work = [lambda j=j: project_n("i", j, 0, evac_tok(view(VA, 256 * j, [[512, 2], [1, 256]]), ("v", j))) for j in range(2)]
    for nm, c0, dst in (("mq", 16, MQ), ("mk", 20, MK)):
        for j in range(2):
            work.append(lambda nm=nm, c0=c0, j=j, dst=dst: project_t(
                nm, j, evac_act(lambda m: view(dst, 256 * (2 * j + m), [[1, 256]]), c0 + 2 * j, ACT.Identity, (nm, j))))
    for j in range(2):
        work.append(lambda j=j: project_n("mv", j, 512, evac_tok(view(MV, 256 * j, [[512, 2], [1, 256]]), ("mv", j))))
    for j in range(2):
        work.append(lambda j=j: project_t("g", j, evac_act(lambda m: view(GT, 256 * (2 * j + m), [[1, 256]]), 12 + 2 * j, ACT.Silu, ("g", j))))
    work[0]()
    level_d(1)
    pool.wait(ttab)
    tt_tok = {0: toeplitz(0, pool), 1: toeplitz(1, pool)}
    for n, f in enumerate(work[1:]):
        if n < len(LV):
            level_m(n)
        f()
        if n < len(LV):
            level_s(n)
        if n + 2 < len(LV):
            level_d(n + 2)
    for h in range(4):
        dve.wait(fk["g", h // 2])
        fk["gn"] = dve.go(lambda e, h=h: e.tensor_scalar(view(GT, 256 * h, [[1, 256]]), view(GT, 256 * h, [[1, 256]]), par("hgn", h), None, ALU.mult))

    def gate(nm, j, c0, dst):
        project_t(nm, j, evac_act(lambda m: view(dst, 256 * (2 * j + m), [[1, 256]]), c0 + 2 * j, ACT.Sigmoid, (nm, j)))

    OT = sb("OT", 1024, A0 + 4 * (2048 * 2 + 1024 * 8 + 4096))
    SQ = QE
    OAH = sb("OAH", 1024, A0 + 4 * (2048 * 2), F32R)
    OAL = sb("OAL", 1024, A0 + 4 * (2048 * 2 + 1024), F32R)
    OBH = sb("OBH", 1024, A0 + 4 * (2048 * 2 + 2048), F32R)
    OBL = sb("OBL", 1024, A0 + 4 * (2048 * 2 + 3072), F32R)
    gate("ga", 0, 28, SGA)
    pe.wait(lev["acc"], free[3], fk["v", 0], fk["v", 1], free[5], free[6])
    for h in range(4):
        o = lambda c, w: bank(5 + h // 2, 256 * (h % 2) + c, [1, w])
        mm(o(0, 256), view(VA, 128 * h, [[1, 128]]), view(AA0, 256 * h, [[1, 256]]), True, False)
        r = mm(o(128, 128), view(VA, 512 + 128 * h, [[1, 128]]), view(AA1, 128 * h, [[1, 128]]), False, True, last=(h % 2 == 1))
    dve.wait(r)
    to = dve.go(lambda e: e.tensor_copy(OT[:, :], bank(5, 0, [1, 1024])))
    act.wait(r, lev["pe"], to)
    tq = act.go(lambda e: e.activation(SQ[:, :], OT[:, :], ACT.Square))
    gate("ga", 1, 28, SGA)
    pe.wait(tq, to, tcm)
    for c in range(8):
        r = mm(bank(5, c, [1, 1]), view(SQ, 128 * c, [[1, 128]]), con("ones", w=1), True, True, last=(c == 7))
    dve.wait(r)
    r = dve.go(lambda e: e.tensor_scalar(sm(80, 8), bank(5, 0, [1, 8]), 1.0 / 128, 1e-5, ALU.mult, ALU.add))
    dve.wait(r)
    r = dve.go(lambda e: e.reciprocal(sm(80, 8), sm(80, 8)))
    act.wait(r)
    r = act.go(lambda e: e.activation(sm(80, 8), sm(80, 8), ACT.Sqrt))
    dve.wait(r)
    for c in range(8):
        r = dve.go(lambda e, c=c: e.tensor_scalar(view(KE, 128 * c, [[1, 128]]), con("ident"), sm(80 + c), None, ALU.mult))
    pe.wait(r)
    for i in range(2):
        r = mm(bank(5 + i, 0, [1, 512]), con("ones"), view(KE, 512 * i, [[1, 512]]), True, True, last=True)
    dve.wait(r, to)
    free[5] = free[6] = r = dve.go(lambda e: e.tensor_tensor(OT[:, :], OT[:, :], bank(5, 0, [1, 1024]), ALU.mult))
    dve.wait(r, fk["gn"])
    r = dve.go(lambda e: e.tensor_tensor(OT[:, :], OT[:, :], GT[:, :], ALU.mult))
    act.wait(r, lev["pe"])
    toh = act.go(lambda e: e.copy(OAH[:, :], OT[:, :]))
    dve.wait(toh)
    tol = dve.go(lambda e: e.tensor_tensor(OAL[:, :], OT[:, :], OAH[:, :].bitcast(F32), ALU.subtract))
    xtok = sb("xtok", 2048, A0 + 4 * (2048 * 3 + 1024 * 8 + 2048 + 2048))
    pool.wait(toh, tol)
    txt = dma(pool, view(xtok, 0, [[1024, 2], [1, 1024]]), t["x"][0].rearrange("(i p) n -> p i n", p=128), s_xt)
    gate("ga", 2, 28, SGA)
    gate("ga", 3, 28, SGA)

    moba = {"pt": [None, None], "sl": tol}

    def moba_scores(g):
        pe.wait(fk["mq", 0], fk["mq", 1], fk["mk", 0], fk["mk", 1], free[3], free[4])
        for a in range(2):
            p0 = 64 * a
            mq = lambda i: view(MQ, 256 * g + 128 * i, [[1, 128]], p0, 64)
            mm(bank(3 + a, 0, [1, 128]), mq(0), view(MK, 256 * g, [[1, 128]], p0, 64), True, True)
            r = mm(bank(3 + a, 128, [1, 256]), mq(1), view(MK, 256 * g, [[1, 256]], p0, 64), True, True, last=(a == 1))
        x = TT[g % 2]
        dve.wait(r, tt_tok[g], moba["sl"], moba["pt"][0], moba["pt"][1])
        r0 = dve.go(lambda e: e.scalar_tensor_tensor(view(SL, 0, [[384, 2], [1, 128]]), bank(3, 0, [512, 2], [1, 128]), 0.125,
                                                     view(x, 127, [[256, 2], [-1, 128]]), ALU.mult, ALU.add))
        r1 = dve.go(lambda e: e.scalar_tensor_tensor(view(SL, 128, [[384, 2], [1, 256]]), bank(3, 128, [512, 2], [1, 256]), 0.125,
                                                     view(x, 255, [[256, 2], [-1, 256]]), ALU.mult, ALU.add))
        free[3] = free[4] = r1
        if g + 2 < 4:
            pool.wait(r1)
            tt_tok[g + 2] = toeplitz(g + 2, pool)
        dve.wait(r1)
        dve.go(lambda e: e.tensor_reduce(sm(64, 2), view(SL, 0, [[384, 2], [1, 128]]), AX, ALU.max))
        r = dve.go(lambda e: e.tensor_reduce(sm(66, 2), view(SL, 128, [[384, 2], [1, 256]]), AX, ALU.max))
        dve.wait(r)
        r = dve.go(lambda e: e.tensor_scalar(sm(68, 4), sm(64, 4), -1.0, None, ALU.mult))
        act.wait(r)
        for a in range(2):
            for i in range(2):
                s = view(SL, 384 * a + 128 * i, [[1, 128 + 128 * i]])
                r = act.go(lambda e, s=s, c=68 + 2 * i + a, z=72 + 2 * i + a: e.activation(s, s, ACT.Exp, bias=sm(c), accum_out=sm(z)))
        dve.wait(r)
        r = dve.go(lambda e: e.reciprocal(sm(76, 4), sm(72, 4)))
        dve.wait(r)
        for a in range(2):
            for i in range(2):
                s = view(SL, 384 * a + 128 * i, [[1, 128 + 128 * i]])
                r = dve.go(lambda e, s=s, c=76 + 2 * i + a: e.tensor_scalar(s, s, sm(c), None, ALU.mult))
        moba["p"] = r

    def moba_out(g):
        pe.wait(moba["p"], tcm, free[5], free[6], free[7])
        tr_ = []
        for a in range(2):
            for c, s in ((0, 0), (128, 128), (256, 256)):
                r = pe.go(lambda e, c=c, s=s, a=a: e.transpose(bank(5 + a, c, [1, 128]), view(SL, 384 * a + s, [[1, 128]]), con("ident")))
            q = act if a else dve
            q.wait(r, moba.get("pv"))
            f = (lambda e, a=a: e.copy(view(PT, 384 * a, [[1, 384]]), bank(5 + a, 0, [1, 384]))) if a else \
                (lambda e, a=a: e.tensor_copy(view(PT, 384 * a, [[1, 384]]), bank(5 + a, 0, [1, 384])))
            free[5 + a] = q.go(f)
            tr_.append(free[5 + a])
            moba["pt"][a] = r
        pe.wait(*tr_)
        pe.wait(fk["mv", 0], fk["mv", 1])
        for a in range(2):
            h = 2 * g + a
            mm(bank(7, 0, [1, 256], p0=64 * a, rows=64), view(MV, 64 * h, [[1, 64]]), view(PT, 384 * a, [[1, 256]]), True, False)
            r = mm(bank(7, 128, [1, 128], p0=64 * a, rows=64), view(MV, 512 + 64 * h, [[1, 64]]), view(PT, 384 * a + 256, [[1, 128]]), False, True, last=(a == 1))
        moba["pv"] = r
        act.wait(r, tol)
        rh = act.go(lambda e: e.copy(view(OBH, 256 * g, [[1, 256]]), bank(7, 0, [1, 256])))
        dve.wait(rh)
        free[7] = dve.go(lambda e: e.tensor_tensor(view(OBL, 256 * g, [[1, 256]]), bank(7, 0, [1, 256]),
                                                   view(OBH, 256 * g, [[1, 256]]).bitcast(F32), ALU.subtract))
        moba["hl"] = (rh, free[7])

    moba_scores(0)
    for g in range(4):
        gate("gb", g, 36, SGB)
        moba_out(g)
        if g < 3:
            moba_scores(g + 1)

    def load_extra(n, off, *toks):
        extra[n] = sb(f"EX{n}", 2048, A0 + off * KB)
        _, _, src, w, c = units[E0 + n]
        sp.wait(*toks)
        loaded[E0 + n] = dma(sp, view(extra[n], 0, [[w, c], [1, w]]), src, s_ex[n])

    load_extra(0, 40, moba["hl"][1], moba["p"], moba["pv"])
    load_extra(2, 80)
    load_extra(3, 64)
    load_extra(4, 88)

    MXH = sb("MXH", 2048, A0, F32R)
    MXL = sb("MXL", 2048, A0 + 8192, F32R)
    xdone = used[state["next"] - 1]
    mix, mix_need = {}, {}
    for w, src, sg, need in (("w_proj_a", (OAH, OAL), SGA, (toh, tol)), ("w_proj_b", (OBH, OBL), SGB, moba["hl"])):
        for j in range(2):
            b = 0 if j == 0 else 2
            u = take(w, j)
            pe.wait(*need)
            pe.wait(free[b], free[b + 1])
            for m in range(4):
                tok = stationary_w(u, bank(b + m // 2, 256 * (m % 2), [1, 256]), m, range(4),
                                   lambda k: view(src[0], 256 * k, [[1, 256]]), lambda k: view(src[1], 256 * k, [[1, 256]]))
            release(u, tok)
            dve.wait(tok, fk["ga", 3], fk["gb", 3])
            for n in range(2):
                at2 = 1024 * j + 512 * n
                s = view(sg, at2, [[1, 512]])
                r = dve.go(lambda e: e.tensor_tensor(s, bank(b + n, 0, [1, 512]), s, ALU.mult))
                free[b + n] = r
                if w == "w_proj_b":
                    dve.wait(r, mix["a", j])
                    o, h, l = (view(x, at2, [[1, 512]]) for x in (SGA, MXH, MXL))
                    r = dve.go(lambda e: e.tensor_tensor(o, o, s, ALU.add))
                    act.wait(r, xdone)
                    mix["h", j, n] = act.go(lambda e: e.copy(h, o))
                else:
                    mix["a", j] = r
            if w == "w_proj_b":
                for n in range(2):
                    o, h, l = (view(x, 1024 * j + 512 * n, [[1, 512]]) for x in (SGA, MXH, MXL))
                    rh = mix["h", j, n]
                    dve.wait(rh, xdone)
                    rl = dve.go(lambda e: e.tensor_tensor(l, o, h.bitcast(F32), ALU.subtract))
                    for k in (4 * j + 2 * n, 4 * j + 2 * n + 1):
                        mix_need[k] = (rh, rl)
    LG = sb("LG", 1024, A0 + 56 * KB)
    LBT = sb("LBT", 1024, A0 + 60 * KB)
    s_ln, s_ln2 = sem("s_ln"), sem("s_ln2")

    def bcast_row(q, dst, src, s_ln):
        return dma(q, dst[:, :], bass.AP(tensor=src.tensor, offset=src.offset, ap=[[0, 128], [1, 1024]]), s_ln)

    load_extra(1, 48, *mix_need[3], *mix_need[7])
    WR = sb("WR", 288, A0 + 29 * KB)
    s_wr = sem("s_wr")
    act.wait(*mix_need[7])
    bcast_row(act, LG, t["ln1_g"], s_ln)
    tln = bcast_row(act, LBT, t["ln1_b"], s_ln)
    twr = dma(act, WR[:, :], t["wr"], s_wr)
    wu = {}
    for j, i, ks in ((0, 0, (0, 4)), (0, 1, (0, 4)), (0, 0, (4, 8)), (0, 1, (4, 8)), (1, 0, (0, 8)), (1, 1, (0, 8)),
                     (2, 0, (0, 8)), (3, 0, (0, 8)), (2, 1, (0, 8)), (3, 1, (0, 8))):
        if j not in wu:
            wu[j] = take("w_out", j, ahead=1 if j == 3 else 2)
        b = 4 + 2 * i + j // 2
        pe.wait(free[b])
        for k in range(*ks):
            pe.wait(*mix_need[k])
        u = wu[j]
        for k in range(*ks):
            x, y = (view(m, 256 * k + 128 * i, [[1, 128]]) for m in (MXH, MXL))
            o = bank(b, 256 * (j % 2), [1, 256])
            mm(o, x, u.h(k, 0, 256), k == 0, False)
            mm(o, y, u.h(k, 0, 256), False, False)
            tok = mm(o, x, u.l(k, 0, 256), False, k == 7, last=(k == ks[1] - 1))
        if ks[1] == 8:
            mix["o", i] = tok
            if i == 1:
                release(u, tok)

    X1 = sb("X1", 2048, A0 + 16 * KB)
    X1H = sb("X1H", 2048, A0, F32R)
    X1L = sb("X1L", 2048, A0 + 8 * KB, F32R)
    RTR = sb("RTR", 1024, A0 + 24 * KB)
    ST = sb("ST", 64, A0 + 28 * KB)

    def layer_norm(i, xin, g, b, tok, tl, reads=None):
        o = view(xin, 1024 * i, [[1, 1024]])
        st = lambda c, w: view(ST, 32 * i + c, [[1, w]])
        dve.wait(tok)
        dve.go(lambda e: e.bn_stats(st(0, 6), view(xin, 1024 * i, [[1, 512]])))
        r = dve.go(lambda e: e.bn_stats(st(6, 6), view(xin, 1024 * i + 512, [[1, 512]])))
        dve.wait(r)
        r = dve.go(lambda e: e.bn_aggr(st(12, 2), st(0, 12)))
        dve.wait(r)
        r = dve.go(lambda e: e.tensor_scalar(st(14, 1), st(13, 1), 1e-5, None, ALU.add))
        dve.wait(r)
        r = dve.go(lambda e: e.reciprocal(st(14, 1), st(14, 1)))
        act.wait(r)
        r = act.go(lambda e: e.activation(st(14, 1), st(14, 1), ACT.Sqrt))
        dve.wait(r)
        r = dve.go(lambda e: e.tensor_scalar(o, o, st(12, 1), st(14, 1), ALU.subtract, ALU.mult))
        dve.wait(r, tl)
        r = dve.go(lambda e: e.tensor_tensor(o, o, g[:, :], ALU.mult))
        q = dve if i else pool
        q.wait(r, tl)
        return q.go(lambda e: e.tensor_tensor(o, o, b[:, :], ALU.add))

    x1_tok = []
    for i in range(2):
        dve.wait(mix["o", i], txt)
        r = dve.go(lambda e, i=i: e.scalar_tensor_tensor(view(X1, 1024 * i, [[1, 1024]]), view(xtok, 1024 * i, [[1, 1024]]), ALPHA,
                                                         bank(4 + 2 * i, 0, [1, 1024]), ALU.mult, ALU.add))
        free[4 + 2 * i] = free[5 + 2 * i] = r
        x1_tok.append(layer_norm(i, X1, LG, LBT, r, tln))
        prep()
    wout_done = used[state["next"] - 1]

    X1T = sb("X1T", 2048, A0 + 32 * KB)
    LT = sb("LT", 256, A0 + 30 * KB + 256, rows=36)
    lt_tok = []
    pe.wait(twr, free[4], tr)
    for i in range(2):
        pe.wait(x1_tok[i])
        pe.wait(free[2 * i], free[2 * i + 1])
        for k in range(8):
            f = lambda e: e.transpose(bank(2 * i, 128 * k, [1, 128]), view(X1, 1024 * i + 128 * k, [[1, 128]]), con("ident"))
            r = pe.go(f) if k == 7 else pe.quiet(f)
        act.wait(r)
        free[2 * i] = free[2 * i + 1] = act.go(lambda e, i=i: e.copy(view(X1T, 128 * i, [[256, 8], [1, 128]]), bank(2 * i, 0, [128, 8], [1, 128])))
        pe.wait(free[2 * i])
        o = bank(4, 128 * i, [1, 128], rows=36)
        mm(o, view(rowp, 1024, [[1, 36]], rows=1), con("ones", rows=1), True, False)
        for k in range(8):
            r = mm(o, view(WR, 36 * k, [[1, 36]]), view(X1T, 256 * k + 128 * i, [[1, 128]]), False, k == 7, last=(k == 7))
        act.wait(r)
        lt_tok.append(act.go(lambda e: e.copy(view(LT, 128 * i, [[1, 128]], rows=36), o)))
        act.wait(wout_done)
        h, l, x = (view(y, 1024 * i, [[1, 1024]]) for y in (X1H, X1L, X1))
        tx1h = act.go(lambda e: e.copy(h, x))
        pool.wait(tx1h)
        tx1l = pool.go(lambda e: e.tensor_tensor(l, x, h.bitcast(F32), ALU.subtract))
    for i in range(2):
        pe.wait(lt_tok[i], free[7])
        f = lambda e, i=i: e.transpose(bank(7, 64 * i, [1, 36]), view(LT, 128 * i, [[1, 128]], rows=36), con("ident", w=36, rows=36))
        r = pe.go(f)
    rt = lambda o, *d: view(RTR, o, list(d))
    LGT, GP, GM, GI, EXP, OH, EM, ES, V8, I8, EF, O0, O1, OS, RK, RKM, CNT, RA, DST, ROW, TMP = \
        0, 72, 88, 104, 120, 128, 136, 200, 216, 232, 250, 256, 320, 384, 448, 512, 576, 640, 648, 656, 664
    UI = sb("UI", 64, A0 + 28 * KB + 256, U32)
    OV, OD, OVM, MAXC = 680, 684, 688, 692
    dve.wait(r)
    r0 = dve.go(lambda e: e.tensor_copy(rt(LGT, [36, 2], [1, 36]), bank(7, 0, [64, 2], [1, 36])))
    free[4] = free[7] = r0
    r = dve.go(lambda e: e.memset(rt(GP, [1, 16]), -3.0e38))
    dve.wait(r, r0)
    r = dve.go(lambda e: e.tensor_copy(rt(GP, [8, 2], [1, 4]), rt(LGT, [36, 2], [1, 4])))
    dve.wait(r)
    for i in range(2):
        r = dve.go(lambda e, i=i: e.max(rt(GM + 8 * i, [1, 8]), rt(GP + 8 * i, [1, 8])))
    dve.wait(r)
    for i in range(2):
        r = dve.go(lambda e, i=i: e.max_index(view(UI, 8 * i, [[1, 8]]), rt(GM + 8 * i, [1, 8]), rt(GP + 8 * i, [1, 8])))
    r2 = dve.go(lambda e: e.tensor_tensor(rt(TMP, [4, 2], [1, 4]), rt(GP, [8, 2], [1, 4]), rt(GM, [8, 2], [0, 4]), ALU.subtract))
    act.wait(r2)
    re = act.go(lambda e: e.activation(rt(TMP, [1, 8]), rt(TMP, [1, 8]), ACT.Exp))
    dve.wait(r)
    r = dve.go(lambda e: e.tensor_copy(rt(GI, [1, 2]), view(UI, 0, [[8, 2]])))
    dve.wait(r)
    r = dve.go(lambda e: e.tensor_tensor(rt(OH, [4, 2], [1, 4]), view(cm, CM["iota4"][0], [[0, 2], [1, 4]]), rt(GI, [1, 2], [0, 4]), ALU.is_equal))
    dve.wait(r)
    r = dve.go(lambda e: e.tensor_tensor(rt(EM, [32, 2], [8, 4], [1, 8]), rt(LGT + 4, [36, 2], [8, 4], [1, 8]), rt(OH, [4, 2], [1, 4], [0, 8]), ALU.mult))
    dve.wait(r)
    r = dve.go(lambda e: e.tensor_reduce(rt(ES, [8, 2], [1, 8]), rt(EM, [32, 2], [1, 8], [8, 4]), AX, ALU.add))
    dve.wait(r)
    for i in range(2):
        r = dve.go(lambda e, i=i: e.max(rt(V8 + 8 * i, [1, 8]), rt(ES + 8 * i, [1, 8])))
    dve.wait(r)
    for i in range(2):
        r = dve.go(lambda e, i=i: e.max_index(view(UI, 16 + 8 * i, [[1, 8]]), rt(V8 + 8 * i, [1, 8]), rt(ES + 8 * i, [1, 8])))
    dve.wait(r)
    r = dve.go(lambda e: e.tensor_copy(rt(EF, [2, 2], [1, 2]), view(UI, 16, [[8, 2], [1, 2]])))
    dve.wait(r)
    r = dve.go(lambda e: e.scalar_tensor_tensor(rt(EF, [2, 2], [1, 2]), rt(GI, [1, 2], [0, 2]), 8.0, rt(EF, [2, 2], [1, 2]), ALU.mult, ALU.add))
    dve.wait(r)
    for a, o in ((0, O0), (1, O1)):
        r = dve.go(lambda e, a=a, o=o: e.tensor_tensor(rt(o, [32, 2], [1, 32]), view(cm, CM["iota32"][0], [[0, 2], [1, 32]]), rt(EF + a, [2, 2], [0, 32]), ALU.is_equal))
    dve.wait(r)
    ros = dve.go(lambda e: e.tensor_tensor(rt(OS, [1, 64]), rt(O0, [1, 64]), rt(O1, [1, 64]), ALU.add))
    pe.wait(ros, free[5])
    mm(bank(5, 0, [1, 32]), con("ustrict"), rt(OS, [1, 32]), True, True)
    mm(bank(5, 32, [1, 32]), con("ones"), rt(OS, [1, 32]), True, False)
    mm(bank(5, 32, [1, 32]), con("ustrict"), rt(OS + 32, [1, 32]), False, True)
    mm(bank(5, 64, [1, 32]), con("ones"), rt(OS, [1, 32]), True, False)
    r = mm(bank(5, 64, [1, 32]), con("ones"), rt(OS + 32, [1, 32]), False, True, last=True)
    GW = 700
    dve.wait(re)
    dve.go(lambda e: e.tensor_reduce(rt(GW, [1, 2]), rt(TMP, [4, 2], [1, 4]), AX, ALU.add))
    rd = dve.go(lambda e: e.tensor_tensor(rt(GW + 2, [1, 2]), rt(V8 + 1, [8, 2]), rt(V8, [8, 2]), ALU.subtract))
    act.wait(rd)
    rd = act.go(lambda e: e.activation(rt(GW + 2, [1, 2]), rt(GW + 2, [1, 2]), ACT.Exp))
    dve.wait(rd)
    rd = dve.go(lambda e: e.tensor_scalar(rt(GW + 4, [1, 2]), rt(GW + 2, [1, 2]), 1.0, None, ALU.add))
    dve.wait(rd)
    rd = dve.go(lambda e: e.tensor_tensor(rt(GW + 4, [1, 2]), rt(GW + 4, [1, 2]), rt(GW, [1, 2]), ALU.mult))
    dve.wait(rd)
    rd = dve.go(lambda e: e.reciprocal(rt(GW + 6, [1, 2]), rt(GW + 4, [1, 2])))
    dve.wait(rd)
    tw = dve.go(lambda e: e.tensor_tensor(rt(GW + 8, [1, 2]), rt(GW + 6, [1, 2]), rt(GW + 2, [1, 2]), ALU.mult))
    W0, W1 = GW + 6, GW + 8
    dve.wait(r)
    rr = dve.go(lambda e: e.tensor_copy(rt(RK, [1, 64]), bank(5, 0, [1, 64])))
    rc = dve.go(lambda e: e.tensor_copy(rt(CNT, [1, 32]), bank(5, 64, [1, 32])))
    free[5] = rc
    dve.wait(rr)
    for a, o in ((0, O0), (1, O1)):
        r = dve.go(lambda e, o=o: e.tensor_tensor(rt(RKM, [1, 64]), rt(RK, [1, 64]), rt(o, [1, 64]), ALU.mult))
        dve.wait(r)
        r = dve.go(lambda e, a=a: e.tensor_reduce(rt(RA + a, [2, 2]), rt(RKM, [32, 2], [1, 32]), AX, ALU.add))
        dve.wait(r)
    DP = 694
    dve.go(lambda e: e.tensor_scalar(rt(OV, [1, 4]), rt(RA, [1, 4]), float(KEEP), None, ALU.is_ge))
    r = dve.go(lambda e: e.scalar_tensor_tensor(rt(DP, [1, 4]), rt(EF, [1, 4]), float(CAP), rt(RA, [1, 4]), ALU.mult, ALU.add))
    dve.wait(r)
    tdst = dve.go(lambda e: e.scalar_tensor_tensor(rt(DST, [1, 4]), rt(OV, [1, 4]), FAR, rt(DP, [1, 4]), ALU.mult, ALU.add))
    dve.wait(tdst)

    def row_numbers():
        dve.go(lambda e: e.tensor_scalar(rt(OVM, [1, 4]), rt(RA, [1, 4]), float(KEEP), None, ALU.is_lt))
        r = dve.go(lambda e: e.scalar_tensor_tensor(rt(OD, [1, 4]), rt(EF, [1, 4]), float(OVR), rt(RA, [1, 4]), ALU.mult, ALU.add))
        dve.wait(r)
        dve.go(lambda e: e.tensor_tensor(rt(ROW, [1, 4]), rt(DP, [1, 4]), rt(OVM, [1, 4]), ALU.mult))
        r = dve.go(lambda e: e.scalar_tensor_tensor(rt(OD, [1, 4]), rt(OD, [1, 4]), float(-KEEP), rt(OV, [1, 4]), ALU.add, ALU.mult))
        dve.wait(r)
        dve.go(lambda e: e.tensor_copy(view(UI, 32, [[1, 4]]), rt(ROW, [1, 4])))
        r = dve.go(lambda e: e.tensor_copy(view(UI, 36, [[1, 4]]), rt(OD, [1, 4])))
        dve.wait(r)
        dve.go(lambda e: e.scalar_tensor_tensor(rt(OD, [1, 4]), rt(OVM, [1, 4]), -FAR, rt(OD, [1, 4]), ALU.mult, ALU.add))
        r = dve.go(lambda e: e.tensor_reduce(rt(MAXC, [1, 1]), rt(CNT, [1, 32]), AX, ALU.max))
        dve.wait(r)
        r = dve.go(lambda e: e.tensor_scalar(rt(MAXC, [1, 1]), rt(MAXC, [1, 1]), float(KEEP), None, ALU.is_gt))
        dve.wait(r)
        return dve.go(lambda e: e.tensor_copy(view(flag, 0, [[1, 1]]), rt(MAXC, [1, 1])))

    XS = [sb(f"XS{i}", 4096, A0 + 41 * KB + 16 * KB * i, F32R) for i in range(2)]
    SS = [sb(f"SS{i}", 512, A0 + 73 * KB + 2 * KB * i, F32R) for i in range(2)]
    SF = sb("SF", 512, A0 + 29 * KB)
    DG = sb("DG", 8, A0 + 31 * KB)
    T1 = sb("T1", 1024, A0 + 77 * KB, rows=64)
    G1 = sb("G1", 1024, A0 + 81 * KB, rows=64)
    HM = sb("HM", 512, A0 + 85 * KB, rows=64)
    T2 = sb("T2", 1024, A0 + 87 * KB, rows=64)
    YY = [sb(f"YY{i}", 1024, A0 + 91 * KB + 4 * KB * i, rows=64) for i in range(2)]
    HT = [sb(f"HT{i}", 512, A0 + 32 * KB + 2 * KB * i, F32R) for i in range(2)]
    GB, DB, TB, SB_ = 0, 2, 4, (5, 6)
    xs_tok, xs_free, ss_free = {}, [None, None], [None, None]
    ex = {}

    def select(g):
        x = SS[g % 2]
        q = pool if g else dve
        q.wait(tdst, tcm, ss_free[g % 2], ex.get("dg"))
        r = q.go(lambda e: e.tensor_scalar(view(DG, 0, [[1, 4]]), rt(DST, [1, 4]), float(-256 * g), None, ALU.add))
        q.wait(r, ex.get("sf"))
        for i in range(2):
            rs = q.go(lambda e, i=i: e.tensor_scalar(view(SF, 256 * i, [[1, 256]]), con("iota"), view(DG, 2 * i, [[1, 1]]), None, ALU.is_equal))
            r2 = q.go(lambda e, i=i: e.tensor_scalar(view(x, 256 * i, [[1, 256]]), con("iota"), view(DG, 2 * i + 1, [[1, 1]]), None, ALU.is_equal))
        q.wait(r2)
        ex["dg"] = r2
        r = q.go(lambda e: e.tensor_tensor(x[:, :], x[:, :].bitcast(F32), SF[:, :], ALU.add))
        ex["sf"] = r
        ex["sel", g] = r

    def gather(g, ks):
        for k in ks:
            b = SB_[k % 2]
            pe.wait(ex["sel", g], tx1h, tx1l, free[b])
            for half, x in ((0, X1H), (1, X1L)):
                for i in range(2):
                    r = mm(bank(b, 256 * half, [1, 256]), view(x, 1024 * i + 128 * k, [[1, 128]]), view(SS[g % 2], 256 * i, [[1, 256]]),
                           i == 0, i == 1, last=(half == 1 and i == 1))
            act.wait(r, xs_free[g % 2])
            free[b] = act.go(lambda e, b=b, k=k: e.copy(view(XS[g % 2], 512 * k, [[64, 2], [128, 4], [1, 64]]), bank(b, 0, [256, 2], [64, 4], [1, 64])))
            xs_tok[g, k] = free[b]
            if k == 7:
                ss_free[g % 2] = r
                ex["last_gather"] = r

    def up(e):
        g = e // 4
        for j in range(4):
            u = take("gu", (e, j))
            if j == 0:
                pe.wait(free[GB], free[GB + 1])
            for kk in range(2):
                k = 2 * j + kk
                pe.wait(xs_tok[g, k])
                x = view(XS[g % 2], 512 * k + 128 * (e % 4), [[1, 128]])
                for c in range(2):
                    o = bank(GB + c, 0, [1, 512])
                    mm(o, x, u.h(kk, 512 * c, 512), k == 0, False)
                    tok = mm(o, x, u.l(kk, 512 * c, 512), False, k == 7, last=(kk == 1 and c == 1))
            release(u, tok)
        if e % 4 == 3:
            xs_free[g % 2] = tok
        act.wait(tok, ex.get("g1"))
        ra = act.go(lambda q: q.copy(T1[:, :], bank(GB, 0, [1, 1024], p0=64, rows=64)))
        dve.wait(ra, ex.get("hm"))
        r = dve.go(lambda q: q.tensor_tensor(G1[:, :], bank(GB, 0, [1, 1024], rows=64), T1[:, :], ALU.add))
        free[GB] = free[GB + 1] = ex["g1"] = r
        act.wait(r)
        r = act.go(lambda q: q.activation(view(T1, 0, [[1, 512]], rows=64), view(G1, 0, [[1, 512]], rows=64), ACT.Silu))
        dve.wait(r, ex.get("tr"))
        ex["hm"] = ex["g1"] = dve.go(lambda q: q.tensor_tensor(HM[:, :], view(T1, 0, [[1, 512]], rows=64), view(G1, 512, [[1, 512]], rows=64), ALU.mult))

    def turn(e):
        pe.wait(ex["hm"], free[TB])
        for k in range(4):
            f = lambda q, k=k: q.transpose(bank(TB, 64 * k, [1, 64]), view(HM, 128 * k, [[1, 128]], rows=64), con("ident", w=64, rows=64))
            r = pe.go(f) if k == 3 else pe.quiet(f)
        ex["tr"] = r
        x = HT[e % 2]
        act.wait(r, ex.get(("down", e - 2)))
        ra = act.go(lambda q: q.copy(view(x, 0, [[128, 4], [1, 64]]), bank(TB, 0, [64, 4], [1, 64])))
        dve.wait(ra, ex.get(("down", e - 2)))
        rb = dve.go(lambda q: q.tensor_tensor(view(x, 64, [[128, 4], [1, 64]]), bank(TB, 0, [64, 4], [1, 64]), view(x, 0, [[128, 4], [1, 64]]).bitcast(F32), ALU.subtract))
        free[TB] = rb
        ex["ht", e] = (ra, rb)

    s_y = [sem("s_y0"), sem("s_y1")]
    y_tok = {}

    def down(e):
        x = HT[e % 2]
        for j in range(2):
            u = take("dn", (e, j))
            if j == 0:
                pe.wait(free[DB], free[DB + 1], *ex["ht", e])
            for kk in range(2):
                k = 2 * j + kk
                for c in range(2):
                    o = bank(DB + c, 0, [1, 512])
                    s = view(x, 128 * k, [[1, 128]])
                    mm(o, s, u.h(kk, 512 * c, 512), k == 0, False)
                    tok = mm(o, s, u.l(kk, 512 * c, 512), False, k == 3, last=(kk == 1 and c == 1))
            release(u, tok)
        ex["down", e] = tok
        act.wait(tok, ex.get("t2"))
        ra = act.go(lambda q: q.copy(T2[:, :], bank(DB, 0, [1, 1024], p0=64, rows=64)))
        dve.wait(ra, y_tok.get(e - 2))
        y = YY[e % 2]
        r = dve.go(lambda q: q.tensor_tensor(y[:, :], bank(DB, 0, [1, 1024], rows=64), T2[:, :], ALU.add))
        free[DB] = free[DB + 1] = ex["t2"] = r
        pool.wait(r)
        y_tok[e] = dma(pool, d_y[CAP * e:CAP * (e + 1), :], y[:, :], s_y[e % 2])

    PM = sb("PM", POOLW, A0 + 41 * KB)
    LG2 = sb("LG2", 1024, A0 + 65 * KB)
    LB2 = sb("LB2", 1024, A0 + 69 * KB)
    MT = sb("MT", 1024, A0 + 81 * KB, rows=NMETA)
    s_pm, s_mt = sem("s_pm"), sem("s_mt")

    def load_pm(q, s_):
        return dma(q, PM[:, :], t["pool"], s_)

    def load_norm(q, s_):
        bcast_row(q, LG2, t["ln2_g"], s_)
        return bcast_row(q, LB2, t["ln2_b"], s_)

    def load_mt(q, s_):
        return dma(q, MT[:, :], t["meta"], s_)

    act.wait(*[free[4], rd])
    select(0)
    trow = row_numbers()
    gather(0, range(8))
    for e in range(NE):
        g = e // 4
        if e % 4 == 0 and g + 1 < 8:
            select(g + 1)
        up(e)
        if e:
            down(e - 1)
        if g + 1 < 8:
            gather(g + 1, (2 * (e % 4), 2 * (e % 4) + 1))
        turn(e)
        if e == NE - 4:
            act.wait(xs_free[0])
            tpm = load_pm(act, s_pm)
    act.wait(xs_free[1])
    tln2 = load_norm(act, s_ln2)
    down(NE - 1)
    act.wait(ex["g1"])
    tmt = load_mt(act, s_mt)

    RR = [sb(f"RR{i}", 1024, A0 + 4 * KB * i) for i in range(4)]
    s_g = [sem(f"s_g{i}") for i in range(4)]
    pool.wait(trow, y_tok[NE - 2], y_tok[NE - 1], ex["last_gather"], ex["t2"])
    rr_tok = []
    for n in range(4):
        pool.quiet(lambda e: e.indirect_dma_start(RR[n][:, :], None, d_y, bass.IndirectOffsetOnAxis(ap=view(UI, 32 + n, [[1, 1]]), axis=0)).then_inc(s_g[n], 16))
        rr_tok.append((s_g[n], 16))

    s_ov = [sem(f"s_ov_{n}") for n in ("pe", "act", "dve", "pool", "sp")]
    s_ore = sem("s_ore")
    s_ow, s_oy, s_og = sem("s_ow"), sem("s_oy"), [sem(f"s_og{i}") for i in range(4)]
    before = [(q.sem, q.n) for q in (pe, act, dve, pool)] + rr_tok + [tln2, tpm, tmt]
    engines = (nc.tensor, nc.scalar, nc.vector, nc.gpsimd, nc.sync)
    for q in (pe, act, dve, pool, sp):
        q.wait(trow)
    over = nc.values_load(view(flag, 0, [[1, 1]], rows=1).bitcast(I32), min_val=0, max_val=1)
    with nc.If(over > 0):
        ope, oact, odve, opool, osp = (Queue(q, x) for q, x in zip(engines, s_ov))
        for q in (ope, oact, odve, opool, osp):
            q.wait(*before)
        GUW = sb("GUW", 8192, A0 + 41 * KB)
        DNW = sb("DNW", 4096, A0 + 85 * KB)
        XG = sb("XG", 1536, A0 + 32 * KB)
        OS_ = sb("OS_", 384, A0 + 73 * KB)
        OT_ = sb("OT_", 512, A0 + 75 * KB)
        OG = sb("OG", 512, A0 + 38 * KB)
        OY = sb("OY", 512, A0 + 29 * KB)
        OX = sb("OX", 192, A0 + 31 * KB)
        nc.all_engine_barrier()
        with nc.Fori(0, NE) as ei:
            ope, oact, odve, opool, osp = (Queue(q, x) for q, x in zip(engines, s_ov))
            nd = [0]

            def odma(q, dst, src, s_, n):
                q.eng.dma_start(dst, src).then_inc(s_, 16)
                return s_, n

            odma(osp, view(GUW, 0, [[1024, 8], [1, 1024]]), t["w_gate_up"][bass.ds(ei, 1)].rearrange("o (c p) n -> p (o c) n", p=128), s_ow, 16)
            w_tok = odma(osp, view(DNW, 0, [[1024, 4], [1, 1024]]), t["w_down"][bass.ds(ei, 1)].rearrange("o (c p) n -> p (o c) n", p=128), s_ow, 32)
            for i in range(2):
                sl = view(OS_, OVR * i, [[1, OVR]])
                r = odve.go(lambda e: e.tensor_scalar(sl, con("iota", w=OVR), rt(OD + 2 * i, [1, 1]), None, ALU.is_equal))
                r = odve.go(lambda e: e.tensor_scalar(view(OX, 0, [[1, OVR]]), con("iota", w=OVR), rt(OD + 2 * i + 1, [1, 1]), None, ALU.is_equal))
                odve.wait(r)
                ts = odve.go(lambda e: e.tensor_tensor(sl, sl, view(OX, 0, [[1, OVR]]), ALU.add))
                odve.wait(ts)
            odve.go(lambda e: e.tensor_scalar(rt(OD, [1, 4]), rt(OD, [1, 4]), float(-OVR), None, ALU.add))

            def omm(o, a, b, start, stop):
                return ope.go(lambda e: e.matmul(o, a, b, start=start, stop=stop))

            ope.wait(ts)
            rg = None
            for k in range(8):
                ope.wait(rg)
                for i in range(2):
                    r = omm(bank(0, 0, [1, OVR]), view(X1, 1024 * i + 128 * k, [[1, 128]]), view(OS_, OVR * i, [[1, OVR]]), i == 0, i == 1)
                oact.wait(r)
                rg = oact.go(lambda e: e.copy(view(XG, OVR * k, [[1, OVR]]), bank(0, 0, [1, OVR])))
            ope.wait(rg, w_tok)
            ry = None
            for s0, w in ((0, 128), (128, 64)):
                for c in range(2):
                    for k in range(8):
                        r = omm(bank(1 + c, 0, [1, 512], rows=w), view(XG, OVR * k + s0, [[1, w]]), view(GUW, 1024 * k + 512 * c, [[1, 512]]), k == 0, k == 7)
                oact.wait(r)
                r = oact.go(lambda e: e.activation(view(OG, 0, [[1, 512]], rows=w), bank(1, 0, [1, 512], rows=w), ACT.Silu))
                odve.wait(r)
                r = odve.go(lambda e: e.tensor_tensor(view(OG, 0, [[1, 512]], rows=w), view(OG, 0, [[1, 512]], rows=w), bank(2, 0, [1, 512], rows=w), ALU.mult))
                ope.wait(r)
                for k in range(4):
                    r = ope.go(lambda e: e.transpose(bank(3, w * k, [1, w]), view(OG, 128 * k, [[1, 128]], rows=w), con("ident", w=w, rows=w)))
                odve.wait(r)
                r = odve.go(lambda e: e.tensor_copy(view(OT_, 0, [[1, 4 * w]]), bank(3, 0, [1, 4 * w])))
                ope.wait(r)
                for c in range(2):
                    for k in range(4):
                        r = omm(bank(4, 0, [1, 512], rows=w), view(OT_, w * k, [[1, w]]), view(DNW, 1024 * k + 512 * c, [[1, 512]]), k == 0, k == 3)
                    odve.wait(r, ry)
                    r = odve.go(lambda e: e.tensor_copy(view(OY, 0, [[1, 512]], rows=w), bank(4, 0, [1, 512], rows=w)))
                    ope.wait(r)
                    osp.wait(r)
                    nd[0] += 16
                    ry = odma(osp, d_o[bass.ds(ei * OVR + s0, w), 512 * c:512 * c + 512], view(OY, 0, [[1, 512]], rows=w), s_oy, nd[0])
            osp.wait(ry)
            nc.all_engine_barrier(sems_to_clear=range(s_ov[0].num, s_ov[4].num + 1))
            for q, x in ((osp, s_ow), (osp, s_oy)):
                q.eng.sem_clear(x)
            nc.all_engine_barrier()
        odve = Queue(nc.vector, s_ov[2])
        for n in range(4):
            ro = sb(f"RO{n}", 1024, A0 + 41 * KB + 4 * KB * n)
            nc.gpsimd.indirect_dma_start(ro[:, :], None, d_o, bass.IndirectOffsetOnAxis(ap=view(UI, 36 + n, [[1, 1]]), axis=0)).then_inc(s_og[n], 16)
            nc.vector.wait_ge(s_og[n], 16)
            r = odve.go(lambda e: e.copy_predicated(RR[n][:, :], rt(OV + n, [0, 1024]).bitcast(U32), ro[:, :]))
        odve.wait(r)
        n = 0
        nc.sync.wait_ge(odve.sem, odve.n)
        for dst, src in ((PM[:, :], t["pool"]), (MT[:, :], t["meta"])) + tuple(
                (x[:, :], bass.AP(tensor=y.tensor, offset=y.offset, ap=[[0, 128], [1, 1024]])) for x, y in ((LG2, t["ln2_g"]), (LB2, t["ln2_b"]))):
            nc.sync.dma_start(dst, src).then_inc(s_ore, 16)
            n += 16
        nc.sync.wait_ge(s_ore, n)
        nc.all_engine_barrier()
    AX2 = sb("AX2", 2048, A0 + 57 * KB)
    XRH = sb("XRH", 2048, A0 + 85 * KB, F32R)
    XRL = sb("XRL", 2048, A0 + 93 * KB, F32R)
    MTH = sb("MTH", 1024, A0 + 73 * KB, F32R, rows=NMETA)
    MTL = sb("MTL", 1024, A0 + 77 * KB, F32R, rows=NMETA)
    PMR = sb("PMR", 4 * BANDW + 4 * L, A0 + 41 * KB, F32R)
    pmr = lambda off, w, rows=128: view(PMR, off, [[1, w]], rows=rows)
    SCR = sb("SCR", 1024, A0 + 89 * KB, rows=NMETA)
    HH = sb("HH", 8 * L, A0 + 32 * KB)
    HW = 4 * 8 * L
    act.wait(tx1l, xs_free[1])
    tax = act.go(lambda e: e.activation(AX2[:, :], X1[:, :], ACT.Copy, scale=ALPHA))
    act.wait(tpm)
    tpmr = act.go(lambda e: e.copy(PMR[:, :], view(PM, 0, [[1, 4 * BANDW + 4 * L]])))

    def token_rms(key, src, h, l, rows, tok, dead, scratch):
        c = 80 + 2 * key
        s1, s2 = (view(small, c + i, [[1, 1]], rows=rows) for i in range(2))
        act.wait(tok, *dead)
        r = act.go(lambda e: e.activation(scratch, src, ACT.Square, accum_out=s1))
        dve.wait(r)
        r = dve.go(lambda e: e.tensor_scalar(s2, s1, 1.0 / D, 1e-6, ALU.mult, ALU.add))
        dve.wait(r)
        r = dve.go(lambda e: e.reciprocal(s2, s2))
        act.wait(r)
        r = act.go(lambda e: e.activation(s2, s2, ACT.Sqrt))
        act.wait(r)
        rh = act.go(lambda e: e.activation(h, src, ACT.Copy, scale=s2))
        dve.wait(rh)
        return rh, dve.go(lambda e: e.scalar_tensor_tensor(l, src, s2, h.bitcast(F32), ALU.mult, ALU.subtract))

    mt_tok = token_rms(2, MT[:, :], MTH[:, :], MTL[:, :], NMETA, tmt, (ex["last_gather"], ex["g1"], ex["t2"], y_tok[NE - 1], y_tok[NE - 2]), SCR[:, :])
    x2_tok, xr_tok = [], {}
    for i in range(2):
        o = view(X1, 1024 * i, [[1, 1024]])
        dve.wait(rr_tok[2 * i], tw, tax)
        r = dve.go(lambda e, i=i: e.scalar_tensor_tensor(RR[2 * i][:, :], RR[2 * i][:, :], rt(W0 + i, [1, 1]), view(AX2, 1024 * i, [[1, 1024]]), ALU.mult, ALU.add))
        dve.wait(r, rr_tok[2 * i + 1])
        r = dve.go(lambda e, i=i, o=o: e.scalar_tensor_tensor(o, RR[2 * i + 1][:, :], rt(W1 + i, [1, 1]), RR[2 * i][:, :], ALU.mult, ALU.add))
        x2_tok.append(layer_norm(i, X1, LG2, LB2, r, tln2))
    for i in range(2):
        v = lambda x: view(x, 1024 * i, [[1, 1024]])
        xr_tok[i] = token_rms(i, v(X1), v(XRH), v(XRL), 128, x2_tok[i], (), v(AX2))

    AH = sb("AH", 8 * L + 128, A0, F32R)
    AL = sb("AL", 8 * L + 128, A0 + 9 * KB, F32R)
    RS = sb("RS", L, A0 + 18 * KB)
    SQ1 = sb("SQ1", L, A0 + 18 * KB + 1088)
    SQS = sb("SQS", L, A0 + 18 * KB + 2176)
    PF = sb("PF", 8 * L, A0 + 22 * KB)
    AM = sb("AM", 128 + AW, A0 + 22 * KB)
    FH = sb("FH", 22 * L, A0 + 41 * KB, F32R)
    FL = sb("FL", 22 * L, A0 + 41 * KB + 88 * L, F32R)
    F2 = [sb(f"F2{i}", 4 * L, A0 + 41 * KB + 2 * 88 * L + 16 * L * i) for i in range(2)]
    assert 41 * KB + 2 * 88 * L + 32 * L <= 102 * KB
    hc = lambda x, k, n=1: view(x, L * k, [[1, n * L]])
    tc = lambda x, k, q0=0: view(x, L * k + q0, [[1, L - q0]])

    s_m = sem("s_m")
    pool.wait(*x2_tok)
    pool.wait(ex["down", NE - 1])
    tmeta = dma(pool, view(HH, 0, [[L, 8], [1, NMETA]]), t["metaT"].rearrange("p (c n) -> p c n", c=8), s_m)
    hh_tok = [tmeta]
    for i in range(2):
        pe.wait(x2_tok[i])
        pe.wait(free[2 * i], free[2 * i + 1])
        for k in range(8):
            f = lambda e, i=i, k=k: e.transpose(bank(2 * i, 128 * k, [1, 128]), view(X1, 1024 * i + 128 * k, [[1, 128]]), con("ident"))
            r = pe.go(f) if k == 7 else pe.quiet(f)
        act.wait(r)
        free[2 * i] = free[2 * i + 1] = act.go(lambda e, i=i: e.copy(view(HH, NMETA + 128 * i, [[L, 8], [1, 128]]), bank(2 * i, 0, [128, 8], [1, 128])))
        hh_tok.append(free[2 * i])

    pooled = {}
    pe.wait(tpmr, *mt_tok)
    pe.wait(*xr_tok[0])
    pe.wait(*xr_tok[1])
    for k in range(8):
        g = k // 2
        b = (4 + k) % 8
        pe.wait(free[b])
        for n, (h, l, col, off, rows) in enumerate(((XRH, XRL, 0, BANDW * g + 128, 128), (XRH, XRL, 1024, BANDW * g, 128),
                                                    (MTH, MTL, 0, 4 * BANDW + L * g, NMETA))):
            for x in (h, l):
                r = mm(bank(b, 0, [1, L]), view(x, col + 128 * k, [[1, 128]], rows=rows), pmr(off, L, rows),
                       n == 0 and x is h, n == 2 and x is l, last=(n == 2 and x is l))
        dve.wait(r, *xr_tok[1])
        rp = dve.go(lambda e, k=k, b=b, g=g: e.scalar_tensor_tensor(hc(PF, k), bank(b, 0, [1, L]), par("nm", k), view(PM, 4 * BANDW + 4 * L + L * g, [[1, L]]),
                                                                    ALU.mult, ALU.mult))
        free[b] = rp
        if k % 2:
            act.wait(rp)
            rh = act.go(lambda e, k=k: e.copy(hc(AH, k - 1, 2), hc(PF, k - 1, 2)))
            dve.wait(rh)
            rl = dve.go(lambda e, k=k: e.tensor_tensor(hc(AL, k - 1, 2), hc(PF, k - 1, 2), hc(AH, k - 1, 2).bitcast(F32), ALU.subtract))
            pooled[g] = (rh, rl)
    dve.go(lambda e: e.memset(view(AH, 8 * L, [[1, 128]]).bitcast(F32), 0.0))
    ttail = dve.go(lambda e: e.memset(view(AL, 8 * L, [[1, 128]]).bitcast(F32), 0.0))
    ah, al = (lambda k: hc(AH, k)), (lambda k: hc(AL, k))

    class Norm:

        def __init__(self, gname, gi, afree, q0=0, half=True):
            self.g, self.gi, self.afree, self.q0, self.half = gname, gi, afree, q0, half
            self.need = {}
            self.sq = None

        def chunk(self, k, tok):
            q0 = self.q0
            g = par(self.g, self.gi + k)
            act.wait(tok, *self.afree)
            dve.wait(*self.afree)
            if self.half:
                rh = act.go(lambda e: e.activation(tc(AH, k, q0), tc(HH, k, q0), ACT.Copy, scale=g))
                dve.wait(rh)
                rl = dve.go(lambda e: e.scalar_tensor_tensor(tc(AL, k, q0), tc(HH, k, q0), g, tc(AH, k, q0).bitcast(F32), ALU.mult, ALU.subtract))
                self.need[k] = (rh, rl)
            else:
                self.need[k] = (act.go(lambda e: e.activation(tc(FO, k, q0), tc(HH, k, q0), ACT.Copy, scale=g)),)
            pool.wait(tok, self.sq, ss["mm"])
            x = SQS if self.sq is None else SQ1
            r = pool.go(lambda e: e.tensor_tensor(tc(x, 0, q0), tc(HH, k, q0), tc(HH, k, q0), ALU.mult))
            if x is SQ1:
                pool.wait(r)
                r = pool.go(lambda e: e.tensor_tensor(tc(SQS, 0, q0), tc(SQS, 0, q0), tc(SQ1, 0, q0), ALU.add))
            self.sq = r

        def factors(self, b):
            q0 = self.q0
            pe.wait(self.sq, free[b])
            ss["mm"] = r = mm(bank(b, 0, [1, L - q0]), con("ones"), tc(SQS, 0, q0), True, True, last=True)
            dve.wait(r)
            r = dve.go(lambda e: e.tensor_scalar(tc(RS, 0, q0), bank(b, 0, [1, L - q0]), 1.0 / D, 1e-6, ALU.mult, ALU.add))
            free[b] = r
            dve.wait(r)
            r = dve.go(lambda e: e.reciprocal(tc(RS, 0, q0), tc(RS, 0, q0)))
            act.wait(r)
            self.rs = act.go(lambda e: e.activation(tc(RS, 0, q0), tc(RS, 0, q0), ACT.Sqrt))
            return self.rs

        def columns(self, b, tiles, col):
            pe.wait(self.sq, free[b])
            for n, (p0, w) in enumerate(tiles):
                r = mm(bank(b, n, [1, 1], rows=w), view(SQS, p0, [[1, w]]), con("ones", w=1), True, True, last=True)
            ss["mm"] = r
            for n, (p0, w) in enumerate(tiles):
                v = view(small, col + n, [[1, 1]], rows=w)
                dve.wait(r)
                free[b] = x = dve.go(lambda e: e.tensor_scalar(v, bank(b, n, [1, 1], rows=w), 1.0 / D, 1e-6, ALU.mult, ALU.add))
                dve.wait(x)
                x = dve.go(lambda e: e.reciprocal(v, v))
                act.wait(x)
                x = act.go(lambda e: e.activation(v, v, ACT.Sqrt))
            return x

    ss = {"mm": None}
    nxt = Norm("nf", 0, ())
    hn = {}
    for g in range(4):
        u = take("pw", g)
        pe.wait(*pooled[g])
        for m in range(2):
            k = 2 * g + m
            b = k % 4
            pe.wait(free[b])
            tok = stationary_w(u, bank(b, 0, [1, L]), m, range(2), lambda k: hc(AH, 2 * g + k), lambda k: hc(AL, 2 * g + k))
            dve.wait(tok, *hh_tok)
            r = dve.go(lambda e, k=k, b=b: e.scalar_tensor_tensor(hc(HH, k), bank(b, 0, [1, L]), par("ps", k), hc(HH, k), ALU.mult, ALU.add))
            free[b] = hn[k] = r
        nxt.afree = (tok,)
        for k in (2 * g, 2 * g + 1):
            nxt.chunk(k, hn[k])
        release(u, tok)

    def ffn(i, cur, nxt, q0, tiles=None):
        w = L - q0
        fh = {}
        for f in range(11):
            bb = 4 * (f % 2)
            for which, nm in enumerate(("fg", "fu")):
                u = take(nm, (i, f))
                for m in range(2):
                    b = (bb + 2 * which + m) % 8
                    pe.wait(free[b])
                    tok = stationary_w(u, bank(b, 0, [1, w]), m, range(8), lambda k: tc(AH, k, q0), lambda k: tc(AL, k, q0), need=cur.need)
                release(u, tok)
                if which == 0:
                    gtok = tok
                    if f == 0:
                        cur.factors(7)
            x = F2[f % 2]
            pair = lambda b: bank(b, 0, [512, 2], [1, w])
            rs = view(RS, q0, [[0, 2], [1, w]])
            xa, xb = (view(x, 2 * L * n, [[w, 2], [1, w]]) for n in range(2))
            flat = view(x, 0, [[1, 2 * w]])
            dve.wait(gtok, cur.rs, fh.get(f - 2))
            r = dve.go(lambda e, xa=xa, bb=bb: e.tensor_tensor(xa, pair(bb), rs, ALU.mult))
            free[bb] = free[bb + 1] = r
            act.wait(r)
            r1 = act.go(lambda e, xa=xa: e.activation(xa, xa, ACT.Silu))
            dve.wait(tok)
            r = dve.go(lambda e, xb=xb, bb=bb: e.tensor_tensor(xb, pair(bb + 2), rs, ALU.mult))
            free[bb + 2] = free[bb + 3] = r
            dve.wait(r, r1)
            r = dve.go(lambda e, xa=xa, xb=xb: e.tensor_tensor(xa, xa, xb, ALU.mult))
            act.wait(r)
            rh = act.go(lambda e, flat=flat, f=f: e.copy(view(FH, 2 * w * f, [[1, 2 * w]]), flat))
            dve.wait(rh)
            rl = dve.go(lambda e, flat=flat, f=f: e.tensor_tensor(view(FL, 2 * w * f, [[1, 2 * w]]), flat, view(FH, 2 * w * f, [[1, 2 * w]]).bitcast(F32), ALU.subtract))
            fh[f] = rl
        nxt.afree = (tok,)
        for c in range(4):
            b0 = 2 * (c % 2)
            for k3 in range(3):
                u = take("fd", (i, c, k3))
                n = 8 if k3 < 2 else 6
                for m in range(2):
                    if k3 == 0:
                        pe.wait(free[b0 + m])
                    tok = stationary_w(u, bank(b0 + m, 0, [1, w]), m, range(8 * k3, 8 * k3 + n), lambda k: view(FH, w * k, [[1, w]]),
                                       lambda k: view(FL, w * k, [[1, w]]), start=(k3 == 0), stop=(k3 == 2), need={k: (fh[k // 2],) for k in range(22)})
                    if k3 == 2:
                        k = 2 * c + m
                        dve.wait(tok)
                        r = dve.go(lambda e, k=k, b=b0 + m: e.tensor_tensor(tc(HH, k, q0), bank(b, 0, [1, w]), tc(HH, k, q0), ALU.add))
                        free[b0 + m] = r
                        nxt.chunk(k, r)
                release(u, tok)
        return tok

    s_am = sem("s_am")
    act.wait(*pooled[3])
    tam = dma(act, AM[:, :], t["am"], s_am)
    AMR = sb("AMR", 128 + AW, A0 + 22 * KB, F32R)
    amr = lambda off, w: view(AMR, off, [[1, w]])
    cur, nxt = nxt, Norm("nm", 8, ())
    pe_f = ffn(0, cur, nxt, 0)

    cur = nxt
    Q2 = sb("Q2", 8 * S, A0 + 41 * KB)
    K2 = sb("K2", 8 * 384, A0 + 49 * KB)
    V2 = sb("V2", 3072, A0 + 61 * KB)
    EE = [sb(f"EE{i}", 2 * AW, A0 + 73 * KB + 8 * AW * i) for i in range(2)]
    PP = [sb(f"PP{i}", 2 * AW, A0 + 73 * KB + 8 * AW * (2 + i)) for i in range(2)]
    OH2 = sb("OH2", 8 * S, A0 + 86 * KB, F32R)
    OL2 = sb("OL2", 8 * S, A0 + 94 * KB, F32R)
    act.wait(tam)
    tam = act.go(lambda e: e.copy(AMR[:, :], AM[:, :]))
    dve.wait(pe_f)
    tpad = dve.go(lambda e: e.memset(view(K2, 272, [[384, 8], [1, 112]]), 0.0))
    qk = {}
    PB_ = (6, 7)

    def qkv_unit(i, j):
        u = take("qkv", (i, j))
        if i < 2:
            q0, w = (NMETA, S) if i == 0 else (0, L)
            for m in range(2):
                pe.wait(free[PB_[m]])
                tok = stationary_w(u, bank(PB_[m], 0, [1, w]), m, range(8), lambda k: tc(AH, k, q0), lambda k: tc(AL, k, q0), need=cur.need)
            if i == 0 and j == 0:
                cur.factors(5)
                cur.rc = cur.columns(4, ((0, 128), (128, 128), (256, 16)), 96)
            dve.wait(tok, cur.rs, pe_f)
            dst = view(Q2, 512 * j, [[S, 2], [1, w]]) if i == 0 else view(K2, 768 * j, [[384, 2], [1, w]])
            r = dve.go(lambda e: e.scalar_tensor_tensor(dst, bank(6, 0, [512, 2], [1, w]), 0.125 if i == 0 else 1.0, view(RS, q0, [[0, 2], [1, w]]), ALU.mult, ALU.mult))
            free[6] = free[7] = r
            qk[i, j] = r
        else:
            for n in range(3):
                b = PB_[(n + j) % 2]
                pe.wait(free[b], ttail)
                tok = moving_w(u, bank(b, 0, [1, 256]), 0, 256, range(8), lambda k: view(AH, L * k + 128 * n, [[1, 128]]),
                               lambda k: view(AL, L * k + 128 * n, [[1, 128]]))
                act.wait(tok, cur.rc, pe_f)
                rows = 128 if n < 2 else 16
                r = act.go(lambda e: e.activation(view(V2, 1024 * n + 256 * j, [[1, 256]], rows=rows), bank(b, 0, [1, 256], rows=rows), ACT.Copy,
                                                  scale=view(small, 96 + n, [[1, 1]], rows=rows)))
                free[b] = r
            qk[i, j] = r
        release(u, tok)

    att, o_tok = {}, {}
    two = lambda x: view(x, 0, [[AW, 2], [1, AW]])

    def att_scores(g):
        b = 2 * (g % 2)
        pe.wait(qk[0, g // 2], qk[1, g // 2], free[b], free[b + 1], tam, tpad)
        for w in range(2):
            mm(bank(b + w, 0, [1, AW]), amr(0, 128), amr(128, AW), True, False, skip_group_check=True)
        for w in range(2):
            for k0, q0, n, c in ATILES:
                r = mm(bank(b + w, c, [1, n]), view(K2, 384 * g + k0, [[1, 128]], 64 * w, 64), view(Q2, S * g + q0, [[1, n]], 64 * w, 64),
                       False, True, last=(w == 1 and c == 400), skip_group_check=True)
        E, P, z = EE[g % 2], PP[g % 2], bank(b, 0, [512, 2], [1, AW])
        act.wait(r, att.get(("pv", g - 2)), att.get(("sp", g - 2)))
        r = act.go(lambda e: e.activation(two(E), z, ACT.Abs))
        act.wait(r)
        r = act.go(lambda e: e.activation(two(E), two(E), ACT.Exp, scale=-1.0))
        act.wait(r)
        r = act.go(lambda e: e.activation(two(E), two(E), ACT.Ln, bias=1.0))
        dve.wait(r, att.get(("r", g - 2)))
        att["sp", g] = dve.go(lambda e: e.scalar_tensor_tensor(two(P), z, 0.0, two(E), ALU.max, ALU.add))

    def att_decay(g):
        b = 2 * (g % 2)
        P = PP[g % 2]
        pe.wait(att["sp", g])
        kw = dict(skip_group_check=True)
        for w in range(2):
            x = lambda c, n: view(P, AW * w + c, [[1, n]])
            o = lambda c, n: bank(b + w, c, [1, n])
            mm(o(0, 256), con("trineg"), x(0, 256), False, True, **kw)
            mm(o(112, 144), con("negones"), x(256, 144), False, True, **kw)
            mm(o(240, 16), con("negones"), x(400, 16), False, True, **kw)
            mm(o(256, 160), con("trineg"), x(256, 160), False, True, **kw)
            r = mm(o(384, 16), con("negones"), x(400, 16), False, True, last=True, **kw)
        att["r", g] = r
        act.wait(r, att["sp", g])
        free[b] = free[b + 1] = att["a", g] = act.go(lambda e: e.activation(two(EE[g % 2]), bank(b, 0, [512, 2], [1, AW]), ACT.Exp))

    def att_out(g):
        bo = 4 + g % 2
        A = EE[g % 2]
        pe.wait(att["a", g], qk[2, g // 2], free[bo])
        for w in range(2):
            for n, (k0, q0, wd, c) in enumerate(ATILES):
                rows = 128 if n < 2 else 16
                r = mm(bank(bo, q0, [1, wd], p0=64 * w, rows=64), view(V2, 1024 * n + 64 * (2 * g + w), [[1, 64]], rows=rows),
                       view(A, AW * w + c, [[1, wd]], rows=rows), n == 0, n == 2, last=(w == 1 and n == 2))
        att["pv", g] = r
        act.wait(r, pe_f)
        rh = act.go(lambda e: e.copy(view(OH2, S * g, [[1, S]]), bank(bo, 0, [1, S])))
        dve.wait(rh, pe_f)
        free[bo] = dve.go(lambda e: e.tensor_tensor(view(OL2, S * g, [[1, S]]), bank(bo, 0, [1, S]), view(OH2, S * g, [[1, S]]).bitcast(F32), ALU.subtract))
        o_tok[g] = (rh, free[bo])

    nxt = Norm("nf", 8, (), NMETA)

    def wo_unit(j):
        u = take("wo", j)
        ks = range(6) if j < 4 else range(6, 8)
        for m in range(2 if j < 4 else 8):
            b = PB_[m] if j < 4 else (6, 7, 4, 5)[m % 4]
            k = 2 * j + m if j < 4 else m
            pe.wait(free[b])
            tok = stationary_w(u, bank(b, 0, [1, S]), m, ks, lambda k: view(OH2, S * k, [[1, S]]), lambda k: view(OL2, S * k, [[1, S]]), need=o_tok)
            dve.wait(tok, att.get(("wo", k)))
            free[b] = r = att["wo", k] = dve.go(lambda e: e.tensor_tensor(tc(HH, k, NMETA), bank(b, 0, [1, S]), tc(HH, k, NMETA), ALU.add))
            if j == 4:
                nxt.chunk(k, r)
        release(u, tok)

    for i in range(3):
        qkv_unit(i, 0)
    for j in range(4):
        g = 2 * j
        fill = [lambda i=i: qkv_unit(i, j + 1) for i in range(3)] if j < 3 else [lambda i=i: wo_unit(i) for i in range(3)]
        att_scores(g)
        fill[0]()
        att_decay(g)
        att_scores(g + 1)
        fill[1]()
        att_out(g)
        att_decay(g + 1)
        fill[2]()
        att_out(g + 1)
        if j == 2:
            nxt.afree = (used[state["next"] - 1],)
    wo_unit(3)
    wo_unit(4)
    cur, nxt = nxt, Norm("fn", 0, (), NMETA, half=False)
    FO = sb("FO", 8 * L, A0)
    pe_f = ffn(1, cur, nxt, NMETA)

    OUTB = sb("OUTB", 2048, A0 + 22 * KB)
    s_o = [sem(f"s_o{i}") for i in range(4)]
    fin = []
    for i in range(2):
        pe.wait(free[4 + 2 * i], free[5 + 2 * i])
    for k in range(8):
        pe.wait(*nxt.need[k])
        for i in range(2):
            f = lambda e, k=k, i=i: e.transpose(bank(4 + 2 * i, 128 * k, [1, 128]), view(FO, L * k + NMETA + 128 * i, [[1, 128]]), con("ident"))
            r = pe.go(f) if k == 7 and i == 1 else pe.quiet(f)
    rc = nxt.columns(0, ((NMETA, 128), (NMETA + 128, 128)), 100)
    for n in range(4):
        i, c = n // 2, n % 2
        o, b = view(OUTB, 512 * n, [[1, 512]]), bank(4 + n, 0, [1, 512])
        q, f = (act, lambda e: e.activation(o, b, ACT.Copy, scale=sm(100 + i))) if c else (dve, lambda e: e.tensor_scalar(o, b, sm(100 + i), None, ALU.mult))
        q.wait(r, rc)
        x = q.go(f)
        sp.wait(x)
        fin.append(dma(sp, out[0, 128 * i:128 * (i + 1), 512 * c:512 * c + 512], o, s_o[n]))
    sp.wait(*fin)
    sp.wait(ttab, y_tok[NE - 1], y_tok[NE - 2])
    assert state["next"] == NU


def layout(inputs):
    g = {k: np.ascontiguousarray(np.asarray(v)) for k, v in inputs.items()}
    cmat, hot, scan, pool, am = shape_constants()
    col = lambda v: np.asarray(v).reshape(-1, 128).T
    x = g["x"]
    a = {
        "x": x,
        "xT": x[0].T.reshape(8, 128, S).transpose(1, 0, 2).reshape(128, 2048),
        "cm": cmat, "hot": hot, "scan": scan, "pool": pool, "am": am, "meta": g["meta_2"],
        "pc": np.concatenate([col(g["b_in"][0]), col(g["lb_logits"]), col(g["hg_norm_g"][0]), col(g["norm_mix_2"]),
                              col(g["norm_ffn_2"]), col(g["pool_scale_2"][0]), col(g["final_norm_2"])], 1),
        "rows": np.concatenate([g["b_in"][0, 1024:1536], g["b_in"][0, 3072:3584], g["b_group"][0], g["b_expert"][0]])[None, :],
        "rb": np.concatenate([g["rel_bias"], np.ones((1, 8), np.float32)], 0),
        "wr": np.concatenate([g["w_group"][0], g["w_expert"][0]], 1).reshape(8, 128, 36).transpose(1, 0, 2).reshape(128, 288),
        "metaT": g["meta_2"].T.reshape(8, 128, NMETA).transpose(1, 0, 2).reshape(128, 8 * NMETA),
        "w_in": g["w_in"][0], "w_proj_a": g["w_proj_a"][0], "w_proj_b": g["w_proj_b"][0], "w_out": g["w_out"][0],
        "ln1_g": g["ln1_g"][0], "ln1_b": g["ln1_b"][0], "ln2_g": g["ln2_g"][0], "ln2_b": g["ln2_b"][0],
        "w_gate_up": g["w_gate_up"][0], "w_down": g["w_down"][0],
        "pool_w": g["pool_w_2"][0], "sb_w_qkv": g["sb_w_qkv_2"][0], "sb_w_o": g["sb_w_o_2"][0],
        "ffn_w_gate": g["ffn_w_gate_2"], "ffn_w_up": g["ffn_w_up_2"], "ffn_w_down": g["ffn_w_down_2"],
    }
    return {k: np.ascontiguousarray(v) for k, v in a.items()}


def kernel(**inputs):
    import concourse.bacc as _bacc
    from concourse.bass_utils import run_bass_kernel_spmd as _run

    nc = _bacc.Bacc("TRN2", target_bir_lowering=False, num_devices=1)
    arrays, args = {}, {}
    for name, a in layout(inputs).items():
        arrays[f"in_{name}_dram"] = a
        args[name] = nc.dram_tensor(f"in_{name}_dram", a.shape, mybir.dt.from_np(a.dtype), kind="ExternalInput").ap()
    out = nc.dram_tensor("out_0_dram", (1, S, D), F32, kind="ExternalOutput").ap()
    build(nc, args, out)
    r = _run(nc, [arrays], core_ids=[0])
    return r.results[0]["out_0_dram"]
```
